# Optimizing a Trainium2 kernel written in Bass

```python
import jax, jax.numpy as jnp
from jax import lax
import numpy as np

D_MODEL = 1024
BATCH = 1
SEQ = 256
DEPTH = 2

HEAD_DIM = 64
ROT_DIM = HEAD_DIM // 4
ROPE_THETA = 500000.0
NORM_EPS = 1e-6
NEG_INF = -1e30

MOBA_HEADS = 8
MOBA_BLOCK = 256
MOBA_TOPK = 3
MOBA_Q_CHUNK = 32

NSA_HEADS = 8
NSA_KV_HEADS = 2
NSA_GROUP = NSA_HEADS // NSA_KV_HEADS
NSA_CMP_LEN = 32
NSA_CMP_STRIDE = 16
NSA_CMP_HIDDEN = 256
NSA_SEL_BLOCK = 64
NSA_SEL_TOPK = 16
NSA_WINDOW = 512
NSA_Q_CHUNK = 32
NSA_FORCE = 1e4

DIFF_HEADS = 8
DIFF_QK_DIM = HEAD_DIM
DIFF_V_DIM = 2 * HEAD_DIM
DIFF_Q_CHUNK = 128

FFN_HIDDEN = -(-8 * D_MODEL // (3 * 256)) * 256

MOBA_W = MOBA_HEADS * HEAD_DIM
NSA_Q_W = NSA_HEADS * HEAD_DIM
NSA_KV_W = 3 * 2 * NSA_KV_HEADS * HEAD_DIM
NSA_GATE_W = 3 * NSA_HEADS
SPARSE_IN = 3 * MOBA_W + NSA_Q_W + NSA_KV_W + NSA_GATE_W
SPARSE_SPLITS = [MOBA_W, 2 * MOBA_W, 3 * MOBA_W, 3 * MOBA_W + NSA_Q_W, 3 * MOBA_W + NSA_Q_W + NSA_KV_W]
SPARSE_OUT = MOBA_W + NSA_Q_W
DIFF_IN = 2 * DIFF_HEADS * 2 * DIFF_QK_DIM + DIFF_HEADS * DIFF_V_DIM
DIFF_OUT = DIFF_HEADS * DIFF_V_DIM


def rms_norm(t, gain):
    tf = t.astype(jnp.float32)
    y = tf * lax.rsqrt(jnp.mean(tf * tf, axis=-1, keepdims=True) + NORM_EPS)
    return (y * gain.astype(jnp.float32)).astype(t.dtype)

def rope_tables(positions):
    inv_freq = 1.0 / (ROPE_THETA ** (jnp.arange(0, ROT_DIM, 2, dtype=jnp.float32) / ROT_DIM))
    ang = positions.astype(jnp.float32)[:, None, :, None] * inv_freq
    return jnp.cos(ang), jnp.sin(ang)

def partial_rope(t, cos, sin):
    half = ROT_DIM // 2
    cos = cos.astype(t.dtype)
    sin = sin.astype(t.dtype)
    t1, t2, rest = t[..., :half], t[..., half:ROT_DIM], t[..., ROT_DIM:]
    return jnp.concatenate([t1 * cos - t2 * sin, t2 * cos + t1 * sin, rest], axis=-1)

def masked_softmax(s, valid):
    s = jnp.where(valid, s.astype(jnp.float32), NEG_INF)
    return jax.nn.softmax(s, axis=-1) * valid

def moba_attention(q, k, v):
    B, H, S, dh = q.shape
    Qc = MOBA_Q_CHUNK
    nb = -(-S // MOBA_BLOCK)
    pad = nb * MOBA_BLOCK - S
    kb = jnp.pad(k, ((0, 0), (0, 0), (0, pad), (0, 0))).reshape(B, H, nb, MOBA_BLOCK, dh)
    vb = jnp.pad(v, ((0, 0), (0, 0), (0, pad), (0, 0))).reshape(B, H, nb, MOBA_BLOCK, dh)
    kmean = jnp.mean(kb.astype(jnp.float32), axis=3)
    topk = min(MOBA_TOPK, nb)
    scale = dh ** -0.5
    bi = jnp.arange(B)[:, None, None, None]
    hi = jnp.arange(H)[None, :, None, None]
    blk = jnp.arange(nb)
    off = jnp.arange(MOBA_BLOCK)

    def one_chunk(ci):
        t0 = ci * Qc
        pos = t0 + jnp.arange(Qc)
        own = t0 // MOBA_BLOCK
        qc = lax.dynamic_slice_in_dim(q, t0, Qc, axis=2)
        gate = jnp.einsum('bhqd,bhnd->bhqn', qc.astype(jnp.float32), kmean)
        gate = jnp.where(blk < own, gate, NEG_INF)
        gval, idx = lax.top_k(gate, topk)
        sel_ok = gval > 0.5 * NEG_INF
        k_sel = kb[bi, hi, idx]
        v_sel = vb[bi, hi, idx]
        k_own = lax.dynamic_index_in_dim(kb, own, axis=2, keepdims=False)
        v_own = lax.dynamic_index_in_dim(vb, own, axis=2, keepdims=False)
        s_sel = jnp.einsum('bhqd,bhqnjd->bhqnj', qc, k_sel).reshape(B, H, Qc, topk * MOBA_BLOCK)
        s_own = jnp.einsum('bhqd,bhjd->bhqj', qc, k_own)
        ok_sel = jnp.broadcast_to(sel_ok[..., None], (B, H, Qc, topk, MOBA_BLOCK)).reshape(B, H, Qc, topk * MOBA_BLOCK)
        ok_own = jnp.broadcast_to((own * MOBA_BLOCK + off)[None, :] <= pos[:, None], (B, H, Qc, MOBA_BLOCK))
        p = masked_softmax(jnp.concatenate([s_sel, s_own], axis=-1) * scale,
                           jnp.concatenate([ok_sel, ok_own], axis=-1)).astype(v.dtype)
        p_sel = p[..., :topk * MOBA_BLOCK].reshape(B, H, Qc, topk, MOBA_BLOCK)
        p_own = p[..., topk * MOBA_BLOCK:]
        return (jnp.einsum('bhqnj,bhqnjd->bhqd', p_sel, v_sel)
                + jnp.einsum('bhqj,bhjd->bhqd', p_own, v_own))

    out = lax.map(one_chunk, jnp.arange(S // Qc))
    return out.transpose(1, 2, 0, 3, 4).reshape(B, H, S, dh)

def nsa_compress(t, pos_emb, w1, w2):
    S = t.shape[2]
    ncmp = (S - NSA_CMP_LEN) // NSA_CMP_STRIDE + 1
    idx = np.arange(ncmp)[:, None] * NSA_CMP_STRIDE + np.arange(NSA_CMP_LEN)[None, :]
    blocks = t[:, :, idx] + pos_emb
    hid = jax.nn.silu(jnp.einsum('bgnld,lde->bgne', blocks, w1))
    return jnp.einsum('bgne,ed->bgnd', hid, w2)

def nsa_overlap(ncmp, nsel):
    cs = np.arange(ncmp) * NSA_CMP_STRIDE
    ss = np.arange(nsel) * NSA_SEL_BLOCK
    ov = np.minimum(cs[:, None] + NSA_CMP_LEN, ss[None, :] + NSA_SEL_BLOCK) - np.maximum(cs[:, None], ss[None, :])
    return jnp.asarray(np.clip(ov, 0, None) / NSA_CMP_LEN, dtype=jnp.float32)

def nsa_attention(q, kc, vc, ks, vs, kw, vw, gates):
    B, H, S, dh = q.shape
    G, R, Qc, SB, W = NSA_KV_HEADS, NSA_GROUP, NSA_Q_CHUNK, NSA_SEL_BLOCK, NSA_WINDOW
    ncmp = kc.shape[2]
    nsel = S // SB
    topk = min(NSA_SEL_TOPK, nsel)
    scale = dh ** -0.5
    cmp_end = jnp.arange(ncmp) * NSA_CMP_STRIDE + NSA_CMP_LEN - 1
    overlap = nsa_overlap(ncmp, nsel)
    ksb = ks.reshape(B, G, nsel, SB, dh)
    vsb = vs.reshape(B, G, nsel, SB, dh)
    kwp = jnp.pad(kw, ((0, 0), (0, 0), (W, 0), (0, 0)))
    vwp = jnp.pad(vw, ((0, 0), (0, 0), (W, 0), (0, 0)))
    bi = jnp.arange(B)[:, None, None, None]
    gi = jnp.arange(G)[None, :, None, None]
    sel_blk = jnp.arange(nsel)
    sel_off = jnp.arange(SB)
    win_off = jnp.arange(W + Qc)

    def one_chunk(ci):
        t0 = ci * Qc
        pos = t0 + jnp.arange(Qc)
        qg = lax.dynamic_slice_in_dim(q, t0, Qc, axis=2).reshape(B, G, R, Qc, dh)
        g = lax.dynamic_slice_in_dim(gates, t0, Qc, axis=2).reshape(B, G, R, Qc, 3)
        ok_c = cmp_end[None, :] <= pos[:, None]
        p_c = masked_softmax(jnp.einsum('bgrqd,bgnd->bgrqn', qg, kc) * scale, ok_c)
        o_c = jnp.einsum('bgrqn,bgnd->bgrqd', p_c.astype(vc.dtype), vc)
        imp = jnp.einsum('bgqn,nm->bgqm', p_c.sum(axis=2), overlap)
        cur = pos // SB
        ok_blk = sel_blk[None, :] <= cur[:, None]
        forced = ok_blk & ((sel_blk[None, :] == 0) | (sel_blk[None, :] >= cur[:, None] - 1))
        score = jnp.where(ok_blk, jnp.where(forced, NSA_FORCE, imp), NEG_INF)
        sval, idx = lax.top_k(score, topk)
        sel_ok = sval > 0.5 * NEG_INF
        k_sel = ksb[bi, gi, idx]
        v_sel = vsb[bi, gi, idx]
        tok = idx[..., None] * SB + sel_off
        ok_s = (sel_ok[..., None] & (tok <= pos[None, None, :, None, None])).reshape(B, G, 1, Qc, topk * SB)
        s_s = jnp.einsum('bgrqd,bgqnjd->bgrqnj', qg, k_sel).reshape(B, G, R, Qc, topk * SB) * scale
        p_s = masked_softmax(s_s, ok_s).astype(vs.dtype).reshape(B, G, R, Qc, topk, SB)
        o_s = jnp.einsum('bgrqnj,bgqnjd->bgrqd', p_s, v_sel)
        k_w = lax.dynamic_slice_in_dim(kwp, t0, W + Qc, axis=2)
        v_w = lax.dynamic_slice_in_dim(vwp, t0, W + Qc, axis=2)
        kpos = t0 - W + win_off
        ok_w = (kpos[None, :] <= pos[:, None]) & (kpos[None, :] > pos[:, None] - W) & (kpos[None, :] >= 0)
        p_w = masked_softmax(jnp.einsum('bgrqd,bgkd->bgrqk', qg, k_w) * scale, ok_w)
        o_w = jnp.einsum('bgrqk,bgkd->bgrqd', p_w.astype(vw.dtype), v_w)
        o = g[..., 0:1] * o_c + g[..., 1:2] * o_s + g[..., 2:3] * o_w
        return o.reshape(B, H, Qc, dh)

    out = lax.map(one_chunk, jnp.arange(S // Qc))
    return out.transpose(1, 2, 0, 3, 4).reshape(B, H, S, dh)

def to_heads(t, n_heads):
    B, S, _ = t.shape
    return t.reshape(B, S, n_heads, HEAD_DIM).transpose(0, 2, 1, 3)

def qk_prep(t, gain, cos, sin):
    return partial_rope(rms_norm(t, gain), cos, sin)

def sparse_mixer(h, cos, sin, w_in, w_out, moba_qn, moba_kn, nsa_qn, nsa_kn, cmp_pos, cmp_w1, cmp_w2):
    B, S, _ = h.shape
    mq, mk, mv, nq, nkv, ng = jnp.split(h @ w_in, SPARSE_SPLITS, axis=-1)
    o_moba = moba_attention(qk_prep(to_heads(mq, MOBA_HEADS), moba_qn, cos, sin),
                            qk_prep(to_heads(mk, MOBA_HEADS), moba_kn, cos, sin),
                            to_heads(mv, MOBA_HEADS))
    kv = nkv.reshape(B, S, 3, 2, NSA_KV_HEADS, HEAD_DIM).transpose(2, 3, 0, 4, 1, 5)
    kc = nsa_compress(qk_prep(kv[0, 0], nsa_kn[0], cos, sin), cmp_pos[0], cmp_w1[0], cmp_w2[0])
    vc = nsa_compress(kv[0, 1], cmp_pos[1], cmp_w1[1], cmp_w2[1])
    gates = jax.nn.sigmoid(ng).reshape(B, S, 3, NSA_HEADS).transpose(0, 3, 1, 2)
    o_nsa = nsa_attention(qk_prep(to_heads(nq, NSA_HEADS), nsa_qn, cos, sin), kc, vc,
                          qk_prep(kv[1, 0], nsa_kn[1], cos, sin), kv[1, 1],
                          qk_prep(kv[2, 0], nsa_kn[2], cos, sin), kv[2, 1], gates)
    o = jnp.concatenate([o_moba, o_nsa], axis=1).transpose(0, 2, 1, 3).reshape(B, S, SPARSE_OUT)
    return o @ w_out

def diff_mixer(h, cos, sin, w_in, w_out, q_norm, k_norm, lam_params, out_norm, lam_init):
    B, S, _ = h.shape
    H, Qc = DIFF_HEADS, DIFF_Q_CHUNK
    qk_w = H * 2 * DIFF_QK_DIM
    q, k, v = jnp.split(h @ w_in, [qk_w, 2 * qk_w], axis=-1)
    cos5, sin5 = cos[:, :, None], sin[:, :, None]
    q = partial_rope(rms_norm(q.reshape(B, S, H, 2, DIFF_QK_DIM).transpose(0, 2, 3, 1, 4), q_norm), cos5, sin5)
    k = partial_rope(rms_norm(k.reshape(B, S, H, 2, DIFF_QK_DIM).transpose(0, 2, 3, 1, 4), k_norm), cos5, sin5)
    v = v.reshape(B, S, H, DIFF_V_DIM).transpose(0, 2, 1, 3)
    lp = lam_params.astype(jnp.float32)
    lam = jnp.exp(jnp.sum(lp[0] * lp[1])) - jnp.exp(jnp.sum(lp[2] * lp[3])) + lam_init
    scale = DIFF_QK_DIM ** -0.5
    key_idx = jnp.arange(S)

    def one_chunk(ci):
        t0 = ci * Qc
        pos = t0 + jnp.arange(Qc)
        qc = lax.dynamic_slice_in_dim(q, t0, Qc, axis=3)
        s = jnp.einsum('bhcqd,bhckd->bhcqk', qc, k) * scale
        p = masked_softmax(s, key_idx[None, :] <= pos[:, None])
        a = p[:, :, 0] - lam * p[:, :, 1]
        return jnp.einsum('bhqk,bhkd->bhqd', a.astype(v.dtype), v)

    o = lax.map(one_chunk, jnp.arange(S // Qc)).transpose(1, 2, 0, 3, 4).reshape(B, H, S, DIFF_V_DIM)
    o = rms_norm(o, out_norm) * (1.0 - lam_init)
    return o.transpose(0, 2, 1, 3).reshape(B, S, DIFF_OUT) @ w_out

def swiglu(h, w_gate, w_up, w_down):
    return (jax.nn.silu(h @ w_gate) * (h @ w_up)) @ w_down

def first_inputs(seed: int = 0) -> dict:
    key = jax.random.key(seed)
    keys = iter(jax.random.split(key, 40))
    n_even = (DEPTH + 1) // 2
    n_odd = DEPTH // 2

    def nrm(shape, scale):
        return jax.random.normal(next(keys), shape, jnp.float32) * scale

    def gain(shape):
        return 1.0 + nrm(shape, 0.05)

    offsets = jax.random.randint(next(keys), (BATCH, 1), 0, 1024, dtype=jnp.int32)
    positions = offsets + jnp.arange(SEQ, dtype=jnp.int32)[None, :]
    return {
        'x': nrm((BATCH, SEQ, D_MODEL), 1.0),
        'c': nrm((BATCH, D_MODEL), 1.0),
        'positions': positions,
        'ada_w': nrm((DEPTH, D_MODEL, 6 * D_MODEL), 0.5 * D_MODEL ** -0.5),
        'ada_b': nrm((DEPTH, 6 * D_MODEL), 0.02),
        'attn_norm': gain((DEPTH, D_MODEL)),
        'ffn_norm': gain((DEPTH, D_MODEL)),
        'ffn_w_gate': nrm((DEPTH, D_MODEL, FFN_HIDDEN), D_MODEL ** -0.5),
        'ffn_w_up': nrm((DEPTH, D_MODEL, FFN_HIDDEN), D_MODEL ** -0.5),
        'ffn_w_down': nrm((DEPTH, FFN_HIDDEN, D_MODEL), FFN_HIDDEN ** -0.5),
        'sp_w_in': nrm((n_even, D_MODEL, SPARSE_IN), D_MODEL ** -0.5),
        'sp_w_out': nrm((n_even, SPARSE_OUT, D_MODEL), SPARSE_OUT ** -0.5),
        'moba_q_norm': gain((n_even, HEAD_DIM)),
        'moba_k_norm': gain((n_even, HEAD_DIM)),
        'nsa_q_norm': gain((n_even, HEAD_DIM)),
        'nsa_k_norm': gain((n_even, 3, HEAD_DIM)),
        'nsa_cmp_pos': nrm((n_even, 2, NSA_CMP_LEN, HEAD_DIM), 0.1),
        'nsa_cmp_w1': nrm((n_even, 2, NSA_CMP_LEN, HEAD_DIM, NSA_CMP_HIDDEN), (NSA_CMP_LEN * HEAD_DIM) ** -0.5),
        'nsa_cmp_w2': nrm((n_even, 2, NSA_CMP_HIDDEN, HEAD_DIM), NSA_CMP_HIDDEN ** -0.5),
        'diff_w_in': nrm((n_odd, D_MODEL, DIFF_IN), D_MODEL ** -0.5),
        'diff_w_out': nrm((n_odd, DIFF_OUT, D_MODEL), DIFF_OUT ** -0.5),
        'diff_q_norm': gain((n_odd, DIFF_QK_DIM)),
        'diff_k_norm': gain((n_odd, DIFF_QK_DIM)),
        'diff_lambda': nrm((n_odd, 4, DIFF_QK_DIM), 0.1),
        'diff_out_norm': gain((n_odd, DIFF_V_DIM)),
    }

def first_block(x, c, positions, ada_w, ada_b, attn_norm, ffn_norm, ffn_w_gate, ffn_w_up, ffn_w_down,
              sp_w_in, sp_w_out, moba_q_norm, moba_k_norm, nsa_q_norm, nsa_k_norm, nsa_cmp_pos,
              nsa_cmp_w1, nsa_cmp_w2, diff_w_in, diff_w_out, diff_q_norm, diff_k_norm, diff_lambda,
              diff_out_norm):
    cos, sin = rope_tables(positions)
    for i in range(DEPTH):
        mod = jax.nn.silu(c) @ ada_w[i] + ada_b[i]
        sh_a, sc_a, g_a, sh_f, sc_f, g_f = jnp.split(mod[:, None, :], 6, axis=-1)
        h = rms_norm(x, attn_norm[i]) * (1.0 + sc_a) + sh_a
        j = i // 2
        if i % 2 == 0:
            y = sparse_mixer(h, cos, sin, sp_w_in[j], sp_w_out[j], moba_q_norm[j], moba_k_norm[j],
                             nsa_q_norm[j], nsa_k_norm[j], nsa_cmp_pos[j], nsa_cmp_w1[j], nsa_cmp_w2[j])
        else:
            lam_init = 0.8 - 0.6 * float(np.exp(-0.3 * i))
            y = diff_mixer(h, cos, sin, diff_w_in[j], diff_w_out[j], diff_q_norm[j], diff_k_norm[j],
                           diff_lambda[j], diff_out_norm[j], lam_init)
        x = x + g_a * y
        h = rms_norm(x, ffn_norm[i]) * (1.0 + sc_f) + sh_f
        x = x + g_f * swiglu(h, ffn_w_gate[i], ffn_w_up[i], ffn_w_down[i])
    return x


GRID_W = 64
CTX_LEN = 256
N_MIXERS = 3
EPS = 1e-6
POOL_WINDOWS = (2, 4, 8, 16)
POOL_GROUPS = 4
POOL_GW = D_MODEL // POOL_GROUPS
HEAD_DIM_2 = 128
N_HEADS = D_MODEL // HEAD_DIM_2
N_KV_HEADS = N_HEADS // 2
QKV_WIDTH = (N_HEADS + 2 * N_KV_HEADS) * HEAD_DIM_2
ROPE_BASE = 10000.0
Q_BLOCK = 128
CHUNK = 128
GMLP_HALF = 2 * D_MODEL
GMLP_GROUPS = 8
GMLP_GW = GMLP_HALF // GMLP_GROUPS
D_FF = 4 * D_MODEL


def n_layers_of(kind):
    return len(range(kind, DEPTH, N_MIXERS))

def rms_norm_2(x, g):
    xf = x.astype(jnp.float32)
    y = xf * lax.rsqrt(jnp.mean(xf * xf, axis=-1, keepdims=True) + EPS)
    return (y * g.astype(jnp.float32)).astype(x.dtype)

def layer_norm(x, g, b):
    xf = x.astype(jnp.float32)
    mu = jnp.mean(xf, axis=-1, keepdims=True)
    xc = xf - mu
    y = xc * lax.rsqrt(jnp.mean(xc * xc, axis=-1, keepdims=True) + EPS)
    return (y * g.astype(jnp.float32) + b.astype(jnp.float32)).astype(x.dtype)

def modulate(h, shift, scale):
    return h * (1 + scale[:, None, :]) + shift[:, None, :]

def pool_mix(h, w, scale):
    B, L, D = h.shape
    hf = h.astype(jnp.float32)
    cs = jnp.concatenate([jnp.zeros((B, 1, D), jnp.float32), jnp.cumsum(hf, axis=1)], axis=1)
    csg = cs.reshape(B, L + 1, POOL_GROUPS, POOL_GW)
    hg = hf.reshape(B, L, POOL_GROUPS, POOL_GW)
    pos = jnp.arange(L)
    outs = []
    for g, win in enumerate(POOL_WINDOWS):
        lo = jnp.clip(pos - win // 2, 0, L)
        hi = jnp.clip(pos + win - win // 2, 0, L)
        s = jnp.take(csg[:, :, g], hi, axis=1) - jnp.take(csg[:, :, g], lo, axis=1)
        cnt = (hi - lo).astype(jnp.float32)[None, :, None]
        outs.append(s / cnt - hg[:, :, g])
    p = jnp.stack(outs, axis=2).astype(h.dtype)
    y = jnp.einsum("blgc,gcd->blgd", p, w).reshape(B, L, D)
    return y * scale

def axial_rope_tables(L):
    rows_n = L // GRID_W
    row = jnp.repeat(jnp.arange(rows_n), GRID_W).astype(jnp.float32)
    col = jnp.tile(jnp.arange(GRID_W), rows_n).astype(jnp.float32)
    half = HEAD_DIM_2 // 2
    inv = ROPE_BASE ** (-jnp.arange(0, half, 2, dtype=jnp.float32) / half)
    ang_r = row[:, None] * inv[None, :]
    ang_c = col[:, None] * inv[None, :]
    return jnp.cos(ang_r), jnp.sin(ang_r), jnp.cos(ang_c), jnp.sin(ang_c)

def rotate(x, cos, sin):
    x1, x2 = jnp.split(x, 2, axis=-1)
    cos = cos[None, :, None, :]
    sin = sin[None, :, None, :]
    return jnp.concatenate([x1 * cos - x2 * sin, x1 * sin + x2 * cos], axis=-1)

def apply_axial_rope(x, tables):
    cr, sr, cc, scol = tables
    xf = x.astype(jnp.float32)
    xr, xc = jnp.split(xf, 2, axis=-1)
    return jnp.concatenate([rotate(xr, cr, sr), rotate(xc, cc, scol)], axis=-1).astype(x.dtype)

def gqa_core(q, k, v):
    B, Lq = q.shape[0], q.shape[1]
    G = N_HEADS // N_KV_HEADS
    qg = q.reshape(B, Lq, N_KV_HEADS, G, HEAD_DIM_2)
    s = jnp.einsum("bqkgd,bskd->bkgqs", qg, k).astype(jnp.float32) * (HEAD_DIM_2 ** -0.5)
    p = jax.nn.softmax(s, axis=-1).astype(v.dtype)
    o = jnp.einsum("bkgqs,bskd->bqkgd", p, v)
    return o.reshape(B, Lq, N_HEADS * HEAD_DIM_2)

def qkv_proj(h, w_qkv, q_g, k_g):
    B, L, _ = h.shape
    qkv = h @ w_qkv
    q, k, v = jnp.split(qkv, [N_HEADS * HEAD_DIM_2, (N_HEADS + N_KV_HEADS) * HEAD_DIM_2], axis=-1)
    q = rms_norm_2(q.reshape(B, L, N_HEADS, HEAD_DIM_2), q_g)
    k = rms_norm_2(k.reshape(B, L, N_KV_HEADS, HEAD_DIM_2), k_g)
    v = v.reshape(B, L, N_KV_HEADS, HEAD_DIM_2)
    return q, k, v

def attn_mix(h_ctx, h_lat, w_qkv, w_o, q_g, k_g, ctx_out):
    B, S, _ = h_lat.shape
    qc, kc, vc = qkv_proj(h_ctx, w_qkv, q_g, k_g)
    ql, kl, vl = qkv_proj(h_lat, w_qkv, q_g, k_g)
    tables = axial_rope_tables(S)
    ql = apply_axial_rope(ql, tables)
    kl = apply_axial_rope(kl, tables)
    k_all = jnp.concatenate([kc, kl], axis=1)
    v_all = jnp.concatenate([vc, vl], axis=1)
    nb = S // Q_BLOCK
    qb = ql.reshape(B, nb, Q_BLOCK, N_HEADS, HEAD_DIM_2).transpose(1, 0, 2, 3, 4)
    ob = lax.map(lambda qq: gqa_core(qq, k_all, v_all), qb)
    y_lat = ob.transpose(1, 0, 2, 3).reshape(B, S, N_HEADS * HEAD_DIM_2) @ w_o
    y_ctx = gqa_core(qc, kc, vc) @ w_o if ctx_out else None
    return y_ctx, y_lat

def gmlp_mix(h, w_in, ln_g, ln_b, ws, bs, w_out):
    B, L, _ = h.shape
    z = jax.nn.gelu(h @ w_in)
    u, v = jnp.split(z, 2, axis=-1)
    v = layer_norm(v, ln_g, ln_b)
    vg = v.reshape(B, L // CHUNK, CHUNK, GMLP_GROUPS, GMLP_GW)
    sv = jnp.einsum("gqp,bnpgc->bnqgc", ws, vg) + bs.T[None, None, :, :, None]
    return (u * sv.reshape(B, L, GMLP_HALF)) @ w_out

def sq_relu_mlp(h, w1, w2):
    return jnp.square(jax.nn.relu(h @ w1)) @ w2

def second_inputs(seed: int = 0) -> dict:
    key = jax.random.key(seed)
    ks = jax.random.split(key, 24)
    f32 = jnp.float32
    D = D_MODEL
    nP, nA, nG = n_layers_of(0), n_layers_of(1), n_layers_of(2)

    def nrm(k, shape, s):
        return jax.random.normal(k, shape, f32) * s

    return {
        "x": nrm(ks[0], (BATCH, SEQ, D), 1.0),
        "c": nrm(ks[1], (BATCH, D), 1.0),
        "ctx": nrm(ks[2], (BATCH, CTX_LEN, D), 1.0),
        "c_ctx": nrm(ks[3], (D,), 1.0),
        "ada_w": nrm(ks[4], (DEPTH, D, 6 * D), 0.5 * D ** -0.5),
        "ada_b": nrm(ks[5], (DEPTH, 6 * D), 0.02),
        "norm_g": 1.0 + nrm(ks[6], (DEPTH, 2, D), 0.02),
        "mlp_w1": nrm(ks[7], (DEPTH, D, D_FF), D ** -0.5),
        "mlp_w2": nrm(ks[8], (DEPTH, D_FF, D), D_FF ** -0.5),
        "pool_w": nrm(ks[9], (nP, POOL_GROUPS, POOL_GW, POOL_GW), POOL_GW ** -0.5),
        "pool_scale": 1.0 + nrm(ks[10], (nP, D), 0.02),
        "attn_w_qkv": nrm(ks[11], (nA, D, QKV_WIDTH), D ** -0.5),
        "attn_w_o": nrm(ks[12], (nA, N_HEADS * HEAD_DIM_2, D), (N_HEADS * HEAD_DIM_2) ** -0.5),
        "attn_q_g": 1.0 + nrm(ks[13], (nA, HEAD_DIM_2), 0.02),
        "attn_k_g": 1.0 + nrm(ks[14], (nA, HEAD_DIM_2), 0.02),
        "gm_w_in": nrm(ks[15], (nG, D, 2 * GMLP_HALF), D ** -0.5),
        "gm_ln_g": 1.0 + nrm(ks[16], (nG, GMLP_HALF), 0.02),
        "gm_ln_b": nrm(ks[17], (nG, GMLP_HALF), 0.02),
        "gm_ws": nrm(ks[18], (nG, GMLP_GROUPS, CHUNK, CHUNK), CHUNK ** -0.5),
        "gm_bs": nrm(ks[19], (nG, GMLP_GROUPS, CHUNK), 0.02),
        "gm_w_out": nrm(ks[20], (nG, GMLP_HALF, D), GMLP_HALF ** -0.5),
        "final_g": 1.0 + nrm(ks[21], (D,), 0.02),
    }

def second_block(x, c, ctx, c_ctx, ada_w, ada_b, norm_g, mlp_w1, mlp_w2, pool_w, pool_scale,
              attn_w_qkv, attn_w_o, attn_q_g, attn_k_g, gm_w_in, gm_ln_g, gm_ln_b, gm_ws, gm_bs,
              gm_w_out, final_g):
    last_ctx_read = max([i for i in range(DEPTH) if i % N_MIXERS == 1], default=-1)
    s_lat = jax.nn.silu(c)
    s_ctx = jax.nn.silu(c_ctx)[None, :]
    h_lat, h_ctx = x, ctx
    for i in range(DEPTH):
        kind, j = i % N_MIXERS, i // N_MIXERS
        ctx_in = i <= last_ctx_read
        ctx_out = i < last_ctx_read
        sh1, sc1, g1, sh2, sc2, g2 = jnp.split(s_lat @ ada_w[i] + ada_b[i], 6, axis=-1)
        a_l = modulate(rms_norm_2(h_lat, norm_g[i, 0]), sh1, sc1)
        if ctx_in:
            csh1, csc1, cg1, csh2, csc2, cg2 = jnp.split(s_ctx @ ada_w[i] + ada_b[i], 6, axis=-1)
            a_c = modulate(rms_norm_2(h_ctx, norm_g[i, 0]), csh1, csc1)
        y_c = None
        if kind == 0:
            y_l = pool_mix(a_l, pool_w[j], pool_scale[j])
            if ctx_out:
                y_c = pool_mix(a_c, pool_w[j], pool_scale[j])
        elif kind == 1:
            y_c, y_l = attn_mix(a_c, a_l, attn_w_qkv[j], attn_w_o[j], attn_q_g[j], attn_k_g[j], ctx_out)
        else:
            y_l = gmlp_mix(a_l, gm_w_in[j], gm_ln_g[j], gm_ln_b[j], gm_ws[j], gm_bs[j], gm_w_out[j])
            if ctx_out:
                y_c = gmlp_mix(a_c, gm_w_in[j], gm_ln_g[j], gm_ln_b[j], gm_ws[j], gm_bs[j], gm_w_out[j])
        h_lat = h_lat + g1[:, None, :] * y_l
        m_l = modulate(rms_norm_2(h_lat, norm_g[i, 1]), sh2, sc2)
        h_lat = h_lat + g2[:, None, :] * sq_relu_mlp(m_l, mlp_w1[i], mlp_w2[i])
        if ctx_out:
            h_ctx = h_ctx + cg1[:, None, :] * y_c
            m_c = modulate(rms_norm_2(h_ctx, norm_g[i, 1]), csh2, csc2)
            h_ctx = h_ctx + cg2[:, None, :] * sq_relu_mlp(m_c, mlp_w1[i], mlp_w2[i])
    return rms_norm_2(h_lat, final_g)


def setup_inputs(seed=0):
    out = dict(first_inputs(seed))
    for name, value in second_inputs(seed + 1).items():
        if name != "x":
            out[name + "_2"] = value
    return out


def reference(
    x, c, positions, ada_w, ada_b, attn_norm, ffn_norm, ffn_w_gate, ffn_w_up, ffn_w_down,
    sp_w_in, sp_w_out, moba_q_norm, moba_k_norm, nsa_q_norm, nsa_k_norm, nsa_cmp_pos,
    nsa_cmp_w1, nsa_cmp_w2, diff_w_in, diff_w_out, diff_q_norm, diff_k_norm, diff_lambda,
    diff_out_norm, c_2, ctx_2, c_ctx_2, ada_w_2, ada_b_2, norm_g_2, mlp_w1_2, mlp_w2_2,
    pool_w_2, pool_scale_2, attn_w_qkv_2, attn_w_o_2, attn_q_g_2, attn_k_g_2, gm_w_in_2,
    gm_ln_g_2, gm_ln_b_2, gm_ws_2, gm_bs_2, gm_w_out_2, final_g_2,
):
    x = first_block(
        x, c, positions, ada_w, ada_b, attn_norm, ffn_norm, ffn_w_gate, ffn_w_up, ffn_w_down,
        sp_w_in, sp_w_out, moba_q_norm, moba_k_norm, nsa_q_norm, nsa_k_norm, nsa_cmp_pos,
        nsa_cmp_w1, nsa_cmp_w2, diff_w_in, diff_w_out, diff_q_norm, diff_k_norm, diff_lambda,
        diff_out_norm,
    )
    return second_block(
        x, c_2, ctx_2, c_ctx_2, ada_w_2, ada_b_2, norm_g_2, mlp_w1_2, mlp_w2_2, pool_w_2,
        pool_scale_2, attn_w_qkv_2, attn_w_o_2, attn_q_g_2, attn_k_g_2, gm_w_in_2, gm_ln_g_2,
        gm_ln_b_2, gm_ws_2, gm_bs_2, gm_w_out_2, final_g_2,
    )


_drawn_inputs = setup_inputs


def setup_inputs(seed=0):
    import zlib

    import numpy as np

    out = dict(_drawn_inputs(seed))
    spreads = {}
    factors = {'attn_norm': 4.057,
     'moba_q_norm': 8.0,
     'moba_k_norm': 8.0,
     'nsa_q_norm': 8.0,
     'nsa_k_norm': 8.0,
     'nsa_cmp_pos': 7.296,
     'diff_q_norm': 8.0,
     'diff_k_norm': 8.0,
     'diff_out_norm': 5.885,
     'ctx_2': 4.216,
     'norm_g_2': 4.592,
     'pool_scale_2': 8.0,
     'attn_q_g_2': 28.529,
     'attn_k_g_2': 27.093,
     'final_g_2': 8.243}
    for name, (base, spread) in spreads.items():
        noise = np.random.default_rng([zlib.crc32(name.encode()), seed]).standard_normal(out[name].shape)
        drawn = base * np.exp(spread * noise) if base else spread * noise
        out[name] = __import__('jax').numpy.asarray(drawn.astype(out[name].dtype))
    for name, factor in factors.items():
        out[name] = (out[name] * factor).astype(out[name].dtype)
    return out
```

```python
from contextlib import ExitStack

import numpy as np

import concourse.bass as bass
from concourse import mybir

F32 = mybir.dt.float32
F32R = mybir.dt.float32r
BF16 = mybir.dt.bfloat16
I32 = mybir.dt.int32
ALU = mybir.AluOpType
ACT = mybir.ActivationFunctionType
AX = mybir.AxisListType.X

P = 128
D = 1024
S = 256
TT = S // P
KT = D // P
F1 = 2816
F2 = 4096
HD = 64
HD2 = 128
SP_IN = 2840
NCMP = 15
EPS = 1e-6
NEG = -1e30
TWO_PI = 6.283185307179586
LAM_INIT = 0.8 - 0.6 * float(np.exp(-0.3 * 1))
POOL_WINDOWS = (2, 4, 8, 16)

CONST_COLS = {}
_at = 0
for _name, _n in (("ident", 128), ("causal", 256), ("cmp_neg", 32), ("cmp_ok", 32), ("ax_cos", 128), ("ax_sin", 128),
                  ("inv_freq", 8), ("sel0", 128), ("sel1", 128), ("spread", 128), ("headmask", 512)):
    CONST_COLS[_name] = (_at, _at + _n)
    _at += _n
NCONST = _at


def shape_constants():
    c = np.zeros((P, NCONST), np.float32)

    def put(name, value):
        a, b = CONST_COLS[name]
        c[:, a:b] = value.reshape(P, b - a)

    i = np.arange(P)
    put("ident", np.eye(P, dtype=np.float32))
    causal = np.where(i[None, :] <= i[:, None], 0.0, NEG).astype(np.float32)
    put("causal", np.concatenate([causal, causal], 1))
    neg = np.full((P, 2, 16), NEG, np.float32)
    ok = np.zeros((P, 2, 16), np.float32)
    for t in range(TT):
        valid = (np.arange(NCMP) * 16 + 31)[None, :] <= (t * P + i)[:, None]
        neg[:, t, :NCMP] = np.where(valid, 0.0, NEG)
        ok[:, t, :NCMP] = valid
    put("cmp_neg", neg)
    put("cmp_ok", ok)
    half = HD2 // 2
    inv = (np.float32(10000.0) ** (-np.arange(0, half, 2, dtype=np.float32) / np.float32(half))).astype(np.float32)
    tok = (np.arange(TT)[None, :] * P + i[:, None])
    ang = np.stack([(tok // 64).astype(np.float32)[..., None] * inv, (tok % 64).astype(np.float32)[..., None] * inv], 2)
    put("ax_cos", np.cos(ang.astype(np.float64)).astype(np.float32))
    put("ax_sin", np.sin(ang.astype(np.float64)).astype(np.float32))
    rot = HD // 4
    invf = (np.float32(1.0) / (np.float32(500000.0) ** (np.arange(0, rot, 2, dtype=np.float32) / np.float32(rot)))).astype(np.float32)
    put("inv_freq", np.tile(invf, (P, 1)))
    put("sel0", np.tile((i % 32 == 0).astype(np.float32)[:, None], (1, P)))
    put("sel1", np.tile((i % 32 == 1).astype(np.float32)[:, None], (1, P)))
    spread = np.zeros((P, P), np.float32)
    for n in range(NCMP):
        spread[n, n::16] = 1.0
    put("spread", spread)
    hm = np.zeros((P, 8, 64), np.float32)
    for h in range(8):
        hm[h * 16:h * 16 + NCMP, h] = 1.0
    put("headmask", hm)
    pool = np.zeros((4, S, S), np.float32)
    for g, w in enumerate(POOL_WINDOWS):
        for t in range(S):
            lo, hi = max(t - w // 2, 0), min(t + w - w // 2, S)
            pool[g, lo:hi, t] += np.float32(1.0) / np.float32(hi - lo)
            pool[g, t, t] -= 1.0
    pool = pool.reshape(4, TT, P, S).transpose(2, 0, 1, 3).reshape(P, 4 * TT * S)
    return c, np.ascontiguousarray(pool)


def build(nc, x, c, positions, ada_w, ada_b, attn_norm, ffn_norm, ffn_w_gate, ffn_w_up, ffn_w_down,
          sp_w_in, sp_w_out, moba_q_norm, moba_k_norm, nsa_q_norm, nsa_k_norm, nsa_cmp_pos,
          nsa_cmp_w1, nsa_cmp_w2, diff_w_in, diff_w_out, diff_q_norm, diff_k_norm, diff_lambda,
          diff_out_norm, c_2, ctx_2, c_ctx_2, ada_w_2, ada_b_2, norm_g_2, mlp_w1_2, mlp_w2_2,
          pool_w_2, pool_scale_2, attn_w_qkv_2, attn_w_o_2, attn_q_g_2, attn_k_g_2, final_g_2,
          consts, pool_mats, out):
    stack = ExitStack()
    with stack:
        def sb(name, shape, dt=F32):
            return stack.enter_context(nc.sbuf_tensor(name, shape, dt))

        sems = {}

        def sem(name):
            if name not in sems:
                sems[name] = stack.enter_context(nc.semaphore(name))
            return sems[name]

        res = sb("res", [P, 2, TT, D])
        hT_hi = sb("hT_hi", [P, KT, S], F32R)
        hT_lo = sb("hT_lo", [P, KT, S], F32R)
        act_hi = sb("act_hi", [P, 2, 2 * S], F32R)
        act_lo = sb("act_lo", [P, 2, 2 * S], F32R)
        work = sb("work", [P, 16384])
        wraw = sb("wraw", [P, 4, 2048])
        whi = sb("whi", [P, 2, 2048], F32R)
        wlo = sb("wlo", [P, 2, 2048], F32R)
        ring = sb("ring", [P, 2, 2048])
        modrow = sb("modrow", [P, 3, 512])
        gate_b = sb("gate_b", [P, D])
        cst = sb("cst", [P, NCONST])
        ident_r = sb("ident_r", [P, P], F32R)
        causal_r = sb("causal_r", [P, 2 * P], F32R)
        params = sb("params", [P, P])
        paramT = sb("paramT", [P, P])
        cpad = sb("cpad", [P, 2, KT, 32])
        modT = sb("modT", [P, 4, 2, 48])
        modA = sb("modA", [P, 4, 2, 2, KT])
        gains = sb("gains", [P, 8, HD])
        gains2 = sb("gains2", [P, 2, HD2])
        gain_o = sb("gain_o", [P, HD2])
        pos_i = sb("pos_i", [P, TT], I32)
        pos_f = sb("pos_f", [P, TT])
        trig = sb("trig", [P, 2, TT, 8])
        trig_t = sb("trig_t", [P, 2, TT, 8])
        lam_p = sb("lam_p", [P, 4, HD])
        lam_s = sb("lam_s", [P, 8])
        mark = sb("mark", [P, 4])
        stat = sb("stat", [P, 64])
        rstat = sb("rstat", [P, 64])
        expo = sb("expo", [P, 64])
        sums = sb("sums", [P, 2, 2])
        zero16 = sb("zero16", [1, 512], BF16)
        hbuf = sb("hbuf", [P, 2, 512])
        rowsum = sb("rowsum", [P, 48])
        rowmax = sb("rowmax", [P, 2, 4])
        coef = sb("coef", [P, 2, 4])
        gsig = sb("gsig", [P, TT, 24])
        kcs = sb("kcs", [P, 32])
        vcr = sb("vcr", [16, 2 * HD])
        w2k = sb("w2k", [P, 2, 2, HD])
        w2v = sb("w2v", [P, 2, HD])
        cmp_m = sb("cmp_m", [P, 16])
        ps = stack.enter_context(nc.psum_tensor("ps", [P, 8, 512], F32))

        def const(name):
            a, b = CONST_COLS[name]
            return cst[:, a:b]

        def wk(a, n):
            return work[:, a:a + n]

        ident = const("ident")
        D_BANKS = (4, 5, 6, 2)
        ADA_BANK = 7
        xn = wk(12288, 2048).rearrange("p (t n) -> p t n", t=TT)
        full = wk(14336, 2048).rearrange("p (k n) -> p k n", k=KT)
        hid = wk(0, 8192)

        r0 = wk(0, TT * SP_IN).rearrange("p (t n) -> p t n", t=TT)
        kd0 = wk(5680, 2048).rearrange("p (t y g n) -> p t y g n", t=TT, y=4, g=2)
        qt0 = wk(7728, 5120).rearrange("p (r n) -> p r n", r=20)
        cmp_s = wk(14384, 256).rearrange("p (t h n) -> p t h n", t=TT, h=8)
        cmp_T = wk(14640, 256).rearrange("p (t n) -> p t n", t=TT)
        hidr = work[0:64, 14896:15152]
        r1 = wk(0, TT * 3072).rearrange("p (t n) -> p t n", t=TT)
        qt1 = wk(6144, 4096).rearrange("p (r n) -> p r n", r=16)
        kvc = wk(0, 2048).rearrange("p (t n) -> p t n", t=TT)
        kvl = wk(2048, 2048).rearrange("p (t n) -> p t n", t=TT)
        q3 = wk(4096, 2048).rearrange("p (t n) -> p t n", t=TT)
        qt3 = wk(6144, 2048).rearrange("p (r n) -> p r n", r=8)
        kt3 = wk(8192, 2048).rearrange("p (r n) -> p r n", r=4)

        segs = []

        def rows_of(w):
            return w.rearrange("(t p) n -> p t n", p=P)

        def seg(name, kind, srcs, count, width=1024):
            base = segs[-1]["base"] + segs[-1]["count"] if segs else 0
            segs.append(dict(name=name, kind=kind, srcs=srcs, count=count, base=base, width=width))
            return segs[-1]

        SPI, DFI, QKV = rows_of(sp_w_in[0]), rows_of(diff_w_in[0]), rows_of(attn_w_qkv_2[0])
        for n, (a, b) in enumerate(((0, 1024), (1024, 2048), (2048, SP_IN))):
            seg(f"in0_{n}", "row", [SPI[:, :, a:b]], 4, b - a)
        seg("out0", "row", [rows_of(sp_w_out[0])], 4)
        seg("up0", "pair", [rows_of(ffn_w_gate[0]), rows_of(ffn_w_up[0])], 22)
        seg("down0", "down", [rows_of(ffn_w_down[0])], 11)
        for n in range(3):
            seg(f"in1_{n}", "row", [DFI[:, :, n * 1024:(n + 1) * 1024]], 4)
        seg("out1", "row", [rows_of(diff_w_out[0])], 4)
        seg("up1", "pair", [rows_of(ffn_w_gate[1]), rows_of(ffn_w_up[1])], 22)
        seg("down1", "down", [rows_of(ffn_w_down[1])], 11)
        for s_ in range(2):
            seg(f"pool{s_}", "pool", [pool_w_2[0]], 1)
            seg(f"up2{s_}", "up", [rows_of(mlp_w1_2[0])], 16)
            seg(f"down2{s_}", "down", [rows_of(mlp_w2_2[0])], 16)
        seg("kvc", "row", [QKV[:, :, 1024:2048]], 4)
        seg("kvl", "row", [QKV[:, :, 1024:2048]], 4)
        seg("q3", "row", [QKV[:, :, 0:1024]], 4)
        seg("out3", "row", [rows_of(attn_w_o_2[0])], 4)
        seg("up3", "up", [rows_of(mlp_w1_2[1])], 16)
        seg("down3", "down", [rows_of(mlp_w2_2[1])], 16)
        by_name = {s_["name"]: s_ for s_ in segs}
        last_seg = segs[-1]
        UNITS = last_seg["base"] + last_seg["count"]
        LOOPED = ("pair", "up", "down")

        def bodies(s_):
            return (s_["count"] - 2) // 4 if s_["kind"] in LOOPED else 0

        def seg_of(u):
            return next(s_ for s_ in segs if s_["base"] <= u < s_["base"] + s_["count"])

        def unit_source(s_, i, k4=None):
            kind = s_["kind"]
            if kind in ("row", "down"):
                at = 2 * i if k4 is None else k4 * 8 + 2 * i
                return s_["srcs"][0][:, bass.ds(at, 2), :]
            if kind == "pool":
                return s_["srcs"][0].rearrange("g (k p) n -> p (g k) n", p=P)
            if kind == "pair":
                at = (i // 2) * 256 if k4 is None else k4 * 512 + (i // 2) * 256
                return s_["srcs"][i % 2][:, :, bass.ds(at, 256)]
            at = i * 256 if k4 is None else k4 * 1024 + i * 256
            return s_["srcs"][0][:, :, bass.ds(at, 256)]

        def unit_width(s_):
            return 2 * s_["width"] if s_["kind"] == "row" else 2048

        def unit_split(s_):
            return {"row": 2, "down": 2, "pair": 8, "up": 8, "pool": 8}[s_["kind"]]

        raw_full = [sem(f"raw_full{j}") for j in range(4)]
        hi_ready, lo_ready, unit_done = sem("hi_ready"), sem("lo_ready"), sem("unit_done")

        hid_base, n_ = {}, 2
        for s_ in segs:
            if s_["kind"] in ("pair", "up"):
                tag = s_["name"][2:]
                hid_base[tag] = n_
                n_ += s_["count"] // 2 if s_["kind"] == "pair" else s_["count"]
        hid_done, hact_done = sem("hid_done"), sem("hact_done")

        PANELS = 12
        ring_units = []
        STEPS_BEFORE_CMP = 9 + 12
        adaw = [ada_w[0], ada_w[1], ada_w_2[0], ada_w_2[1]]
        adab = [ada_b[0:1], ada_b[1:2], ada_b_2[0:1], ada_b_2[1:2]]
        w1c = nsa_cmp_w1[0].rearrange("s l d e -> s (l d) e").rearrange("s (k p) e -> s p k e", p=P)
        step = 0
        for a in range(PANELS):
            l, p = a // 3, a % 3
            for k in range(9):
                if step == STEPS_BEFORE_CMP:
                    ring_units += [("cmp", s_, h_) for s_ in range(2) for h_ in range(2)]
                step += 1
                if k < 8:
                    ring_units.append(("ada", a, k))
                if k == 7:
                    ring_units.append(("bias", a, 0))
        ring_at = {key: n for n, key in enumerate(ring_units)}
        ring_full = [sem("ring_full0"), sem("ring_full1")]
        ring_used = sem("ring_used")
        ada_rows, ada_turn, ada_cols = sem("ada_rows"), sem("ada_turn"), sem("ada_cols")

        def ring_dma(eng, r):
            if r >= len(ring_units):
                return
            kind, a, b = ring_units[r]
            if r >= 2:
                eng.wait_ge(ring_used, r - 1)
            dst = ring[:, r % 2, :]
            if kind == "ada":
                l, p = a // 3, a % 3
                src = adaw[l][b * P:(b + 1) * P, p * 2048:(p + 1) * 2048]
            elif kind == "bias":
                l, p = a // 3, a % 3
                dst, src = ring[0:1, r % 2, :], adab[l][:, p * 2048:(p + 1) * 2048]
            else:
                dst = dst.rearrange("p (k e) -> p k e", k=8)
                src = w1c[a][:, b * 8:(b + 1) * 8, :]
            eng.dma_start(dst, src).then_inc(ring_full[r % 2], 16)

        def ring_wait(eng, r):
            eng.wait_ge(ring_full[r % 2], 16 * (r // 2 + 1))

        PANEL_KIND = ["rows"] * 3 + ["res", "res"] + ["rows"] * 3 + ["res", "res"] + ["res"] * 4 + ["rows"] * 3 + ["res", "res"]
        act_emptied, dve_emptied = sem("act_emptied"), sem("dve_emptied")
        act_count, dve_count = [0], [0]
        for kind_ in PANEL_KIND:
            act_count.append(act_count[-1] + (2 if kind_ == "rows" else 0))
            dve_count.append(dve_count[-1] + (2 if kind_ == "rows" else 4))
        PANEL_SEGS = ["in0_0", "in0_1", "in0_2", "out0", "down0", "in1_0", "in1_1", "in1_2", "out1", "down1",
                      "pool0", "down20", "pool1", "down21", "kvc", "kvl", "q3", "out3", "down3"]
        panel_end = [by_name[n_]["base"] + by_name[n_]["count"] for n_ in PANEL_SEGS]
        gate_psum, gate_copied = sem("gate_psum"), sem("gate_copied")
        pow_asked, pow_done = sem("pow_asked"), sem("pow_done")
        NPOW = 12 + 3 + 3 + 3

        NORMS = [(0, 0, 0), (0, 0, 1), (0, 1, 0), (0, 1, 1), (0, 2, 0), (0, 2, 1), (1, 2, 0), (1, 2, 1),
                 (1, 3, 0), (0, 3, 0), (0, 3, 1)]
        RESIDUALS_BEFORE = [0, 1, 2, 3, 4, 5, 6, 7, 8, 8, 9, 10]
        GATES = [(0, 0, 0), (0, 0, 1), (1, 0, 0), (1, 0, 1), (2, 0, 0), (2, 0, 1), (2, 1, 0), (2, 1, 1), (3, 0, 0), (3, 0, 1)]
        res_panels = [n for n, k_ in enumerate(PANEL_KIND) if k_ == "res"]

        def pair_rows(rows, r, t):
            return rows[:, t, r * P:(r + 1) * P]

        def q_groups(stage):
            if stage == 0:
                def src(r, t):
                    if r < 8:
                        return r0[:, t, r * P:(r + 1) * P]
                    if r < 12:
                        return r0[:, t, 1536 + (r - 8) * P:1536 + (r - 7) * P]
                    y, g = {12: (2, 0), 13: (2, 1), 14: (3, 0), 15: (3, 1), 16: (0, 0), 17: (0, 1), 18: (1, 0), 19: (1, 1)}[r]
                    return kd0[:, t, y, g, :]
                return [([src(r, t) for r in (2 * g, 2 * g + 1) for t in range(TT)], qt0[:, 2 * g:2 * g + 2, :]) for g in range(10)]
            if stage == 1:
                return [([r1[:, t, r * P:(r + 1) * P] for r in (2 * g, 2 * g + 1) for t in range(TT)],
                         qt1[:, 2 * g:2 * g + 2, :]) for g in range(8)]
            q = [([q3[:, t, r * P:(r + 1) * P] for r in (2 * g, 2 * g + 1) for t in range(TT)],
                  qt3[:, 2 * g:2 * g + 2, :]) for g in range(4)]
            k = [([src[:, t, h * P:(h + 1) * P] for src in (kvc, kvl) for t in range(TT)], kt3[:, h, :]) for h in range(4)]
            return q + k

        class Att:
            pass

        def att(stage):
            a = Att()
            a.n = stage
            a.scores, a.negmax, a.exps = sem(f"a{stage}_scores"), sem(f"a{stage}_negmax"), sem(f"a{stage}_exps")
            a.turned, a.pT, a.pv = sem(f"a{stage}_turned"), sem(f"a{stage}_pT"), sem(f"a{stage}_pv")
            a.taken, a.mixed = sem(f"a{stage}_taken"), sem(f"a{stage}_mixed")
            a.steps = {0: 12, 1: 8, 3: 8}[stage]
            a.width = 512 if stage == 3 else 384
            a.maps = 1 if stage == 1 else 2
            base = {0: 12848, 1: 10240, 3: 10240}[stage]
            a.p = wk(base, 4 * a.width).rearrange("p (b m n) -> p b m n", b=2, m=2)
            base += 4 * a.width
            if stage == 1:
                a.mix = wk(base, 2 * a.width).rearrange("p (b m n) -> p b m n", b=2, m=1)
                base += 2 * a.width
            a.pt = wk(base, 2 * a.maps * a.width).rearrange("p (b m n) -> p b m n", b=2, m=a.maps)
            a.scale = float(HD2 if stage == 3 else HD) ** -0.5
            return a

        ATT = {n: att(n) for n in (0, 1, 3)}
        out_rows = {0: r0, 1: r1, 3: q3}

        block = stack.enter_context(nc.Block())

        @block.sync
        def _(sp):
            ld = sem("small_params")
            sp.dma_start(cst[:, :], consts).then_inc(ld, 16)
            sp.wait_ge(sem("params_zero"), 1)
            sp.dma_start(params[0:16, :], attn_norm.rearrange("l (k n) -> (l k) n", n=P)).then_inc(ld, 16)
            sp.dma_start(params[16:32, :], ffn_norm.rearrange("l (k n) -> (l k) n", n=P)).then_inc(ld, 16)
            sp.dma_start(params[32:64, :], norm_g_2.rearrange("l j (k n) -> (l j k) n", n=P)).then_inc(ld, 16)
            sp.dma_start(params[64:96, :], nsa_cmp_pos[0].rearrange("s (k a) d -> (s k) (a d)", a=2)).then_inc(ld, 16)
            sp.dma_start(params[96:104, :], c.rearrange("b (k n) -> (b k) n", n=P)).then_inc(ld, 16)
            sp.dma_start(params[104:112, :], c_2.rearrange("b (k n) -> (b k) n", n=P)).then_inc(ld, 16)
            sp.dma_start(params[112:120, :], c_ctx_2.rearrange("(k n) -> k n", n=P)).then_inc(ld, 16)
            xl = sem("x_landed")
            sp.dma_start(res[:, 0, :, :], x[0].rearrange("(t p) n -> p t n", p=P)).then_inc(xl, 16)
            sp.dma_start(pos_i[:, :], positions[0].rearrange("(t p) -> p t", p=P), allow_slow_non_contiguous=True).then_inc(xl, 16)

            def weight_dma(s_, i, k4=None):
                u = s_["base"] + i
                slot = u % 4
                if u >= 4 or k4 is not None:
                    sp.wait_ge(lo_ready, u - 3 if k4 is None else k4 * 4 + (u - 3))
                dst = wraw[:, slot, 0:unit_width(s_)].rearrange("p (k n) -> p k n", k=unit_split(s_))
                sp.dma_start(dst, unit_source(s_, i, k4)).then_inc(raw_full[slot], 16)

            for s_ in segs:
                if s_["name"] == "in0_1":
                    g = sem("gains_landed")
                    rows = [moba_q_norm[0:1], moba_k_norm[0:1], nsa_q_norm[0:1], nsa_k_norm[0, 0:1], nsa_k_norm[0, 1:2],
                            nsa_k_norm[0, 2:3], diff_q_norm[0:1], diff_k_norm[0:1]]
                    for n, row in enumerate(rows):
                        sp.dma_start(gains[:, n, :], row.to_broadcast([P, HD])).then_inc(g, 16)
                    sp.dma_start(gains2[:, 0, :], attn_q_g_2[0:1].to_broadcast([P, HD2])).then_inc(g, 16)
                    sp.dma_start(gains2[:, 1, :], attn_k_g_2[0:1].to_broadcast([P, HD2])).then_inc(g, 16)
                    sp.dma_start(gain_o[:, :], diff_out_norm[0:1].to_broadcast([P, HD2])).then_inc(g, 16)
                    for n in range(4):
                        sp.dma_start(lam_p[:, n, :], diff_lambda[0, n:n + 1].to_broadcast([P, HD])).then_inc(g, 16)
                    w2 = nsa_cmp_w2[0].rearrange("s (k p) d -> s p k d", p=P)
                    sp.dma_start(w2k[:, :, 0, :], w2[0]).then_inc(g, 16)
                    sp.dma_start(w2k[:, :, 1, :], w2[0]).then_inc(g, 16)
                    sp.dma_start(w2v[:, :, :], w2[1]).then_inc(g, 16)
                    sp.dma_start(res[:, 1, :, :], ctx_2[0].rearrange("(t p) n -> p t n", p=P)).then_inc(sem("ctx_landed"), 16)
                n = bodies(s_)
                if n:
                    with sp.Fori(0, n) as k4:
                        for j in range(4):
                            weight_dma(s_, j, k4)
                for i in range(4 * n, s_["count"]):
                    weight_dma(s_, i)
            sp.wait_ge(unit_done, UNITS)
            sp.dma_start(wk(0, D), final_g_2.rearrange("(a n) -> a n", a=1).to_broadcast([P, D])).then_inc(sem("final_landed"), 16)
            for t in range(TT):
                sp.wait_ge(sem("out_ready"), t + 1)
                sp.dma_start(out[0, t * P:(t + 1) * P, :], xn[:, t, :]).then_inc(sem("stored"), 16)
            sp.wait_ge(sem("stored"), 16 * TT)

        @block.gpsimd
        def _(pool):
            nc.gpsimd.memset(expo[:, :], -0.5).then_inc(sem("expo_set"), 1)
            pool.wait_ge(sem("expo_set"), 1)
            with pool.Fori(0, NPOW) as n:
                pool.wait_ge(pow_asked, n + 1)
                nc.gpsimd.tensor_tensor(rstat[:, :], stat[:, :], expo[:, :], ALU.pow).then_inc(pow_done, 1)

        @block.scalar
        def _(act):
            chained = [0]
            chain = sem("act_chain")
            ring_next = [0]
            step_no = [0]
            panel_no = [0]
            norm_no = [0]
            gate_no = [0]

            def link(ins):
                chained[0] += 1
                ins.then_inc(chain, 1)
                act.wait_ge(chain, chained[0])

            def ring_fill(upto):
                while ring_next[0] < min(upto, len(ring_units)):
                    ring_dma(act, ring_next[0])
                    ring_next[0] += 1

            def ada_step(n=1):
                for _ in range(n):
                    a, k = step_no[0] // 9, step_no[0] % 9
                    step_no[0] += 1
                    if a < PANELS:
                        last = ring_at[("bias", a, 0)] if k >= 7 else ring_at[("ada", a, k)]
                        ring_fill(last + 3)

            def split_weights(s_, i, k4=None):
                u = s_["base"] + i
                act.wait_ge(raw_full[u % 4], 16 * (u // 4 + 1) if k4 is None else k4 * 16 + 16 * (u // 4 + 1))
                if u >= 2 or k4 is not None:
                    act.wait_ge(unit_done, u - 1 if k4 is None else k4 * 4 + (u - 1))
                if s_["kind"] == "down":
                    if k4 is None:
                        act.wait_ge(hid_done, hid_base[s_["name"][4:]] + i + 1)
                    at = 512 * i if k4 is None else k4 * 2048 + 512 * i
                    nc.scalar.activation(act_hi[:, u % 2, :], hid[:, bass.ds(at, 512)], ACT.Copy)
                w = unit_width(s_)
                nc.scalar.activation(whi[:, u % 2, 0:w], wraw[:, u % 4, 0:w], ACT.Copy).then_inc(hi_ready, 1)

            def split_unit(u):
                if u < UNITS:
                    s_ = seg_of(u)
                    split_weights(s_, u - s_["base"])

            def hidden_out(s_, i, k4=None):
                u = s_["base"] + i
                tag = s_["name"][2:]
                plus = (lambda v: v) if k4 is None else (lambda v: k4 * (2 if s_["kind"] == "pair" else 4) + v)
                if s_["kind"] == "pair":
                    if i % 2:
                        return
                    n = i // 2
                    act.wait_ge(unit_done, u + 1 if k4 is None else k4 * 4 + (u + 1))
                    act.wait_ge(hid_done, plus(hid_base[tag] + n - 1))
                    nc.scalar.activation(hbuf[:, n % 2, :], ps[:, i % 4, :], ACT.Silu).then_inc(hact_done, 1)
                else:
                    act.wait_ge(unit_done, u + 1 if k4 is None else k4 * 4 + (u + 1))
                    b = i % 2
                    act.wait_ge(hid_done, plus(hid_base[tag] + i - 1))
                    nc.scalar.activation(hbuf[:, b, :], ps[:, i % 4, :], ACT.Relu).then_inc(hact_done, 1)
                    act.wait_ge(hact_done, plus(hid_base[tag] + i + 1))
                    at = 512 * i if k4 is None else k4 * 2048 + 512 * i
                    nc.scalar.activation(hid[:, bass.ds(at, 512)], hbuf[:, b, :], ACT.Square).then_inc(hid_done, 1)

            def stream(name, hold_last=False):
                s_ = by_name[name]
                n = bodies(s_)
                if s_["kind"] == "down":
                    act.wait_ge(hid_done, hid_base[name[4:]] + s_["count"])
                if n:
                    with act.Fori(0, n) as k4:
                        for j in range(4):
                            if s_["kind"] != "down":
                                hidden_out(s_, j, k4)
                            split_weights(s_, j + 2, k4)
                for i in range(4 * n, s_["count"]):
                    if s_["kind"] != "down":
                        hidden_out(s_, i)
                    if not (hold_last and i == s_["count"] - 1):
                        split_unit(s_["base"] + i + 2)

            def row_segment(name, hold_last=True, ada=True):
                s_ = by_name[name]
                for i in range(s_["count"]):
                    if ada:
                        ada_step()
                    if not (hold_last and i == s_["count"] - 1):
                        split_unit(s_["base"] + i + 2)

            def held_split(name):
                s_ = by_name[name]
                split_unit(s_["base"] + s_["count"] + 1)

            def panel_rows(rows, col, width):
                n = panel_no[0]
                act.wait_ge(unit_done, panel_end[n])
                for h in range(2):
                    w = min(512, width - 512 * h)
                    nc.scalar.activation(rows[:, 0, col + 512 * h:col + 512 * h + w], ps[:, D_BANKS[h], 0:w], ACT.Copy).then_inc(act_emptied, 1)

            def next_panel():
                panel_no[0] += 1

            def norm(src):
                n = norm_no[0]
                norm_no[0] += 1
                strm, l, f = NORMS[n] if n < len(NORMS) else (0, 0, 0)
                if n > 0:
                    act.wait_ge(sem("hT_ready"), n)
                    act.wait_ge(sem("res_ready"), 2 * RESIDUALS_BEFORE[n])
                if n == 6:
                    act.wait_ge(sem("ctx_landed"), 16)
                for t in range(TT):
                    nc.scalar.activation(xn[:, t, :], res[:, strm, t, :], ACT.Square, accum_out=sums[:, n % 2, t:t + 1]).then_inc(sem("squares"), 1)
                if n >= len(NORMS):
                    return
                for b in range(2):
                    act.wait_ge(sem("xT_psum"), 4 * n + b + 1)
                    if b == 0:
                        act.wait_ge(sem("mod_ready"), 3 * l + (1 if f == 0 else 3))
                    for k in (2 * b, 2 * b + 1):
                        shift = 0.0 if n in (4, 6) else modT[:, l, strm, (0 if f == 0 else 24) + k:(0 if f == 0 else 24) + k + 1]
                        ins = nc.scalar.activation(full[:, k, :], ps[:, b, (k % 2) * S:(k % 2 + 1) * S], ACT.Identity,
                                                   bias=shift, scale=modA[:, l, strm, f, k:k + 1])
                link(ins)
                nc.scalar.activation(hT_hi[:, 0:4, :], full[:, 0:4, :], ACT.Copy).then_inc(sem("hT_hi_act"), 1)

            def gate():
                e = gate_no[0]
                gate_no[0] += 1
                if e > 0:
                    act.wait_ge(dve_emptied, dve_count[res_panels[e - 1] + 1])
                for h in range(2):
                    act.wait_ge(gate_psum, 2 * e + h + 1)
                    nc.scalar.activation(gate_b[:, 512 * h:512 * h + 512], ps[:, D_BANKS[h], :], ACT.Copy).then_inc(gate_copied, 1)

            def turns(stage):
                for g, (_, dst) in enumerate(q_groups(stage)):
                    if g % 2 == 0:
                        act.wait_ge(sem(f"turned{stage}"), g + 1)
                        d = dst if len(dst.shape) == 2 else dst.rearrange("p a b -> p (a b)")
                        nc.scalar.activation(d, ps[:, g % 4, :], ACT.Copy).then_inc(sem(f"turn_act{stage}"), 1)

            def attention(stage):
                a = ATT[stage]

                def exps(i):
                    act.wait_ge(a.negmax, i + 1)
                    if i >= 2:
                        if stage == 1:
                            act.wait_ge(a.mixed, i - 1)
                        else:
                            act.wait_ge(a.turned, i - 1)
                    for m in range(2):
                        bank = 2 * (i % 2) + m
                        if stage == 3:
                            spans = ((0, 512, 0),)
                        else:
                            spans = ((0, 128, 0), (128, 384, 1))
                        for lo, hi, r in spans:
                            col = 4 * i + 2 * m + r if stage != 3 else 2 * i + m
                            bias = rowmax[:, i % 2, 2 * m + r:2 * m + r + 1] if stage != 3 else rowmax[:, i % 2, m:m + 1]
                            ins = nc.scalar.activation(a.p[:, i % 2, m, lo:hi], ps[:, bank, lo:hi], ACT.Exp, bias=bias,
                                                       scale=a.scale, accum_out=rowsum[:, col:col + 1])
                    ins.then_inc(a.exps, 1)

                def copy_pt(i):
                    act.wait_ge(a.turned, i + 1)
                    if i >= 2:
                        act.wait_ge(a.pv, i - 1)
                    if stage == 1:
                        src = ps[:, 4 + i % 2, 0:a.width]
                        dst = a.pt[:, i % 2, 0, :]
                    else:
                        src = ps[:, 4:6, 0:a.width]
                        dst = a.pt[:, i % 2, :, :]
                    nc.scalar.activation(dst, src, ACT.Copy).then_inc(a.pT, 1)

                for i in range(a.steps + 2):
                    if i < a.steps:
                        exps(i)
                    if 1 <= i <= a.steps:
                        copy_pt(i - 1)
                    ada_step()

            def out_turn(stage):
                for b in range(4):
                    act.wait_ge(sem(f"out_turned{stage}"), b + 1)
                    nc.scalar.activation(hT_hi[:, 2 * b:2 * b + 2, :], ps[:, b, :].rearrange("p (k n) -> p k n", k=2), ACT.Copy).then_inc(sem(f"out_hi{stage}"), 1)

            act.wait_ge(sem("paramT_ready"), 1)
            for n, (blk, col) in enumerate(((0, 96), (1, 104), (1, 112))):
                ins = nc.scalar.activation(cpad[:, blk, :, n // 2:n // 2 + 1], paramT[:, col:col + 8].rearrange("p (k a) -> p k a", a=1), ACT.Silu)
            ins.then_inc(sem("silu_c"), 1)
            ring_fill(2)
            act.wait_ge(sem("angles"), 1)
            nc.scalar.activation(trig[:, :, :, :], trig_t[:, :, :, :], ACT.Sin).then_inc(sem("trig_ready"), 1)
            act.wait_ge(sem("cst_r"), 1)
            act.wait_ge(sem("x_landed"), 32)
            split_unit(0)
            split_unit(1)
            ada_step(9)
            norm(0)
            for n, w in enumerate((1024, 1024, 792)):
                row_segment(f"in0_{n}")
                panel_rows(r0, 1024 * n, w)
                next_panel()
                held_split(f"in0_{n}")
            act.wait_ge(dve_emptied, 6)
            act.wait_ge(act_emptied, 6)
            nc.scalar.activation(gsig[:, :, :], r0[:, :, 2816:2840], ACT.Exp, scale=-1.0).then_inc(sem("gsig_exp"), 1)
            act.wait_ge(sem("heads0"), 1)
            for t in range(TT):
                for y, col, w in ((0, 2048, 4), (2, 2304, 2), (3, 2560, 2)):
                    src = r0[:, t, col:col + w * HD].rearrange("p (g d) -> p g d", d=HD)
                    dst = kd0[:, t, :, :, :].rearrange("p y g n -> p (y g) n")[:, 2 * y:2 * y + w, :].rearrange("p g (u d) -> p g u d", u=2)
                    for u_ in range(2):
                        ins = nc.scalar.activation(dst[:, :, u_, :], src, ACT.Copy)
            ins.then_inc(sem("doubled"), 1)
            turns(0)
            c0 = ring_at[("cmp", 0, 0)]
            ring_fill(c0 + 4)
            act.wait_ge(ring_used, c0 + 4)
            act.wait_ge(sem("hidr_zero"), 1)
            for s_ in range(2):
                ins = nc.scalar.activation(hidr[32 * s_:32 * s_ + 30, :], ps[32 * s_:32 * s_ + 30, 0, 0:256], ACT.Silu)
            ins.then_inc(sem("cmp_silu"), 1)
            ring_fill(c0 + 6)
            act.wait_ge(sem("cmp_shift"), 1)
            nc.scalar.activation(cmp_s, cmp_s, ACT.Exp, scale=float(HD) ** -0.5).then_inc(sem("cmp_exp"), 1)
            attention(0)
            out_turn(0)
            gate()
            row_segment("out0")
            next_panel()
            norm(0)
            gate()
            held_split("out0")
            stream("up0")
            stream("down0", hold_last=True)
            next_panel()
            norm(0)
            held_split("down0")
            for n in range(3):
                row_segment(f"in1_{n}")
                panel_rows(r1, 1024 * n, 1024)
                next_panel()
                held_split(f"in1_{n}")
            act.wait_ge(sem("lam_sum"), 1)
            nc.scalar.activation(lam_s[:, 2:4], lam_s[:, 0:2], ACT.Exp).then_inc(sem("lam_exp"), 1)
            turns(1)
            attention(1)
            out_turn(1)
            gate()
            row_segment("out1")
            next_panel()
            norm(0)
            gate()
            held_split("out1")
            stream("up1")
            stream("down1", hold_last=True)
            next_panel()
            ada_step(max(0, 9 * 9 - step_no[0]))
            for s_ in range(2):
                act.wait_ge(unit_done, panel_end[9 if s_ == 0 else 11])
                act.dma_start(wk(0, 2048), pool_mats).then_inc(sem("pool_landed"), 16)
                act.dma_start(wk(2048, D), pool_scale_2[0:1].to_broadcast([P, D])).then_inc(sem("pool_landed"), 16)
                norm(s_)
                if s_ == 0:
                    held_split("down1")
                else:
                    held_split("down20")
                gate_no[0] += 1
                split_unit(by_name[f"pool{s_}"]["base"] + 2)
                next_panel()
                norm(s_)
                gate()
                stream(f"up2{s_}")
                stream(f"down2{s_}", hold_last=True)
                next_panel()
            ada_step(max(0, 9 * 12 - step_no[0]))
            norm(1)
            held_split("down21")
            row_segment("kvc", ada=False)
            panel_rows(kvc, 0, 1024)
            next_panel()
            norm(0)
            held_split("kvc")
            for name, rows in (("kvl", kvl), ("q3", q3)):
                row_segment(name, ada=False)
                panel_rows(rows, 0, 1024)
                next_panel()
                held_split(name)
            turns(3)
            attention(3)
            out_turn(3)
            gate()
            row_segment("out3", ada=False)
            next_panel()
            norm(0)
            gate()
            held_split("out3")
            stream("up3")
            stream("down3")
            next_panel()
            norm(0)

        @block.vector
        def _(dve):
            chained = [0]
            chain = sem("dve_chain")
            step_no = [0]
            panel_no = [0]
            norm_no = [0]
            gate_no = [0]
            pows = [0]

            def link(ins):
                chained[0] += 1
                ins.then_inc(chain, 1)
                dve.wait_ge(chain, chained[0])

            def ada_step(n=1):
                for _ in range(n):
                    a, k = step_no[0] // 9, step_no[0] % 9
                    step_no[0] += 1
                    if a >= PANELS:
                        continue
                    l, p = a // 3, a % 3
                    if k == 7:
                        dve.wait_ge(ring_used, ring_at[("bias", a, 0)] + 1)
                        nc.vector.tensor_copy(modrow[:, p, :], ps[:, ADA_BANK, :]).then_inc(ada_rows, 1)
                    if k == 8:
                        dve.wait_ge(ada_turn, a + 1)
                        for strm in range(2 if l >= 2 else 1):
                            src = ps[:, ADA_BANK, :].rearrange("p (q j r) -> p q j r", q=4, r=32)[:, :, :, strm]
                            dst = modT[:, l, strm, p * 16:p * 16 + 16].rearrange("p (j q) -> p q j", q=4)
                            ins = nc.vector.tensor_copy(dst, src)
                        ins.then_inc(ada_cols, 1)
                        dve.wait_ge(ada_cols, a + 1)
                        ins = None
                        for strm in range(2 if l >= 2 else 1):
                            if p in (0, 2):
                                f = 0 if p == 0 else 1
                                at = 8 if p == 0 else 32
                                g = {0: 8 * l, 1: 16 + 8 * l}[f] if l < 2 else 32 + (l - 2) * 16 + 8 * f
                                ins = nc.vector.scalar_tensor_tensor(out=modA[:, l, strm, f, :], in0=modT[:, l, strm, at:at + 8], scalar=1.0,
                                                                     in1=paramT[:, g:g + 8], op0=ALU.add, op1=ALU.mult)
                            elif strm == 0:
                                ins = nc.vector.memset(mark[:, 0:1], 0.0)
                        ins.then_inc(sem("mod_ready"), 1)
                        dve.wait_ge(sem("mod_ready"), a + 1)

            def split_weights(s_, i, k4=None):
                u = s_["base"] + i
                dve.wait_ge(hi_ready, u + 1 if k4 is None else k4 * 4 + (u + 1))
                if s_["kind"] == "down":
                    at = 512 * i if k4 is None else k4 * 2048 + 512 * i
                    nc.vector.tensor_tensor(act_lo[:, u % 2, :], hid[:, bass.ds(at, 512)], act_hi[:, u % 2, :].bitcast(F32), ALU.subtract)
                w = unit_width(s_)
                nc.vector.tensor_tensor(wlo[:, u % 2, 0:w], wraw[:, u % 4, 0:w], whi[:, u % 2, 0:w].bitcast(F32), ALU.subtract).then_inc(lo_ready, 1)

            def split_unit(u):
                if u < UNITS:
                    s_ = seg_of(u)
                    split_weights(s_, u - s_["base"])

            def hidden_out(s_, i, k4=None):
                if s_["kind"] != "pair" or i % 2 == 0:
                    return
                u = s_["base"] + i
                n = i // 2
                hb = hid_base[s_["name"][2:]]
                dve.wait_ge(unit_done, u + 1 if k4 is None else k4 * 4 + (u + 1))
                dve.wait_ge(hact_done, hb + n + 1 if k4 is None else k4 * 2 + (hb + n + 1))
                at = 512 * n if k4 is None else k4 * 1024 + 512 * n
                nc.vector.tensor_tensor(hid[:, bass.ds(at, 512)], ps[:, i % 4, :], hbuf[:, n % 2, :], ALU.mult).then_inc(hid_done, 1)

            def stream(name, hold_last=False):
                s_ = by_name[name]
                n = bodies(s_)
                if n:
                    with dve.Fori(0, n) as k4:
                        for j in range(4):
                            hidden_out(s_, j, k4)
                            split_weights(s_, j + 2, k4)
                for i in range(4 * n, s_["count"]):
                    hidden_out(s_, i)
                    if not (hold_last and i == s_["count"] - 1):
                        split_unit(s_["base"] + i + 2)

            def row_segment(name, hold_last=True, ada=True):
                s_ = by_name[name]
                for i in range(s_["count"]):
                    if ada:
                        ada_step()
                    if not (hold_last and i == s_["count"] - 1):
                        split_unit(s_["base"] + i + 2)

            def held_split(name):
                s_ = by_name[name]
                split_unit(s_["base"] + s_["count"] + 1)

            def panel_rows(rows, col, width):
                dve.wait_ge(unit_done, panel_end[panel_no[0]])
                panel_no[0] += 1
                for h in range(2):
                    w = min(512, width - 512 * h)
                    nc.vector.tensor_copy(rows[:, 1, col + 512 * h:col + 512 * h + w], ps[:, D_BANKS[2 + h], 0:w]).then_inc(dve_emptied, 1)

            def residual(strm):
                n = panel_no[0]
                panel_no[0] += 1
                dve.wait_ge(unit_done, panel_end[n])
                e = gate_no[0]
                gate_no[0] += 1
                if GATES[e][0] == 2 and GATES[e][2] == 0:
                    dve.wait_ge(sem("pool_gate"), 2 * (GATES[e][1] + 1))
                else:
                    dve.wait_ge(gate_copied, 2 * sum(1 for g in GATES[:e + 1] if not (g[0] == 2 and g[2] == 0)))
                tmp = xn
                if norm_no[0] > 0:
                    dve.wait_ge(sem("hT_ready"), norm_no[0])
                for q in range(4):
                    t, h = q // 2, q % 2
                    nc.vector.tensor_tensor(tmp[:, t, 512 * h:512 * h + 512], ps[:, D_BANKS[q], :], gate_b[:, 512 * h:512 * h + 512], ALU.mult).then_inc(dve_emptied, 1)
                dve.wait_ge(dve_emptied, dve_count[n + 1])
                for t in range(TT):
                    nc.vector.tensor_tensor(res[:, strm, t, :], res[:, strm, t, :], tmp[:, t, :], ALU.add).then_inc(sem("res_ready"), 1)
                dve.wait_ge(sem("res_ready"), 2 * gate_no[0])

            def rsqrt(n, ins):
                pows[0] += 1
                ins.then_inc(pow_asked, 1)
                dve.wait_ge(pow_done, pows[0])

            def norm():
                n = norm_no[0]
                norm_no[0] += 1
                strm, l, f = NORMS[n] if n < len(NORMS) else (0, 0, 0)
                dve.wait_ge(sem("squares"), 2 * (n + 1))
                rsqrt(2, nc.vector.tensor_scalar(stat[:, 0:2], sums[:, n % 2, :], 1.0 / D, EPS, ALU.mult, ALU.add))
                for t in range(TT):
                    ins = nc.vector.tensor_scalar(xn[:, t, :], res[:, strm, t, :], rstat[:, t:t + 1], None, ALU.mult)
                    ins.then_inc(sem("xn_ready"), 1)
                if n >= len(NORMS):
                    return
                for b in range(2, 4):
                    dve.wait_ge(sem("xT_psum"), 4 * n + b + 1)
                    for k in (2 * b, 2 * b + 1):
                        src = ps[:, b, (k % 2) * S:(k % 2 + 1) * S]
                        c_ = (0 if f == 0 else 24) + k
                        if n in (4, 6):
                            ins = nc.vector.tensor_scalar(full[:, k, :], src, modA[:, l, strm, f, k:k + 1], None, ALU.mult)
                        else:
                            ins = nc.vector.tensor_scalar(full[:, k, :], src, modA[:, l, strm, f, k:k + 1], modT[:, l, strm, c_:c_ + 1], ALU.mult, ALU.add)
                link(ins)
                link(nc.vector.tensor_copy(hT_hi[:, 4:8, :], full[:, 4:8, :]))
                nc.vector.tensor_tensor(hT_lo[:, 4:8, :], full[:, 4:8, :], hT_hi[:, 4:8, :].bitcast(F32), ALU.subtract)
                dve.wait_ge(sem("hT_hi_act"), n + 1)
                nc.vector.tensor_tensor(hT_lo[:, 0:4, :], full[:, 0:4, :], hT_hi[:, 0:4, :].bitcast(F32), ALU.subtract).then_inc(sem("hT_ready"), 1)

            def head_norm(views, width, sq, gain_aps):
                a, b = views[0].shape[1], views[0].shape[2]
                nh = a * b
                for t, v in enumerate(views):
                    s4 = sq[t].rearrange("p (a b d) -> p a b d", a=a, b=b)
                    ins = nc.vector.tensor_tensor(s4, v, v, ALU.mult)
                link(ins)
                for t, v in enumerate(views):
                    ins = nc.vector.tensor_reduce(stat[:, t * nh:(t + 1) * nh], sq[t].rearrange("p (h d) -> p h d", h=nh), AX, ALU.add)
                link(ins)
                n = len(views) * nh
                rsqrt(n, nc.vector.tensor_scalar(stat[:, 0:n], stat[:, 0:n], 1.0 / width, EPS, ALU.mult, ALU.add))
                for t, v in enumerate(views):
                    r = rstat[:, t * nh:(t + 1) * nh].rearrange("p (a b c) -> p a b c", a=a, b=b).to_broadcast([P, a, b, width])
                    ins = nc.vector.tensor_tensor(v, v, r, ALU.mult)
                link(ins)
                for t, v in enumerate(views):
                    ins = nc.vector.tensor_tensor(v, v, gain_aps.to_broadcast([P, a, b, width]), ALU.mult)
                link(ins)

            def rotate(views, cos, sin, tmp, half):
                for v, c_, s_, z in zip(views, cos, sin, tmp):
                    a, b = v.shape[1], v.shape[2]
                    x1, x2 = v[:, :, :, 0:half], v[:, :, :, half:2 * half]
                    cb, sb_ = c_.to_broadcast([P, a, b, half]), s_.to_broadcast([P, a, b, half])
                    zz = [z[:, n * a * b * half:(n + 1) * a * b * half].rearrange("p (a b d) -> p a b d", a=a, b=b) for n in range(4)]
                    nc.vector.tensor_tensor(zz[0], x1, cb, ALU.mult)
                    nc.vector.tensor_tensor(zz[1], x2, sb_, ALU.mult)
                    nc.vector.tensor_tensor(zz[2], x2, cb, ALU.mult)
                    link(nc.vector.tensor_tensor(zz[3], x1, sb_, ALU.mult))
                    nc.vector.tensor_tensor(x1, zz[0], zz[1], ALU.subtract)
                    ins = nc.vector.tensor_tensor(x2, zz[2], zz[3], ALU.add)
                link(ins)

            def turns(stage):
                for g, (_, dst) in enumerate(q_groups(stage)):
                    if g % 2 == 1:
                        dve.wait_ge(sem(f"turned{stage}"), g + 1)
                        d = dst if len(dst.shape) == 2 else dst.rearrange("p a b -> p (a b)")
                        nc.vector.tensor_copy(d, ps[:, g % 4, :]).then_inc(sem(f"turn_dve{stage}"), 1)

            def attention(stage):
                a = ATT[stage]

                def maxima(i):
                    dve.wait_ge(a.scores, i + 1)
                    b = 2 * (i % 2)
                    if i >= 2:
                        dve.wait_ge(a.exps, i - 1)
                    if stage == 3:
                        link(nc.vector.tensor_reduce(rowmax[:, i % 2, 0:2], ps[:, b:b + 2, :], AX, ALU.max))
                        nc.vector.tensor_scalar(rowmax[:, i % 2, 0:2], rowmax[:, i % 2, 0:2], -a.scale, None, ALU.mult).then_inc(a.negmax, 1)
                    else:
                        mx = rowmax[:, i % 2, :].rearrange("p (m r) -> p m r", r=2)
                        nc.vector.tensor_reduce(mx[:, :, 0], ps[:, b:b + 2, 0:128], AX, ALU.max)
                        link(nc.vector.tensor_reduce(mx[:, :, 1], ps[:, b:b + 2, 128:384], AX, ALU.max))
                        nc.vector.tensor_scalar(rowmax[:, i % 2, :], rowmax[:, i % 2, :], -a.scale, None, ALU.mult).then_inc(a.negmax, 1)

                def mix(i):
                    dve.wait_ge(a.exps, i + 1)
                    if i >= 2:
                        dve.wait_ge(a.turned, i - 1)
                    cf = coef[:, i % 2, :]
                    link(nc.vector.reciprocal(cf, rowsum[:, 4 * i:4 * i + 4]))
                    link(nc.vector.tensor_scalar(cf[:, 2:4], cf[:, 2:4], lam_s[:, 4:5], None, ALU.mult))
                    for lo, hi, r in ((0, 128, 0), (128, 384, 1)):
                        ins = nc.vector.tensor_scalar(a.mix[:, i % 2, 0, lo:hi], a.p[:, i % 2, 1, lo:hi], cf[:, 2 + r:3 + r], None, ALU.mult)
                    link(ins)
                    for lo, hi, r in ((0, 128, 0), (128, 384, 1)):
                        ins = nc.vector.scalar_tensor_tensor(out=a.mix[:, i % 2, 0, lo:hi], in0=a.p[:, i % 2, 0, lo:hi], scalar=cf[:, r:r + 1],
                                                             in1=a.mix[:, i % 2, 0, lo:hi], op0=ALU.mult, op1=ALU.subtract)
                    ins.then_inc(a.mixed, 1)

                def take(i):
                    dve.wait_ge(a.pv, i + 1)
                    if stage == 0:
                        cf = coef[:, i % 2, :]
                        link(nc.vector.reciprocal(cf, rowsum[:, 4 * i:4 * i + 4]))
                        h = (2 * i) % 8
                        o = ps[:, 6, 0:256].rearrange("p (m t d) -> p m t d", m=2, t=TT)
                        cols = (0 if i < 4 else 512) + h * HD
                        dst = r0[:, :, cols:cols + 2 * HD].rearrange("p t (m d) -> p m t d", m=2)
                        cf3 = cf.rearrange("p (m t c) -> p m t c", m=2, t=TT)
                        if i < 4:
                            for m in range(2):
                                ins = nc.vector.tensor_tensor(dst[:, m], o[:, m], cf3[:, m].to_broadcast([P, TT, HD]), ALU.mult)
                            ins.then_inc(a.taken, 1)
                            return
                        y = 1 if i < 8 else 2
                        gs = gsig[:, :, 8 * y + h:8 * y + h + 2].rearrange("p t m -> p m t")
                        link(nc.vector.tensor_tensor(cf.rearrange("p (m t) -> p m t", m=2), cf.rearrange("p (m t) -> p m t", m=2), gs, ALU.mult))
                        tmp = hbuf[:, 0, 0:256].rearrange("p (m t d) -> p m t d", m=2, t=TT)
                        for m in range(2):
                            ins = nc.vector.tensor_tensor(tmp[:, m], o[:, m], cf3[:, m].to_broadcast([P, TT, HD]), ALU.mult)
                        link(ins)
                        for m in range(2):
                            ins = nc.vector.tensor_tensor(dst[:, m], dst[:, m], tmp[:, m], ALU.add)
                        ins.then_inc(a.taken, 1)
                        dve.wait_ge(a.taken, i + 1)
                    elif stage == 1:
                        nc.vector.tensor_copy(r1[:, :, i * P:(i + 1) * P], ps[:, 6, 0:256].rearrange("p (t d) -> p t d", t=TT)).then_inc(a.taken, 1)
                    else:
                        cf = coef[:, i % 2, 0:2]
                        link(nc.vector.reciprocal(cf, rowsum[:, 2 * i:2 * i + 2]))
                        nc.vector.tensor_tensor(q3[:, :, i * P:(i + 1) * P], ps[:, 6, 0:256].rearrange("p (t d) -> p t d", t=TT),
                                                cf.rearrange("p (t c) -> p t c", c=1).to_broadcast([P, TT, P]), ALU.mult).then_inc(a.taken, 1)

                for i in range(a.steps + 2):
                    if i < a.steps:
                        maxima(i)
                    if stage == 1 and 1 <= i <= a.steps:
                        mix(i - 1)
                    if i >= 2:
                        take(i - 2)
                    ada_step()
                dve.wait_ge(a.taken, a.steps)

            def out_turn(stage):
                for b in range(4):
                    dve.wait_ge(sem(f"out_hi{stage}"), b + 1)
                    nc.vector.tensor_tensor(hT_lo[:, 2 * b:2 * b + 2, :], ps[:, b, :].rearrange("p (k n) -> p k n", k=2),
                                            hT_hi[:, 2 * b:2 * b + 2, :].bitcast(F32), ALU.subtract).then_inc(sem(f"out_lo{stage}"), 1)

            nc.vector.memset(params[:, :], 0.0).then_inc(sem("params_zero"), 1)
            nc.vector.memset(zero16[:, :], 0.0).then_inc(hid_done, 2)
            nc.vector.memset(mark[:, :], 0.0).then_inc(hact_done, 2)
            nc.vector.memset(cpad[:, :, :, :], 0.0)
            link(nc.vector.memset(stat[:, :], 1.0))
            nc.vector.memset(lam_s[:, :], 0.0).then_inc(sem("zeros_set"), 1)
            dve.wait_ge(sem("small_params"), 128)
            nc.vector.tensor_copy(ident_r[:, :], ident)
            nc.vector.tensor_copy(causal_r[:, :], const("causal")).then_inc(sem("cst_r"), 1)
            dve.wait_ge(sem("param_psum"), 1)
            nc.vector.tensor_copy(paramT[:, :], ps[:, 0, 0:P]).then_inc(sem("paramT_ready"), 1)
            dve.wait_ge(sem("x_landed"), 32)
            link(nc.vector.tensor_copy(pos_f[:, :], pos_i[:, :]))
            ang = trig_t[:, 0, :, :]
            rev = trig[:, :, :, :]
            link(nc.vector.tensor_tensor(ang, pos_f[:, :].rearrange("p (t c) -> p t c", c=1).to_broadcast([P, TT, 8]),
                                         const("inv_freq").rearrange("p (c n) -> p c n", c=1).to_broadcast([P, TT, 8]), ALU.mult))
            MAGIC = 12582912.0
            link(nc.vector.tensor_scalar(rev[:, 0], ang, 1.0 / TWO_PI, 0.25, ALU.mult, ALU.add))
            link(nc.vector.tensor_scalar(rev[:, 1], ang, 1.0 / TWO_PI, None, ALU.mult))
            link(nc.vector.tensor_scalar(rev, rev, MAGIC, None, ALU.add))
            link(nc.vector.tensor_scalar(rev, rev, -MAGIC, None, ALU.add))
            link(nc.vector.tensor_copy(trig_t[:, 1, :, :], ang))
            c1 = 6.28125
            c2 = round((TWO_PI - c1) * 2 ** 20) / 2 ** 20
            c3 = TWO_PI - c1 - c2
            for part in (c1, c2, c3):
                link(nc.vector.scalar_tensor_tensor(out=trig_t[:, :, :, :], in0=rev, scalar=-part, in1=trig_t[:, :, :, :], op0=ALU.mult, op1=ALU.add))
            link(nc.vector.tensor_scalar(trig_t[:, 0, :, :], trig_t[:, 0, :, :], TWO_PI / 4, None, ALU.add))
            link(nc.vector.tensor_scalar(trig_t[:, :, :, :], trig_t[:, :, :, :], 3.141592, -3.141592, ALU.min, ALU.max))
            nc.vector.memset(mark[:, 2:3], 0.0).then_inc(sem("angles"), 1)

            split_unit(0)
            split_unit(1)
            ada_step(9)
            norm()
            cosv = [trig[:, 0, t:t + 1, :].rearrange("p a (b d) -> p a b d", b=1) for t in range(TT)]
            sinv = [trig[:, 1, t:t + 1, :].rearrange("p a (b d) -> p a b d", b=1) for t in range(TT)]
            sq0 = [wk(7728 + 1024 * t, 1024) for t in range(TT)]
            rot0 = [wk(9776 + 512 * t, 512) for t in range(TT)]
            for n, w in enumerate((1024, 1024, 792)):
                row_segment(f"in0_{n}")
                panel_rows(r0, 1024 * n, w)
                held_split(f"in0_{n}")
                if n == 0:
                    dve.wait_ge(sem("gains_landed"), 16 * 18)
                    dve.wait_ge(sem("trig_ready"), 1)
                dve.wait_ge(dve_emptied, 2 * n + 2)
                dve.wait_ge(act_emptied, 2 * n + 2)
                if n == 0:
                    views = [r0[:, t, 0:1024].rearrange("p (a b d) -> p a b d", a=2, b=8) for t in range(TT)]
                    g = gains[:, 0:2, :].rearrange("p a (c d) -> p a c d", c=1)
                elif n == 1:
                    views = [r0[:, t, 1536:2048].rearrange("p (a b d) -> p a b d", a=1, b=8) for t in range(TT)]
                    g = gains[:, 2:3, :].rearrange("p a (c d) -> p a c d", c=1)
                else:
                    views = [r0[:, t, 2048:2816].rearrange("p (a z b d) -> p a z b d", a=3, z=2, b=2)[:, :, 0] for t in range(TT)]
                    g = gains[:, 3:6, :].rearrange("p a (c d) -> p a c d", c=1)
                nh = 16 if n == 0 else 8 if n == 1 else 6
                head_norm(views, HD, [q[:, 0:nh * HD] for q in sq0], g)
                rotate([v[:, :, :, 0:16] for v in views], cosv, sinv, rot0, 8)
            nc.vector.memset(mark[:, 1:2], 0.0).then_inc(sem("heads0"), 1)
            dve.wait_ge(sem("gsig_exp"), 1)
            link(nc.vector.tensor_scalar(gsig[:, :, :], gsig[:, :, :], 1.0, None, ALU.add))
            link(nc.vector.reciprocal(gsig[:, :, :], gsig[:, :, :]))
            nc.vector.memset(hidr[:, :], 0.0).then_inc(sem("hidr_zero"), 1)
            turns(0)
            dve.wait_ge(sem("turn_act0"), 5)
            dve.wait_ge(sem("turn_dve0"), 5)
            blk = wk(12848, 1024).rearrange("p (s k n) -> p s k n", s=2, k=16)
            posT = paramT[:, 64:96].rearrange("p (s k c) -> p s k c", s=2, c=1)
            for s_ in range(2):
                for half in range(2):
                    lo, hi = 64 * half, 64 * half + 64
                    for g in range(2):
                        src = qt0[lo:hi, 16 + 2 * s_ + g, :].rearrange("p (n k a) -> p k n a", k=8, a=2)
                        for kh in range(2):
                            s_ap = src[:, :, kh:kh + NCMP, half]
                            dst = blk[lo:hi, s_, 8 * kh:8 * kh + 8, g * NCMP:(g + 1) * NCMP]
                            ins = nc.vector.tensor_tensor(dst, s_ap, posT[lo:hi, s_, 8 * kh:8 * kh + 8, :].to_broadcast([64, 8, NCMP]), ALU.add)
            ins.then_inc(sem("cmp_blocks"), 1)
            hidT = hbuf[:, 0, 0:128].rearrange("p (k n) -> p k n", k=2)
            vbd = hbuf[:, 1, :]
            dve.wait_ge(sem("cmp_hidT"), 1)
            nc.vector.tensor_copy(hidT, ps[:, 1, 0:128].rearrange("p (k n) -> p k n", k=2)).then_inc(sem("cmp_hidT_sb"), 1)
            dve.wait_ge(sem("cmp_kv"), 1)
            nc.vector.tensor_copy(kcs[:, 0:30], ps[:, 2, 0:30])
            nc.vector.tensor_copy(vcr[0:NCMP, :], ps[0:NCMP, 2, 64:192]).then_inc(sem("cmp_kv_sb"), 1)
            dve.wait_ge(sem("cmp_vrep"), 1)
            nc.vector.tensor_tensor(vbd, ps[:, 3, :], const("headmask"), ALU.mult).then_inc(sem("cmp_vbd"), 1)
            link(nc.vector.memset(cmp_s, NEG))
            dve.wait_ge(sem("cmp_scores"), 1)
            neg = const("cmp_neg").rearrange("p (t c n) -> p t c n", t=TT, c=1)
            okm = const("cmp_ok").rearrange("p (t c n) -> p t c n", t=TT, c=1)
            for t in range(TT):
                for m in range(2):
                    ins = nc.vector.tensor_tensor(cmp_s[:, t, m:8:2, 0:NCMP], ps[:, t + 2 * m, 0:64].rearrange("p (h n) -> p h n", h=4)[:, :, 0:NCMP],
                                                  neg[:, t, :, 0:NCMP].to_broadcast([P, 4, NCMP]), ALU.add)
            link(ins)
            flat = cmp_s.rearrange("p t h n -> p (t h) n")
            link(nc.vector.tensor_reduce(cmp_m[:, :], flat, AX, ALU.max))
            nc.vector.tensor_tensor(flat, flat, cmp_m[:, :].rearrange("p (h c) -> p h c", c=1).to_broadcast([P, 16, 16]), ALU.subtract).then_inc(sem("cmp_shift"), 1)
            dve.wait_ge(sem("cmp_exp"), 1)
            for t in range(TT):
                ins = nc.vector.tensor_tensor(cmp_s[:, t], cmp_s[:, t], okm[:, t].to_broadcast([P, 8, 16]), ALU.mult)
            link(ins)
            link(nc.vector.tensor_reduce(cmp_m[:, :], flat, AX, ALU.add))
            link(nc.vector.tensor_scalar(cmp_m[:, :], cmp_m[:, :], 0.5, None, ALU.max))
            link(nc.vector.reciprocal(cmp_m[:, :], cmp_m[:, :]))
            link(nc.vector.tensor_tensor(cmp_m[:, :].rearrange("p (t h) -> p t h", t=TT), cmp_m[:, :].rearrange("p (t h) -> p t h", t=TT),
                                         gsig[:, :, 0:8], ALU.mult))
            nc.vector.tensor_tensor(flat, flat, cmp_m[:, :].rearrange("p (h c) -> p h c", c=1).to_broadcast([P, 16, 16]), ALU.mult).then_inc(sem("cmp_p"), 1)
            dve.wait_ge(sem("cmp_turned"), 1)
            nc.vector.tensor_copy(cmp_T, ps[:, 2, 0:256].rearrange("p (t n) -> p t n", t=TT)).then_inc(sem("cmp_pT"), 1)
            dve.wait_ge(sem("cmp_pv"), 1)
            link(nc.vector.tensor_copy(r0[:, :, 512:1024], ps[:, 0:2, :]))
            nc.vector.memset(mark[:, 1:2], 0.0).then_inc(sem("cmp_taken"), 1)
            attention(0)
            out_turn(0)
            gate_wait = None
            row_segment("out0")
            residual(0)
            norm()
            held_split("out0")
            stream("up0")
            stream("down0", hold_last=True)
            residual(0)
            norm()
            held_split("down0")
            sq1 = [wk(6144 + 2048 * t, 2048) for t in range(TT)]
            rot1 = [wk(10240 + 1024 * t, 1024) for t in range(TT)]
            for n in range(3):
                row_segment(f"in1_{n}")
                panel_rows(r1, 1024 * n, 1024)
                held_split(f"in1_{n}")
                if n == 2:
                    continue
                dve.wait_ge(dve_emptied, dve_count[6 + n])
                dve.wait_ge(act_emptied, act_count[6 + n])
                views = [r1[:, t, 1024 * n:1024 * n + 1024].rearrange("p (a b d) -> p a b d", a=1, b=16) for t in range(TT)]
                head_norm(views, HD, [q[:, 0:1024] for q in sq1], gains[:, 6 + n:7 + n, :].rearrange("p a (c d) -> p a c d", c=1))
                rotate([v[:, :, :, 0:16] for v in views], cosv, sinv, [z[:, 0:512] for z in rot1], 8)
            lp = lam_p[:, :, :].rearrange("p (a b) d -> p a b d", b=2)
            lt = hbuf[:, 0, 0:128].rearrange("p (a d) -> p a d", a=2)
            link(nc.vector.tensor_tensor(lt, lp[:, :, 0, :], lp[:, :, 1, :], ALU.mult))
            nc.vector.tensor_reduce(lam_s[:, 0:2], lt, AX, ALU.add).then_inc(sem("lam_sum"), 1)
            dve.wait_ge(sem("lam_exp"), 1)
            link(nc.vector.tensor_tensor(lam_s[:, 4:5], lam_s[:, 2:3], lam_s[:, 3:4], ALU.subtract))
            link(nc.vector.tensor_scalar(lam_s[:, 4:5], lam_s[:, 4:5], LAM_INIT, None, ALU.add))
            link(nc.vector.tensor_scalar(gain_o[:, :], gain_o[:, :], 1.0 - LAM_INIT, None, ALU.mult))
            nc.vector.memset(mark[:, 1:2], 0.0).then_inc(sem("heads1"), 1)
            turns(1)
            attention(1)
            head_norm([r1[:, t, 0:1024].rearrange("p (a b d) -> p a b d", a=1, b=8) for t in range(TT)], HD2, [q[:, 0:1024] for q in sq1],
                      gain_o[:, :].rearrange("p (a c d) -> p a c d", a=1, c=1))
            nc.vector.memset(mark[:, 1:2], 0.0).then_inc(sem("rows1"), 1)
            out_turn(1)
            row_segment("out1")
            residual(0)
            norm()
            held_split("out1")
            stream("up1")
            stream("down1", hold_last=True)
            residual(0)
            ada_step(max(0, 9 * 9 - step_no[0]))
            for s_ in range(2):
                norm()
                held_split("down1" if s_ == 0 else "down20")
                dve.wait_ge(sem("pool_landed"), 32 * (s_ + 1))
                for h in range(2):
                    dve.wait_ge(gate_psum, 2 * (4 + 2 * s_) + h + 1)
                    nc.vector.tensor_tensor(gate_b[:, 512 * h:512 * h + 512], ps[:, D_BANKS[h], :], wk(2048 + 512 * h, 512), ALU.mult).then_inc(sem("pool_gate"), 1)
                split_unit(by_name[f"pool{s_}"]["base"] + 2)
                residual(s_)
                norm()
                stream(f"up2{s_}")
                stream(f"down2{s_}", hold_last=True)
                residual(s_)
            ada_step(max(0, 9 * 12 - step_no[0]))
            norm()
            held_split("down21")
            row_segment("kvc", ada=False)
            panel_rows(kvc, 0, 1024)
            norm()
            held_split("kvc")
            acos = [const("ax_cos").rearrange("p (t a b d) -> p t a b d", t=TT, a=1, b=2)[:, t] for t in range(TT)]
            asin = [const("ax_sin").rearrange("p (t a b d) -> p t a b d", t=TT, a=1, b=2)[:, t] for t in range(TT)]
            sq3 = [wk(6144 + 1024 * t, 1024) for t in range(TT)]
            rot3 = [wk(8192 + 2048 * t, 2048) for t in range(TT)]
            for n, (name, rows, gn, nh) in enumerate((("kvc", kvc, 1, 4), ("kvl", kvl, 1, 4), ("q3", q3, 0, 8))):
                if n > 0:
                    row_segment(name, ada=False)
                    panel_rows(rows, 0, 1024)
                    held_split(name)
                dve.wait_ge(dve_emptied, dve_count[15 + n])
                dve.wait_ge(act_emptied, act_count[15 + n])
                views = [rows[:, t, 0:nh * P].rearrange("p (a b d) -> p a b d", a=1, b=nh) for t in range(TT)]
                head_norm(views, HD2, [q[:, 0:nh * P] for q in sq3], gains2[:, gn:gn + 1, :].rearrange("p a (c d) -> p a c d", c=1))
                if n > 0:
                    rv = [rows[:, t, 0:nh * P].rearrange("p (a b d) -> p a b d", a=nh, b=2) for t in range(TT)]
                    rotate(rv, acos, asin, [z[:, 0:nh * 256] for z in rot3], 32)
            nc.vector.memset(mark[:, 1:2], 0.0).then_inc(sem("heads3"), 1)
            turns(3)
            attention(3)
            out_turn(3)
            row_segment("out3", ada=False)
            residual(0)
            norm()
            held_split("out3")
            stream("up3")
            stream("down3")
            residual(0)
            norm()
            dve.wait_ge(sem("xn_ready"), 2 * (len(NORMS) + 1))
            dve.wait_ge(sem("final_landed"), 16)
            for t in range(TT):
                nc.vector.tensor_tensor(xn[:, t, :], xn[:, t, :], wk(0, D), ALU.mult).then_inc(sem("out_ready"), 1)

        @block.tensor
        def _(pe):
            mm = nc.tensor.matmul
            step_no = [0]
            panel_no = [0]
            norm_no = [0]
            gate_no = [0]
            bank7 = [None]
            gate_out = [None]

            def bank7_wait():
                if bank7[0] is not None:
                    pe.wait_ge(*bank7[0])

            def ada_step(n=1):
                for _ in range(n):
                    a, k = step_no[0] // 9, step_no[0] % 9
                    step_no[0] += 1
                    if a >= PANELS:
                        continue
                    b = 0 if a < 6 else 1
                    if k < 8:
                        if k == 0:
                            bank7_wait()
                        r = ring_at[("ada", a, k)]
                        ring_wait(pe, r)
                        for j in range(4):
                            ins = mm(ps[32 * j:32 * j + 32, ADA_BANK, :], cpad[:, b, k, :], ring[:, r % 2, 512 * j:512 * j + 512],
                                     start=(k == 0), stop=False)
                        ins.then_inc(ring_used, 1)
                        if k == 7:
                            r = ring_at[("bias", a, 0)]
                            ring_wait(pe, r)
                            for j in range(4):
                                ins = mm(ps[32 * j:32 * j + 32, ADA_BANK, :], const("sel0")[0:1, 0:32], ring[0:1, r % 2, 512 * j:512 * j + 512],
                                         start=False, stop=True)
                            ins.then_inc(ring_used, 1)
                    else:
                        p = a % 3
                        pe.wait_ge(ada_rows, a + 1)
                        for q in range(4):
                            ins = nc.tensor.transpose(ps[:, ADA_BANK, q * P:(q + 1) * P], modrow[:, p, q * P:(q + 1) * P], ident)
                        ins.then_inc(ada_turn, 1)
                        bank7[0] = (ada_cols, a + 1)

            def unit_wait(u, k4=None):
                pe.wait_ge(hi_ready, u + 1 if k4 is None else k4 * 4 + (u + 1))
                pe.wait_ge(lo_ready, u + 1 if k4 is None else k4 * 4 + (u + 1))

            def three(dst, s_hi, s_lo, m_hi, m_lo, start, stop, skip=False):
                mm(dst, s_hi, m_hi, start=start, stop=False, skip_group_check=skip)
                mm(dst, s_hi, m_lo, start=False, stop=False, skip_group_check=skip)
                return mm(dst, s_lo, m_hi, start=False, stop=stop, skip_group_check=skip)

            def emptied(n, t):
                if n == 0:
                    return
                if gate_out[0] is not None:
                    pe.wait_ge(*gate_out[0])
                if t == 0:
                    if act_count[n]:
                        pe.wait_ge(act_emptied, act_count[n])
                    if PANEL_KIND[n - 1] == "res":
                        pe.wait_ge(dve_emptied, dve_count[n])
                elif dve_count[n]:
                    pe.wait_ge(dve_emptied, dve_count[n])

            def row_segment(name, ada=True):
                s_ = by_name[name]
                n = panel_no[0]
                panel_no[0] += 1
                w = s_["width"]
                for i in range(4):
                    u = s_["base"] + i
                    if ada:
                        ada_step()
                    unit_wait(u)
                    for t in range(TT):
                        if i == 0:
                            emptied(n, t)
                        for kk in range(2):
                            k = 2 * i + kk
                            for h in range(2):
                                wd = min(512, w - 512 * h)
                                c0 = kk * w + 512 * h
                                ins = three(ps[:, D_BANKS[2 * t + h], 0:wd], hT_hi[:, k, t * P:(t + 1) * P], hT_lo[:, k, t * P:(t + 1) * P],
                                            whi[:, u % 2, c0:c0 + wd], wlo[:, u % 2, c0:c0 + wd], k == 0, k == KT - 1)
                    ins.then_inc(unit_done, 1)

            def hidden_unit(s_, i, k4=None):
                u = s_["base"] + i
                hb = hid_base[s_["name"][2:]]
                unit_wait(u, k4)
                if s_["kind"] == "pair":
                    which, v, per = (hact_done if i % 2 == 0 else hid_done), hb + i // 2 - 1, 2
                else:
                    which, v, per = hact_done, hb + i - 3, 4
                pe.wait_ge(which, v if k4 is None else k4 * per + v)
                for f in range(2):
                    for k in range(KT):
                        c0 = k * 256 + f * P
                        ins = three(ps[:, i % 4, f * S:(f + 1) * S], whi[:, u % 2, c0:c0 + P], wlo[:, u % 2, c0:c0 + P], hT_hi[:, k, :], hT_lo[:, k, :],
                                    k == 0, k == KT - 1)
                ins.then_inc(unit_done, 1)

            def up_segment(name):
                s_ = by_name[name]
                n = bodies(s_)
                with pe.Fori(0, n) as k4:
                    for j in range(4):
                        hidden_unit(s_, j, k4)
                for i in range(4 * n, s_["count"]):
                    hidden_unit(s_, i)

            def down_segment(name):
                s_ = by_name[name]
                n0 = panel_no[0]
                panel_no[0] += 1
                for t in range(TT):
                    emptied(n0, t)
                tag = s_["name"][4:]
                hb = hid_base[tag] + by_name["up" + tag]["count"] // (2 if by_name["up" + tag]["kind"] == "pair" else 1)
                pe.wait_ge(hact_done, hb)
                for q in range(4):
                    mm(ps[:, D_BANKS[q], :], zero16[0:1, 0:P], zero16[0:1, :], start=True, stop=False, skip_group_check=True)

                def unit(i, k4=None):
                    u = s_["base"] + i
                    unit_wait(u, k4)
                    for t in range(TT):
                        for kk in range(2):
                            for h in range(2):
                                c0 = kk * 1024 + 512 * h
                                a0 = kk * S + t * P
                                ins = three(ps[:, D_BANKS[2 * t + h], :], act_hi[:, u % 2, a0:a0 + P], act_lo[:, u % 2, a0:a0 + P],
                                            whi[:, u % 2, c0:c0 + 512], wlo[:, u % 2, c0:c0 + 512], False, False, True)
                    ins.then_inc(unit_done, 1)

                n = bodies(s_)
                with pe.Fori(0, n) as k4:
                    for j in range(4):
                        unit(j, k4)
                for i in range(4 * n, s_["count"]):
                    unit(i)

            def norm():
                n = norm_no[0]
                norm_no[0] += 1
                if n in (4, 6):
                    pe.wait_ge(sem("pool_landed"), 32 * (1 if n == 4 else 2))
                    pe.wait_ge(sem("xn_ready"), 2 * n + 2)
                mats = wk(0, 2048).rearrange("p (g j n) -> p g j n", g=4, j=TT)
                for b in range(4):
                    for t in range(TT):
                        if b == 0:
                            pe.wait_ge(sem("xn_ready"), 2 * n + t + 1)
                        for k in (2 * b, 2 * b + 1):
                            if n in (4, 6):
                                continue
                            ins = nc.tensor.transpose(ps[:, b, (k % 2) * S + t * P:(k % 2) * S + (t + 1) * P], xn[:, t, k * P:(k + 1) * P], ident)
                    if n in (4, 6):
                        for k in (2 * b, 2 * b + 1):
                            for t in range(TT):
                                ins = mm(ps[:, b, (k % 2) * S:(k % 2 + 1) * S], xn[:, t, k * P:(k + 1) * P], mats[:, b, t, :],
                                         start=(t == 0), stop=(t == TT - 1))
                    ins.then_inc(sem("xT_psum"), 1)

            def gate():
                l, strm, f = GATES[gate_no[0]]
                e = gate_no[0]
                gate_no[0] += 1
                pooled = l == 2 and f == 0
                p = 1 if f == 0 else 2
                n = panel_no[0]
                for t in range(TT):
                    emptied(n, t)
                for h in range(2):
                    j = h if f == 0 else 2 + h
                    sl = const("sel1" if strm else "sel0")
                    mm(ps[:, D_BANKS[h], :], sl[32 * j:32 * j + 32, :], modrow[32 * j:32 * j + 32, p, :], start=True, stop=True).then_inc(gate_psum, 1)
                if pooled:
                    gate_out[0] = (sem("pool_gate"), 2 * strm + 2)
                else:
                    gate_out[0] = (gate_copied, 2 * sum(1 for g in GATES[:e + 1] if not (g[0] == 2 and g[2] == 0)))

            def turns(stage):
                for g, (srcs, _) in enumerate(q_groups(stage)):
                    if g >= 4:
                        which = "turn_act" if g % 2 == 0 else "turn_dve"
                        pe.wait_ge(sem(f"{which}{stage}"), (g - 4) // 2 + 1)
                    for n, src in enumerate(srcs):
                        ins = nc.tensor.transpose(ps[:, g % 4, n * P:(n + 1) * P], src, ident)
                    ins.then_inc(sem(f"turned{stage}"), 1)
                n = len(q_groups(stage))
                pe.wait_ge(sem(f"turn_act{stage}"), n // 2)
                pe.wait_ge(sem(f"turn_dve{stage}"), n // 2)

            def attention(stage):
                a = ATT[stage]

                def operands(i, m):
                    if stage == 0:
                        h = (2 * i) % 8 + m
                        lo, hi = 64 * m, 64 * m + 64
                        if i < 4:
                            q, k, v = qt0[lo:hi, i, :], qt0[lo:hi, 4 + i, :], 1024 + h * HD
                        else:
                            y = (i - 4) // 4
                            q, k, v = qt0[lo:hi, 8 + i % 4, :], qt0[lo:hi, 12 + 2 * y + h // 4, :], (2432 if y == 0 else 2688) + (h // 4) * HD
                        return q, k, [r0[:, t, v:v + HD] for t in range(TT)]
                    lo, hi = 64 * m, 64 * m + 64
                    return qt1[lo:hi, i, :], qt1[lo:hi, 8 + i, :], [r1[:, t, 2048 + i * P:2048 + (i + 1) * P] for t in range(TT)]

                def scores(i):
                    if i >= 2:
                        pe.wait_ge(a.exps, i - 1)
                    for m in range(2):
                        bank = 2 * (i % 2) + m
                        if stage == 3:
                            ins = mm(ps[:, bank, :], qt3[:, i, m * P:(m + 1) * P], kt3[:, i // 2, :], start=True, stop=True)
                            continue
                        q, k, _ = operands(i, m)
                        mm(ps[:, bank, 0:256], ident_r[:, :], causal_r[:, :], start=True, stop=False, skip_group_check=True)
                        mm(ps[:, bank, 0:128], q[:, 0:128], k[:, 0:128], start=False, stop=True, skip_group_check=True)
                        mm(ps[:, bank, 128:256], q[:, 128:256], k[:, 128:256], start=False, stop=True, skip_group_check=True)
                        ins = mm(ps[:, bank, 256:384], q[:, 128:256], k[:, 0:128], start=False, stop=True, skip_group_check=True)
                    ins.then_inc(a.scores, 1)

                def turn(i):
                    pe.wait_ge(a.mixed if stage == 1 else a.exps, i + 1)
                    if stage == 1:
                        if i >= 2:
                            pe.wait_ge(a.pT, i - 1)
                        maps = [(4 + i % 2, a.mix[:, i % 2, 0, :])]
                    else:
                        if i >= 1:
                            pe.wait_ge(a.pT, i)
                        maps = [(4 + m, a.p[:, i % 2, m, :]) for m in range(2)]
                    for bank, src in maps:
                        for b in range(a.width // P):
                            ins = nc.tensor.transpose(ps[:, bank, b * P:(b + 1) * P], src[:, b * P:(b + 1) * P], ident)
                    ins.then_inc(a.turned, 1)

                def values(i):
                    pe.wait_ge(a.pT, i + 1)
                    if i >= 1:
                        pe.wait_ge(a.taken, i)
                    if stage == 3:
                        vcol = 512 + (i // 2) * P
                        v = [kvc[:, 0, vcol:vcol + P], kvc[:, 1, vcol:vcol + P], kvl[:, 0, vcol:vcol + P], kvl[:, 1, vcol:vcol + P]]
                        for m in range(2):
                            for b in range(4):
                                ins = mm(ps[:, 6, m * P:(m + 1) * P], a.pt[:, i % 2, m, b * P:(b + 1) * P], v[b], start=(b == 0), stop=(b == 3))
                    else:
                        for m in range(a.maps):
                            _, _, v = operands(i, m)
                            w = HD if stage == 0 else HD2
                            pt = a.pt[:, i % 2, m, :]
                            o = ps[:, 6, m * 2 * w:(m + 1) * 2 * w]
                            mm(o[:, 0:w], pt[:, 0:128], v[0], start=True, stop=True)
                            mm(o[:, w:2 * w], pt[:, 128:256], v[1], start=True, stop=False)
                            ins = mm(o[:, w:2 * w], pt[:, 256:384], v[0], start=False, stop=True)
                    ins.then_inc(a.pv, 1)

                for i in range(a.steps + 2):
                    if i < a.steps:
                        scores(i)
                    if 1 <= i <= a.steps:
                        turn(i - 1)
                    if i >= 2:
                        values(i - 2)
                    ada_step()
                pe.wait_ge(a.taken, a.steps)

            def out_turn(stage):
                rows = out_rows[stage]
                for b in range(4):
                    for k in (2 * b, 2 * b + 1):
                        for t in range(TT):
                            ins = nc.tensor.transpose(ps[:, b, (k % 2) * S + t * P:(k % 2) * S + (t + 1) * P], rows[:, t, k * P:(k + 1) * P], ident)
                    ins.then_inc(sem(f"out_turned{stage}"), 1)
                gate()
                pe.wait_ge(sem(f"out_lo{stage}"), 4)

            pe.wait_ge(sem("small_params"), 128)
            nc.tensor.transpose(ps[:, 0, 0:P], params[:, :], ident).then_inc(sem("param_psum"), 1)
            pe.wait_ge(sem("zeros_set"), 1)
            pe.wait_ge(sem("silu_c"), 1)
            pe.wait_ge(sem("cst_r"), 1)
            ada_step(9)
            norm()
            pe.wait_ge(sem("hT_ready"), 1)
            for n in range(3):
                row_segment(f"in0_{n}")
            pe.wait_ge(sem("heads0"), 1)
            pe.wait_ge(sem("doubled"), 1)
            turns(0)
            pe.wait_ge(sem("cmp_blocks"), 1)
            blk = wk(12848, 1024).rearrange("p (s k n) -> p s k n", s=2, k=16)
            for s_ in range(2):
                for h in range(2):
                    r = ring_at[("cmp", s_, h)]
                    ring_wait(pe, r)
                    for kk in range(8):
                        k = 8 * h + kk
                        ins = mm(ps[32 * s_:32 * s_ + 30, 0, 0:256], blk[:, s_, k, 0:30], ring[:, r % 2, kk * 256:(kk + 1) * 256],
                                 start=(k == 0), stop=(k == 15))
                    ins.then_inc(ring_used, 1)
            pe.wait_ge(sem("cmp_silu"), 1)
            for e in range(2):
                ins = nc.tensor.transpose(ps[:, 1, 64 * e:64 * e + 64], hidr[:, e * P:(e + 1) * P], ident[0:64, 0:64])
            ins.then_inc(sem("cmp_hidT"), 1)
            pe.wait_ge(sem("cmp_hidT_sb"), 1)
            hidT = hbuf[:, 0, 0:128].rearrange("p (k n) -> p k n", k=2)
            vbd = hbuf[:, 1, :]
            for e in range(2):
                mm(ps[:, 2, 0:30], w2k[:, e, :, :].rearrange("p u d -> p (u d)"), hidT[:, e, 0:30], start=(e == 0), stop=(e == 1))
            for g in range(2):
                for e in range(2):
                    ins = mm(ps[0:NCMP, 2, 64 + 64 * g:128 + 64 * g], hidT[:, e, 32 + g * NCMP:32 + (g + 1) * NCMP], w2v[:, e, :],
                             start=(e == 0), stop=(e == 1))
            ins.then_inc(sem("cmp_kv"), 1)
            pe.wait_ge(sem("cmp_kv_sb"), 1)
            for g in range(2):
                for r_ in range(4):
                    h = 4 * g + r_
                    ins = mm(ps[:, 3, h * HD:(h + 1) * HD], const("spread")[0:NCMP, :], vcr[0:NCMP, g * HD:(g + 1) * HD], start=True, stop=True)
            ins.then_inc(sem("cmp_vrep"), 1)
            pe.wait_ge(sem("cmp_vbd"), 1)
            for t in range(TT):
                for h in range(8):
                    lo = 64 * (h % 2)
                    ins = mm(ps[:, t + 2 * (h % 2), (h // 2) * 16:(h // 2) * 16 + NCMP], qt0[lo:lo + 64, 8 + h // 2, t * P:(t + 1) * P], kcs[lo:lo + 64, (h // 4) * NCMP:(h // 4 + 1) * NCMP],
                             start=True, stop=True)
            ins.then_inc(sem("cmp_scores"), 1)
            pe.wait_ge(sem("cmp_p"), 1)
            pe.wait_ge(sem("cmp_vbd"), 1)
            for t in range(TT):
                ins = nc.tensor.transpose(ps[:, 2, t * P:(t + 1) * P], cmp_s[:, t].rearrange("p h n -> p (h n)"), ident)
            ins.then_inc(sem("cmp_turned"), 1)
            pe.wait_ge(sem("cmp_pT"), 1)
            for t in range(TT):
                ins = mm(ps[:, t, :], cmp_T[:, t, :], vbd, start=True, stop=True)
            ins.then_inc(sem("cmp_pv"), 1)
            pe.wait_ge(sem("cmp_taken"), 1)
            attention(0)
            out_turn(0)
            row_segment("out0")
            norm()
            gate()
            pe.wait_ge(sem("hT_ready"), 2)
            up_segment("up0")
            down_segment("down0")
            norm()
            pe.wait_ge(sem("hT_ready"), 3)
            for n in range(3):
                row_segment(f"in1_{n}")
            pe.wait_ge(sem("heads1"), 1)
            turns(1)
            attention(1)
            pe.wait_ge(sem("rows1"), 1)
            out_turn(1)
            row_segment("out1")
            norm()
            gate()
            pe.wait_ge(sem("hT_ready"), 4)
            up_segment("up1")
            down_segment("down1")
            ada_step(max(0, 9 * 9 - step_no[0]))
            for strm in range(2):
                norm()
                gate()
                pe.wait_ge(sem("hT_ready"), norm_no[0])
                s_ = by_name[f"pool{strm}"]
                u = s_["base"]
                n = panel_no[0]
                panel_no[0] += 1
                unit_wait(u)
                for t in range(TT):
                    emptied(n, t)
                    for g in range(4):
                        for kk in range(2):
                            k = 2 * g + kk
                            ins = three(ps[:, D_BANKS[2 * t + g // 2], (g % 2) * 256:(g % 2 + 1) * 256], hT_hi[:, k, t * P:(t + 1) * P], hT_lo[:, k, t * P:(t + 1) * P],
                                        whi[:, u % 2, k * 256:(k + 1) * 256], wlo[:, u % 2, k * 256:(k + 1) * 256], kk == 0, kk == 1)
                ins.then_inc(unit_done, 1)
                norm()
                gate()
                pe.wait_ge(sem("hT_ready"), norm_no[0])
                up_segment(f"up2{strm}")
                down_segment(f"down2{strm}")
            ada_step(max(0, 9 * 12 - step_no[0]))
            norm()
            pe.wait_ge(sem("hT_ready"), norm_no[0])
            row_segment("kvc", ada=False)
            norm()
            pe.wait_ge(sem("hT_ready"), norm_no[0])
            row_segment("kvl", ada=False)
            row_segment("q3", ada=False)
            pe.wait_ge(sem("heads3"), 1)
            turns(3)
            attention(3)
            out_turn(3)
            row_segment("out3", ada=False)
            norm()
            gate()
            pe.wait_ge(sem("hT_ready"), norm_no[0])
            up_segment("up3")
            down_segment("down3")


_INS = ["x", "c", "positions", "ada_w", "ada_b", "attn_norm", "ffn_norm", "ffn_w_gate", "ffn_w_up", "ffn_w_down", "sp_w_in",
        "sp_w_out", "moba_q_norm", "moba_k_norm", "nsa_q_norm", "nsa_k_norm", "nsa_cmp_pos", "nsa_cmp_w1", "nsa_cmp_w2",
        "diff_w_in", "diff_w_out", "diff_q_norm", "diff_k_norm", "diff_lambda", "diff_out_norm", "c_2", "ctx_2", "c_ctx_2",
        "ada_w_2", "ada_b_2", "norm_g_2", "mlp_w1_2", "mlp_w2_2", "pool_w_2", "pool_scale_2", "attn_w_qkv_2", "attn_w_o_2",
        "attn_q_g_2", "attn_k_g_2", "final_g_2"]


def kernel(**inputs):
    import numpy as _np
    import concourse.bacc as _bacc
    from concourse import mybir as _mybir
    from concourse.bass_utils import run_bass_kernel_spmd as _run

    nc = _bacc.Bacc("TRN2", target_bir_lowering=False, num_devices=1, dynamic_dma_scratch_size=1024)
    arrays, args = {}, []
    consts, pool_mats = shape_constants()
    for name, a in [(n, _np.ascontiguousarray(inputs[n])) for n in _INS] + [("consts", consts), ("pool_mats", pool_mats)]:
        arrays[f"in_{name}_dram"] = a
        args.append(nc.dram_tensor(f"in_{name}_dram", a.shape, _mybir.dt.from_np(a.dtype), kind="ExternalInput").ap())
    args.append(nc.dram_tensor("out_0_dram", (1, S, D), F32, kind="ExternalOutput").ap())
    build(nc, *args)
    r = _run(nc, [arrays], core_ids=[0])
    return r.results[0]["out_0_dram"]
```

```python
from contextlib import ExitStack

import numpy as np

import concourse.bass as bass
from concourse import mybir

F32 = mybir.dt.float32
F32R = mybir.dt.float32r
BF16 = mybir.dt.bfloat16
I32 = mybir.dt.int32
ALU = mybir.AluOpType
ACT = mybir.ActivationFunctionType
AX = mybir.AxisListType.X

P = 128
D = 1024
S = 256
TT = S // P
KT = D // P
F1 = 2816
F2 = 4096
HD = 64
HD2 = 128
SP_IN = 2840
NCMP = 15
EPS = 1e-6
NEG = -1e30
TWO_PI = 6.283185307179586
LAM_INIT = 0.8 - 0.6 * float(np.exp(-0.3 * 1))
POOL_WINDOWS = (2, 4, 8, 16)

CONST_COLS = {}
_at = 0
for _name, _n in (("ident", 128), ("causal", 256), ("cmp_neg", 32), ("cmp_ok", 32), ("ax_cos", 128), ("ax_sin", 128),
                  ("inv_freq", 8), ("sel0", 128), ("sel1", 128), ("spread", 128), ("headmask", 512)):
    CONST_COLS[_name] = (_at, _at + _n)
    _at += _n
NCONST = _at


def shape_constants():
    c = np.zeros((P, NCONST), np.float32)

    def put(name, value):
        a, b = CONST_COLS[name]
        c[:, a:b] = value.reshape(P, b - a)

    i = np.arange(P)
    put("ident", np.eye(P, dtype=np.float32))
    causal = np.where(i[None, :] <= i[:, None], 0.0, NEG).astype(np.float32)
    put("causal", np.concatenate([causal, causal], 1))
    neg = np.full((P, 2, 16), NEG, np.float32)
    ok = np.zeros((P, 2, 16), np.float32)
    for t in range(TT):
        valid = (np.arange(NCMP) * 16 + 31)[None, :] <= (t * P + i)[:, None]
        neg[:, t, :NCMP] = np.where(valid, 0.0, NEG)
        ok[:, t, :NCMP] = valid
    put("cmp_neg", neg)
    put("cmp_ok", ok)
    half = HD2 // 2
    inv = (np.float32(10000.0) ** (-np.arange(0, half, 2, dtype=np.float32) / np.float32(half))).astype(np.float32)
    tok = (np.arange(TT)[None, :] * P + i[:, None])
    ang = np.stack([(tok // 64).astype(np.float32)[..., None] * inv, (tok % 64).astype(np.float32)[..., None] * inv], 2)
    put("ax_cos", np.cos(ang.astype(np.float64)).astype(np.float32))
    put("ax_sin", np.sin(ang.astype(np.float64)).astype(np.float32))
    rot = HD // 4
    invf = (np.float32(1.0) / (np.float32(500000.0) ** (np.arange(0, rot, 2, dtype=np.float32) / np.float32(rot)))).astype(np.float32)
    put("inv_freq", np.tile(invf, (P, 1)))
    put("sel0", np.tile((i % 32 == 0).astype(np.float32)[:, None], (1, P)))
    put("sel1", np.tile((i % 32 == 1).astype(np.float32)[:, None], (1, P)))
    spread = np.zeros((P, P), np.float32)
    for n in range(NCMP):
        spread[n, n::16] = 1.0
    put("spread", spread)
    hm = np.zeros((P, 8, 64), np.float32)
    for h in range(8):
        hm[h * 16:h * 16 + NCMP, h] = 1.0
    put("headmask", hm)
    pool = np.zeros((4, S, S), np.float32)
    for g, w in enumerate(POOL_WINDOWS):
        for t in range(S):
            lo, hi = max(t - w // 2, 0), min(t + w - w // 2, S)
            pool[g, lo:hi, t] += np.float32(1.0) / np.float32(hi - lo)
            pool[g, t, t] -= 1.0
    pool = pool.reshape(4, TT, P, S).transpose(2, 0, 1, 3).reshape(P, 4 * TT * S)
    return c, np.ascontiguousarray(pool)


def build(nc, x, c, positions, ada_w, ada_b, attn_norm, ffn_norm, ffn_w_gate, ffn_w_up, ffn_w_down,
          sp_w_in, sp_w_out, moba_q_norm, moba_k_norm, nsa_q_norm, nsa_k_norm, nsa_cmp_pos,
          nsa_cmp_w1, nsa_cmp_w2, diff_w_in, diff_w_out, diff_q_norm, diff_k_norm, diff_lambda,
          diff_out_norm, c_2, ctx_2, c_ctx_2, ada_w_2, ada_b_2, norm_g_2, mlp_w1_2, mlp_w2_2,
          pool_w_2, pool_scale_2, attn_w_qkv_2, attn_w_o_2, attn_q_g_2, attn_k_g_2, final_g_2,
          consts, pool_mats, out):
    stack = ExitStack()
    with stack:
        def sb(name, shape, dt=F32):
            return stack.enter_context(nc.sbuf_tensor(name, shape, dt))

        sems = {}

        def sem(name):
            if name not in sems:
                sems[name] = stack.enter_context(nc.semaphore(name))
            return sems[name]

        res = sb("res", [P, 2, TT, D])
        hT_hi = sb("hT_hi", [P, KT, S], F32R)
        hT_lo = sb("hT_lo", [P, KT, S], F32R)
        act_hi = sb("act_hi", [P, 2, 2 * S], F32R)
        act_lo = sb("act_lo", [P, 2, 2 * S], F32R)
        work = sb("work", [P, 16384])
        wraw = sb("wraw", [P, 4, 2048])
        whi = sb("whi", [P, 2, 2048], F32R)
        wlo = sb("wlo", [P, 2, 2048], F32R)
        ring = sb("ring", [P, 2, 2048])
        modrow = sb("modrow", [P, 6, 256])
        gate_b = sb("gate_b", [P, D])
        cst = sb("cst", [P, NCONST])
        ident_r = sb("ident_r", [P, P], F32R)
        causal_r = sb("causal_r", [P, 2 * P], F32R)
        params = sb("params", [P, P])
        paramT = sb("paramT", [P, P])
        cpad = sb("cpad", [P, 2, KT, 32])
        modT = sb("modT", [P, 4, 2, 2, 2, KT])
        modA = sb("modA", [P, 4, 2, 2, KT])
        gains = sb("gains", [P, 8, HD])
        gains2 = sb("gains2", [P, 2, HD2])
        gain_o = sb("gain_o", [P, HD2])
        pos_i = sb("pos_i", [P, TT], I32)
        pos_f = sb("pos_f", [P, TT])
        trig = sb("trig", [P, 2, TT, 8])
        trig_t = sb("trig_t", [P, 2, TT, 8])
        lam_p = sb("lam_p", [P, 4, HD])
        lam_s = sb("lam_s", [P, 8])
        mark = sb("mark", [P, 4])
        stat = sb("stat", [P, 64])
        rstat = sb("rstat", [P, 64])
        nwt = sb("nwt", [P, 64])
        nwt_i = sb("nwt_i", [P, 64], I32)
        sums = sb("sums", [P, 2, 2])
        zero16 = sb("zero16", [1, 512], BF16)
        hbuf = sb("hbuf", [P, 2, 512])
        rowsum = sb("rowsum", [P, 48])
        rowmax = sb("rowmax", [P, 2, 4])
        coef = sb("coef", [P, 2, 4])
        gsig = sb("gsig", [P, TT, 24])
        kcs = sb("kcs", [P, 32])
        vcr = sb("vcr", [16, 2 * HD])
        w2k = sb("w2k", [P, 2, 2, HD])
        w2v = sb("w2v", [P, 2, HD])
        cmp_m = sb("cmp_m", [P, 16])
        ps = stack.enter_context(nc.psum_tensor("ps", [P, 8, 512], F32))

        def const(name):
            a, b = CONST_COLS[name]
            return cst[:, a:b]

        def wk(a, n):
            return work[:, a:a + n]

        ident = const("ident")
        D_BANKS = (4, 5, 6, 2)
        ADA_BANK = 7
        H_BANKS = (2, 0, 1, 3)
        xn = wk(12288, 2048).rearrange("p (t n) -> p t n", t=TT)
        full = wk(14336, 2048).rearrange("p (k n) -> p k n", k=KT)
        diag = hbuf[:, 0, 0:2 * P].rearrange("p (t n) -> p t n", t=TT)
        hid = wk(0, 8192)

        r0 = wk(0, TT * SP_IN).rearrange("p (t n) -> p t n", t=TT)
        kd0 = wk(5680, 2048).rearrange("p (t y g n) -> p t y g n", t=TT, y=4, g=2)
        qt0 = wk(7728, 5120).rearrange("p (r n) -> p r n", r=20)
        cmp_s = wk(14384, 256).rearrange("p (t h n) -> p t h n", t=TT, h=8)
        cmp_T = wk(14640, 256).rearrange("p (t n) -> p t n", t=TT)
        hidr = work[0:64, 14896:15152]
        r1 = wk(0, TT * 3072).rearrange("p (t n) -> p t n", t=TT)
        qt1 = wk(6144, 4096).rearrange("p (r n) -> p r n", r=16)
        kvc = wk(0, 2048).rearrange("p (t n) -> p t n", t=TT)
        kvl = wk(2048, 2048).rearrange("p (t n) -> p t n", t=TT)
        q3 = wk(4096, 2048).rearrange("p (t n) -> p t n", t=TT)
        qt3 = wk(6144, 2048).rearrange("p (r n) -> p r n", r=8)
        kt3 = wk(8192, 2048).rearrange("p (r n) -> p r n", r=4)

        segs = []

        def rows_of(w):
            return w.rearrange("(t p) n -> p t n", p=P)

        def seg(name, kind, srcs, count, width=1024):
            base = segs[-1]["base"] + segs[-1]["count"] if segs else 0
            segs.append(dict(name=name, kind=kind, srcs=srcs, count=count, base=base, width=width))
            return segs[-1]

        SPI, DFI, QKV = rows_of(sp_w_in[0]), rows_of(diff_w_in[0]), rows_of(attn_w_qkv_2[0])
        for n, (a, b) in enumerate(((0, 1024), (1024, 2048), (2048, SP_IN))):
            seg(f"in0_{n}", "row", [SPI[:, :, a:b]], 4, b - a)
        seg("out0", "row", [rows_of(sp_w_out[0])], 4)
        seg("up0", "pair", [rows_of(ffn_w_gate[0]), rows_of(ffn_w_up[0])], 22)
        seg("down0", "down", [rows_of(ffn_w_down[0])], 11)
        for n in range(3):
            seg(f"in1_{n}", "row", [DFI[:, :, n * 1024:(n + 1) * 1024]], 4)
        seg("out1", "row", [rows_of(diff_w_out[0])], 4)
        seg("up1", "pair", [rows_of(ffn_w_gate[1]), rows_of(ffn_w_up[1])], 22)
        seg("down1", "down", [rows_of(ffn_w_down[1])], 11)
        for s_ in range(2):
            seg(f"pool{s_}", "pool", [pool_w_2[0]], 1)
            seg(f"up2{s_}", "up", [rows_of(mlp_w1_2[0])], 16)
            seg(f"down2{s_}", "down", [rows_of(mlp_w2_2[0])], 16)
        seg("kvc", "row", [QKV[:, :, 1024:2048]], 4)
        seg("q3", "row", [QKV[:, :, 0:1024]], 4)
        seg("kvl", "row", [QKV[:, :, 1024:2048]], 4)
        seg("out3", "row", [rows_of(attn_w_o_2[0])], 4)
        seg("up3", "up", [rows_of(mlp_w1_2[1])], 16)
        seg("down3", "down", [rows_of(mlp_w2_2[1])], 16)
        by_name = {s_["name"]: s_ for s_ in segs}
        last_seg = segs[-1]
        UNITS = last_seg["base"] + last_seg["count"]
        LOOPED = ("pair", "up", "down")

        def bodies(s_):
            return (s_["count"] - 2) // 4 if s_["kind"] in LOOPED else 0

        def loops_of(name):
            n, m = bodies(by_name[name]), LOOP_PLAN.get(name, (0, 0))[1]
            return [x for x in ((0, m, True), (m, n - m, False)) if x[1]]

        def seg_of(u):
            return next(s_ for s_ in segs if s_["base"] <= u < s_["base"] + s_["count"])

        def unit_source(s_, i, k4=None):
            kind = s_["kind"]
            if kind in ("row", "down"):
                at = 2 * i if k4 is None else k4 * 8 + 2 * i
                return s_["srcs"][0][:, bass.ds(at, 2), :]
            if kind == "pool":
                return s_["srcs"][0].rearrange("g (k p) n -> p (g k) n", p=P)
            if kind == "pair":
                at = (i // 2) * 256 if k4 is None else k4 * 512 + (i // 2) * 256
                return s_["srcs"][i % 2][:, :, bass.ds(at, 256)]
            at = i * 256 if k4 is None else k4 * 1024 + i * 256
            return s_["srcs"][0][:, :, bass.ds(at, 256)]

        def unit_width(s_):
            return 2 * s_["width"] if s_["kind"] == "row" else 2048

        def unit_split(s_):
            return {"row": 2, "down": 2, "pair": 8, "up": 8, "pool": 8}[s_["kind"]]

        raw_full = [sem(f"raw_full{j}") for j in range(4)]
        hi_ready, lo_ready, unit_done = sem("hi_ready"), sem("lo_ready"), sem("unit_done")

        hid_base, n_ = {}, 2
        for s_ in segs:
            if s_["kind"] in ("pair", "up"):
                tag = s_["name"][2:]
                hid_base[tag] = n_
                n_ += s_["count"] // 2 if s_["kind"] == "pair" else s_["count"]
        hid_done, hact_done = sem("hid_done"), sem("hact_done")

        VECTORS = 24
        CMP_AT = 12
        RING_UNITS = 4 * VECTORS + 4
        adaw = [ada_w[0], ada_w[1], ada_w_2[0], ada_w_2[1]]
        adab = [ada_b[0:1], ada_b[1:2], ada_b_2[0:1], ada_b_2[1:2]]
        w1c = nsa_cmp_w1[0].rearrange("s l d e -> s (l d) e").rearrange("s (k p) e -> s p k e", p=P)

        def ring_at(g, j):
            return 4 * g + j + (0 if g < 3 else 4)

        def ring_unit(r):
            if CMP_AT <= r < CMP_AT + 4:
                return "cmp", (r - CMP_AT) // 2, (r - CMP_AT) % 2
            r -= 4 if r >= CMP_AT + 4 else 0
            return "ada", r // 4, r % 4

        STEP_PLAN = [g_ for g_ in range(VECTORS) if g_ < 6 or 9 <= g_ < 12 or g_ >= 21]
        LOOP_PLAN = {"up0": (6, 3), "up1": (12, 5), "down1": (17, 1), "up21": (18, 3)}
        EARLY = range(2, 8)
        ring_full = [sem("ring_full0"), sem("ring_full1")]
        early_full = {r: sem(f"early_full{r}") for r in EARLY}
        ring_used = sem("ring_used")
        mod_rows, ada_turn, mod_ready, bias_landed = sem("mod_rows"), sem("ada_turn"), sem("mod_ready"), sem("bias_landed")

        def ring_view(r):
            return wk((r - EARLY.start) * 2048, 2048) if r in EARLY else ring[:, r % 2, :]

        def ring_dma(eng, r, k=None):
            if r >= RING_UNITS:
                return
            kind, a, b = ring_unit(r)
            if r >= EARLY.stop:
                before = r - 1 - (len(EARLY) if r < EARLY.stop + 2 else 0)
                eng.wait_ge(ring_used, before if k is None else k * 4 + before)
            dst = ring_view(r)
            if kind == "ada":
                l, v = a // 6, a % 6
                at = v * D if k is None else k * D + v * D
                src = adaw[l][2 * b * P:(2 * b + 2) * P, :].rearrange("(k p) n -> p k n", p=P)[:, :, bass.ds(at, D)]
                dst = dst.rearrange("p (k n) -> p k n", k=2)
            else:
                dst = dst.rearrange("p (k e) -> p k e", k=8)
                src = w1c[a][:, b * 8:(b + 1) * 8, :]
            eng.dma_start(dst, src).then_inc(early_full[r] if r in EARLY else ring_full[r % 2], 16)

        def ring_wait(eng, r, k=None):
            if r in EARLY:
                eng.wait_ge(early_full[r], 16)
                return
            landed = 16 * (r // 2 + 1 - (len(EARLY) // 2 if r >= EARLY.stop else 0))
            eng.wait_ge(ring_full[r % 2], landed if k is None else k * 32 + landed)

        PANEL_KIND = ["rows"] * 3 + ["res", "res"] + ["rows"] * 3 + ["res", "res"] + ["res"] * 4 + ["rows"] * 3 + ["res", "res"]
        act_emptied, dve_emptied = sem("act_emptied"), sem("dve_emptied")
        act_count, dve_count = [0], [0]
        for kind_ in PANEL_KIND:
            act_count.append(act_count[-1] + (2 if kind_ == "rows" else 0))
            dve_count.append(dve_count[-1] + (2 if kind_ == "rows" else 4))
        PANEL_SEGS = ["in0_0", "in0_1", "in0_2", "out0", "down0", "in1_0", "in1_1", "in1_2", "out1", "down1",
                      "pool0", "down20", "pool1", "down21", "kvc", "q3", "kvl", "out3", "down3"]
        panel_end = [by_name[n_]["base"] + by_name[n_]["count"] for n_ in PANEL_SEGS]
        gate_psum, gate_copied = sem("gate_psum"), sem("gate_copied")

        NORMS = [(0, 0, 0), (0, 0, 1), (0, 1, 0), (0, 1, 1), (0, 2, 0), (0, 2, 1), (1, 2, 0), (1, 2, 1),
                 (1, 3, 0), (0, 3, 0), (0, 3, 1)]
        RESIDUALS_BEFORE = [0, 1, 2, 3, 4, 5, 6, 7, 8, 8, 9, 10]
        GATES = [(0, 0, 0), (0, 0, 1), (1, 0, 0), (1, 0, 1), (2, 0, 0), (2, 0, 1), (2, 1, 0), (2, 1, 1), (3, 0, 0), (3, 0, 1)]
        res_panels = [n for n, k_ in enumerate(PANEL_KIND) if k_ == "res"]

        def pair_rows(rows, r, t):
            return rows[:, t, r * P:(r + 1) * P]

        def q_groups(stage):
            if stage == 0:
                def src(r, t):
                    if r < 8:
                        return r0[:, t, r * P:(r + 1) * P]
                    if r < 12:
                        return r0[:, t, 1536 + (r - 8) * P:1536 + (r - 7) * P]
                    y, g = {12: (2, 0), 13: (2, 1), 14: (3, 0), 15: (3, 1), 16: (0, 0), 17: (0, 1), 18: (1, 0), 19: (1, 1)}[r]
                    return kd0[:, t, y, g, :]
                return [([src(r, t) for r in (2 * g, 2 * g + 1) for t in range(TT)], qt0[:, 2 * g:2 * g + 2, :]) for g in range(10)]
            if stage == 1:
                return [([r1[:, t, r * P:(r + 1) * P] for r in (2 * g, 2 * g + 1) for t in range(TT)],
                         qt1[:, 2 * g:2 * g + 2, :]) for g in range(8)]
            q = [([q3[:, t, r * P:(r + 1) * P] for r in (2 * g, 2 * g + 1) for t in range(TT)],
                  qt3[:, 2 * g:2 * g + 2, :]) for g in range(4)]
            k = [([src[:, t, h * P:(h + 1) * P] for src in (kvc, kvl) for t in range(TT)], kt3[:, h, :]) for h in range(4)]
            return q + k

        class Att:
            pass

        def att(stage):
            a = Att()
            a.n = stage
            a.scores, a.negmax, a.exps = sem(f"a{stage}_scores"), sem(f"a{stage}_negmax"), sem(f"a{stage}_exps")
            a.turned, a.pT, a.pv = sem(f"a{stage}_turned"), sem(f"a{stage}_pT"), sem(f"a{stage}_pv")
            a.taken, a.mixed = sem(f"a{stage}_taken"), sem(f"a{stage}_mixed")
            a.steps = {0: 12, 1: 8, 3: 8}[stage]
            a.width = 512 if stage == 3 else 384
            a.maps = 1 if stage == 1 else 2
            a.lag = 2 if stage == 1 else 1
            a.ada = {0: 4, 1: 8, 3: 8}[stage]
            base = {0: 12848, 1: 10240, 3: 10240}[stage]
            a.p = wk(base, 4 * a.width).rearrange("p (b m n) -> p b m n", b=2, m=2)
            base += 4 * a.width
            if stage == 1:
                a.mix = wk(base, 2 * a.width).rearrange("p (b m n) -> p b m n", b=2, m=1)
                base += 2 * a.width
            a.pt = wk(base, 2 * a.maps * a.width).rearrange("p (b m n) -> p b m n", b=2, m=a.maps)
            a.scale = float(HD2 if stage == 3 else HD) ** -0.5
            return a

        ATT = {n: att(n) for n in (0, 1, 3)}
        out_rows = {0: r0, 1: r1, 3: q3}

        block = stack.enter_context(nc.Block())

        @block.sync
        def _(sp):
            ld = sem("small_params")
            sp.dma_start(cst[:, :], consts).then_inc(ld, 16)
            sp.wait_ge(sem("params_zero"), 1)
            sp.dma_start(params[0:16, :], attn_norm.rearrange("l (k n) -> (l k) n", n=P)).then_inc(ld, 16)
            sp.dma_start(params[16:32, :], ffn_norm.rearrange("l (k n) -> (l k) n", n=P)).then_inc(ld, 16)
            sp.dma_start(params[32:64, :], norm_g_2.rearrange("l j (k n) -> (l j k) n", n=P)).then_inc(ld, 16)
            sp.dma_start(params[64:96, :], nsa_cmp_pos[0].rearrange("s (k a) d -> (s k) (a d)", a=2)).then_inc(ld, 16)
            sp.dma_start(params[96:104, :], c.rearrange("b (k n) -> (b k) n", n=P)).then_inc(ld, 16)
            sp.dma_start(params[104:112, :], c_2.rearrange("b (k n) -> (b k) n", n=P)).then_inc(ld, 16)
            sp.dma_start(params[112:120, :], c_ctx_2.rearrange("(k n) -> k n", n=P)).then_inc(ld, 16)
            xl = sem("x_landed")
            sp.dma_start(res[:, 0, :, :], x[0].rearrange("(t p) n -> p t n", p=P)).then_inc(xl, 16)
            sp.dma_start(pos_i[:, :], positions[0].rearrange("(t p) -> p t", p=P), allow_slow_non_contiguous=True).then_inc(xl, 16)

            def weight_dma(s_, i, k4=None):
                u = s_["base"] + i
                slot = u % 4
                if u >= 4 or k4 is not None:
                    sp.wait_ge(lo_ready, 2 * (u - 3) if k4 is None else k4 * 8 + 2 * (u - 3))
                dst = wraw[:, slot, 0:unit_width(s_)].rearrange("p (k n) -> p k n", k=unit_split(s_))
                sp.dma_start(dst, unit_source(s_, i, k4)).then_inc(raw_full[slot], 16)

            sp.wait_ge(ring_used, 1)
            for s_ in segs:
                if s_["name"] == "in0_1":
                    g = sem("gains_landed")
                    rows = [moba_q_norm[0:1], moba_k_norm[0:1], nsa_q_norm[0:1], nsa_k_norm[0, 0:1], nsa_k_norm[0, 1:2],
                            nsa_k_norm[0, 2:3], diff_q_norm[0:1], diff_k_norm[0:1]]
                    for n, row in enumerate(rows):
                        sp.dma_start(gains[:, n, :], row.to_broadcast([P, HD])).then_inc(g, 16)
                    sp.dma_start(gains2[:, 0, :], attn_q_g_2[0:1].to_broadcast([P, HD2])).then_inc(g, 16)
                    sp.dma_start(gains2[:, 1, :], attn_k_g_2[0:1].to_broadcast([P, HD2])).then_inc(g, 16)
                    sp.dma_start(gain_o[:, :], diff_out_norm[0:1].to_broadcast([P, HD2])).then_inc(g, 16)
                    for n in range(4):
                        sp.dma_start(lam_p[:, n, :], diff_lambda[0, n:n + 1].to_broadcast([P, HD])).then_inc(g, 16)
                    w2 = nsa_cmp_w2[0].rearrange("s (k p) d -> s p k d", p=P)
                    sp.dma_start(w2k[:, :, 0, :], w2[0]).then_inc(g, 16)
                    sp.dma_start(w2k[:, :, 1, :], w2[0]).then_inc(g, 16)
                    sp.dma_start(w2v[:, :, :], w2[1]).then_inc(g, 16)
                    sp.dma_start(res[:, 1, :, :], ctx_2[0].rearrange("(t p) n -> p t n", p=P)).then_inc(sem("ctx_landed"), 16)
                n = bodies(s_)
                if n:
                    with sp.Fori(0, n) as k4:
                        for j in range(4):
                            weight_dma(s_, j, k4)
                for i in range(4 * n, s_["count"]):
                    weight_dma(s_, i)
            sp.wait_ge(unit_done, UNITS)
            sp.dma_start(wk(0, D), final_g_2.rearrange("(a n) -> a n", a=1).to_broadcast([P, D])).then_inc(sem("final_landed"), 16)
            for t in range(TT):
                sp.wait_ge(sem("out_ready"), t + 1)
                sp.dma_start(out[0, t * P:(t + 1) * P, :], xn[:, t, :]).then_inc(sem("stored"), 16)
            sp.wait_ge(sem("stored"), 16 * TT)

        @block.scalar
        def _(act):
            chained = [0]
            chain = sem("act_chain")
            ring_next = [0]
            step_no = [0]
            panel_no = [0]
            norm_no = [0]
            gate_no = [0]

            def link(ins):
                chained[0] += 1
                ins.then_inc(chain, 1)
                act.wait_ge(chain, chained[0])

            def ring_fill(upto):
                while ring_next[0] < min(upto, RING_UNITS):
                    ring_dma(act, ring_next[0])
                    ring_next[0] += 1

            def ada_step(n=1):
                for _ in range(n):
                    q, j = step_no[0] // 4, step_no[0] % 4
                    step_no[0] += 1
                    if q < len(STEP_PLAN):
                        ring_fill(ring_at(STEP_PLAN[q], j) + 3)

            def ada_body_unit(name, j, k):
                ring_dma(act, ring_at(LOOP_PLAN[name][0], j) + 2, k)

            def bias(l):
                for strm in range(2 if l >= 2 else 1):
                    act.dma_start(modrow[strm:P:32, :, :], adab[l].rearrange("a (v j n) -> (a j) v n", v=6, j=4)).then_inc(bias_landed, 16)

            def split_weights(s_, i, k4=None):
                u = s_["base"] + i
                act.wait_ge(raw_full[u % 4], 16 * (u // 4 + 1) if k4 is None else k4 * 16 + 16 * (u // 4 + 1))
                if u >= 2 or k4 is not None:
                    act.wait_ge(unit_done, u - 1 if k4 is None else k4 * 4 + (u - 1))
                if s_["kind"] == "down":
                    if k4 is None:
                        act.wait_ge(hid_done, hid_base[s_["name"][4:]] + i + 1)
                    at = 512 * i if k4 is None else k4 * 2048 + 512 * i
                    nc.scalar.activation(act_hi[:, u % 2, :], hid[:, bass.ds(at, 512)], ACT.Copy)
                w = unit_width(s_)
                for h in range(2):
                    part = slice(h * w // 2, (h + 1) * w // 2)
                    nc.scalar.activation(whi[:, u % 2, part], wraw[:, u % 4, part], ACT.Copy).then_inc(hi_ready, 1)

            def split_unit(u):
                if u < UNITS:
                    s_ = seg_of(u)
                    split_weights(s_, u - s_["base"])

            def hidden_out(s_, i, k4=None):
                u = s_["base"] + i
                tag = s_["name"][2:]
                plus = (lambda v: v) if k4 is None else (lambda v: k4 * (2 if s_["kind"] == "pair" else 4) + v)
                if s_["kind"] == "pair":
                    if i % 2:
                        return
                    n = i // 2
                    act.wait_ge(unit_done, u + 1 if k4 is None else k4 * 4 + (u + 1))
                    act.wait_ge(hid_done, plus(hid_base[tag] + n - 1))
                    nc.scalar.activation(hbuf[:, n % 2, :], ps[:, H_BANKS[i % 4], :], ACT.Silu).then_inc(hact_done, 1)
                else:
                    act.wait_ge(unit_done, u + 1 if k4 is None else k4 * 4 + (u + 1))
                    b = i % 2
                    act.wait_ge(hid_done, plus(hid_base[tag] + i - 1))
                    nc.scalar.activation(hbuf[:, b, :], ps[:, H_BANKS[i % 4], :], ACT.Relu).then_inc(hact_done, 1)
                    act.wait_ge(hact_done, plus(hid_base[tag] + i + 1))
                    at = 512 * i if k4 is None else k4 * 2048 + 512 * i
                    nc.scalar.activation(hid[:, bass.ds(at, 512)], hbuf[:, b, :], ACT.Square).then_inc(hid_done, 1)

            def stream(name, hold_last=False):
                s_ = by_name[name]
                if s_["kind"] == "down":
                    act.wait_ge(hid_done, hid_base[name[4:]] + s_["count"])
                n = bodies(s_)
                for first, many, ada in loops_of(name):
                    if ada and many == 1:
                        for j in range(4):
                            if s_["kind"] != "down":
                                hidden_out(s_, j)
                            split_unit(s_["base"] + j + 2)
                            ring_fill(ring_at(LOOP_PLAN[name][0], j) + 3)
                        continue
                    with act.Fori(first, first + many) as k4:
                        for j in range(4):
                            split_weights(s_, j + 2, k4)
                            if s_["kind"] != "down":
                                hidden_out(s_, j, k4)
                            if ada:
                                ada_body_unit(name, j, k4)
                    if ada:
                        ring_next[0] += 4 * many
                for i in range(4 * n, s_["count"]):
                    if s_["kind"] != "down":
                        hidden_out(s_, i)
                    if not (hold_last and i == s_["count"] - 1):
                        split_unit(s_["base"] + i + 2)

            def row_segment(name, hold_last=True, ada=False):
                s_ = by_name[name]
                for i in range(s_["count"]):
                    if ada:
                        ada_step()
                    if not (hold_last and i == s_["count"] - 1):
                        split_unit(s_["base"] + i + 2)

            def held_split(name):
                s_ = by_name[name]
                split_unit(s_["base"] + s_["count"] + 1)

            def panel_rows(rows, col, width):
                n = panel_no[0]
                act.wait_ge(unit_done, panel_end[n])
                for h in range(2):
                    w = min(512, width - 512 * h)
                    nc.scalar.activation(rows[:, 0, col + 512 * h:col + 512 * h + w], ps[:, D_BANKS[h], 0:w], ACT.Copy).then_inc(act_emptied, 1)

            def next_panel():
                panel_no[0] += 1

            def norm(spread_gate=False):
                n = norm_no[0]
                norm_no[0] += 1
                strm, l, f = NORMS[n] if n < len(NORMS) else (0, 0, 0)
                if n > 0:
                    act.wait_ge(sem("hT_ready"), 4 * n)
                if n == 6:
                    act.wait_ge(sem("ctx_landed"), 16)
                for t in range(TT):
                    if n > 0:
                        act.wait_ge(sem("res_ready"), 2 * RESIDUALS_BEFORE[n] - 1 + t)
                    nc.scalar.activation(xn[:, t, :], res[:, strm, t, :], ACT.Square, accum_out=sums[:, n % 2, t:t + 1]).then_inc(sem("squares"), 1)
                if n >= len(NORMS):
                    return
                if spread_gate:
                    gate()
                for b in (1, 3):
                    act.wait_ge(sem("xT_psum"), 4 * n + b + 1)
                    if b == 1:
                        act.wait_ge(mod_ready, 2 * l + f + 1)
                    for k in (2 * b, 2 * b + 1):
                        shift = 0.0 if n in (4, 6) else modT[:, l, strm, f, 0, k:k + 1]
                        ins = nc.scalar.activation(full[:, k, :], ps[:, H_BANKS[b], (k % 2) * S:(k % 2 + 1) * S], ACT.Identity,
                                                   bias=shift, scale=modA[:, l, strm, f, k:k + 1])
                    link(ins)
                    nc.scalar.activation(hT_hi[:, 2 * b:2 * b + 2, :], full[:, 2 * b:2 * b + 2, :], ACT.Copy).then_inc(sem("hT_hi_act"), 1)

            def gate():
                e = gate_no[0]
                gate_no[0] += 1
                if e > 0:
                    act.wait_ge(dve_emptied, dve_count[res_panels[e - 1] + 1])
                for h in range(2):
                    act.wait_ge(gate_psum, 2 * e + h + 1)
                    nc.scalar.activation(gate_b[:, 512 * h:512 * h + 512], ps[:, D_BANKS[h], :], ACT.Copy).then_inc(gate_copied, 1)

            def turns(stage):
                for g, (_, dst) in enumerate(q_groups(stage)):
                    if g % 2 == 0:
                        act.wait_ge(sem(f"turned{stage}"), g + 1)
                        d = dst if len(dst.shape) == 2 else dst.rearrange("p a b -> p (a b)")
                        nc.scalar.activation(d, ps[:, g % 4, :], ACT.Copy).then_inc(sem(f"turn_act{stage}"), 1)

            def attention(stage):
                a = ATT[stage]

                def exps(i):
                    act.wait_ge(a.negmax, i + 1)
                    if i >= 2:
                        if stage == 1:
                            act.wait_ge(a.mixed, i - 1)
                        else:
                            act.wait_ge(a.turned, i - 1)
                    for m in range(2):
                        bank = 2 * (i % 2) + m
                        if stage == 3:
                            spans = ((0, 512, 0),)
                        else:
                            spans = ((0, 128, 0), (128, 384, 1))
                        for lo, hi, r in spans:
                            col = 4 * i + 2 * m + r if stage != 3 else 2 * i + m
                            bias = rowmax[:, i % 2, 2 * m + r:2 * m + r + 1] if stage != 3 else rowmax[:, i % 2, m:m + 1]
                            ins = nc.scalar.activation(a.p[:, i % 2, m, lo:hi], ps[:, bank, lo:hi], ACT.Exp, bias=bias,
                                                       scale=a.scale, accum_out=rowsum[:, col:col + 1])
                    ins.then_inc(a.exps, 1)

                def copy_pt(i):
                    act.wait_ge(a.turned, i + 1)
                    if i >= 2:
                        act.wait_ge(a.pv, i - 1)
                    if stage == 1:
                        src = ps[:, 4 + i % 2, 0:a.width]
                        dst = a.pt[:, i % 2, 0, :]
                    else:
                        src = ps[:, 4:6, 0:a.width]
                        dst = a.pt[:, i % 2, :, :]
                    nc.scalar.activation(dst, src, ACT.Copy).then_inc(a.pT, 1)

                for i in range(a.steps + a.lag + 1):
                    if i < a.steps:
                        exps(i)
                    if a.lag <= i < a.steps + a.lag:
                        copy_pt(i - a.lag)
                    if i < a.ada:
                        ada_step()

            def out_turn(stage):
                for b in range(4):
                    act.wait_ge(sem(f"out_turned{stage}"), b + 1)
                    nc.scalar.activation(hT_hi[:, 2 * b:2 * b + 2, :], ps[:, H_BANKS[b], :].rearrange("p (k n) -> p k n", k=2), ACT.Copy).then_inc(sem(f"out_hi{stage}"), 1)

            ring_fill(8)
            act.wait_ge(sem("modrow_zero"), 1)
            bias(0)
            act.wait_ge(sem("paramT_ready"), 1)
            for n, (blk, col) in enumerate(((0, 96), (1, 104), (1, 112))):
                ins = nc.scalar.activation(cpad[:, blk, :, n // 2:n // 2 + 1], paramT[:, col:col + 8].rearrange("p (k a) -> p k a", a=1), ACT.Silu)
            ins.then_inc(sem("silu_c"), 1)
            act.wait_ge(sem("angles"), 1)
            nc.scalar.activation(trig[:, :, :, :], trig_t[:, :, :, :], ACT.Sin).then_inc(sem("trig_ready"), 1)
            act.wait_ge(sem("cst_r"), 1)
            act.wait_ge(sem("x_landed"), 32)
            split_unit(0)
            split_unit(1)
            ada_step(8)
            norm()
            for n, w in enumerate((1024, 1024, 792)):
                row_segment(f"in0_{n}", ada=(n == 0))
                panel_rows(r0, 1024 * n, w)
                next_panel()
                held_split(f"in0_{n}")
            act.wait_ge(dve_emptied, 6)
            act.wait_ge(act_emptied, 6)
            nc.scalar.activation(gsig[:, :, :], r0[:, :, 2816:2840], ACT.Exp, scale=-1.0).then_inc(sem("gsig_exp"), 1)
            act.wait_ge(sem("heads0"), 1)
            for t in range(TT):
                for y, col, w in ((0, 2048, 4), (2, 2304, 2), (3, 2560, 2)):
                    src = r0[:, t, col:col + w * HD].rearrange("p (g d) -> p g d", d=HD)
                    dst = kd0[:, t, :, :, :].rearrange("p y g n -> p (y g) n")[:, 2 * y:2 * y + w, :].rearrange("p g (u d) -> p g u d", u=2)
                    for u_ in range(2):
                        ins = nc.scalar.activation(dst[:, :, u_, :], src, ACT.Copy)
            ins.then_inc(sem("doubled"), 1)
            gate()
            turns(0)
            c0 = CMP_AT
            ring_fill(c0 + 4)
            act.wait_ge(ring_used, c0 + 4)
            act.wait_ge(sem("hidr_zero"), 1)
            for s_ in range(2):
                ins = nc.scalar.activation(hidr[32 * s_:32 * s_ + 30, :], ps[32 * s_:32 * s_ + 30, 0, 0:256], ACT.Silu)
            ins.then_inc(sem("cmp_silu"), 1)
            ring_fill(c0 + 6)
            ada_step(4)
            act.wait_ge(sem("cmp_shift"), 1)
            nc.scalar.activation(cmp_s, cmp_s, ACT.Exp, scale=float(HD) ** -0.5).then_inc(sem("cmp_exp"), 1)
            ada_step(4)
            attention(0)
            out_turn(0)
            row_segment("out0")
            next_panel()
            norm(spread_gate=True)
            bias(1)
            held_split("out0")
            stream("up0")
            stream("down0", hold_last=True)
            next_panel()
            norm()
            held_split("down0")
            for n in range(3):
                row_segment(f"in1_{n}")
                panel_rows(r1, 1024 * n, 1024)
                next_panel()
                held_split(f"in1_{n}")
            act.wait_ge(sem("lam_sum"), 1)
            nc.scalar.activation(lam_s[:, 2:4], lam_s[:, 0:2], ACT.Exp).then_inc(sem("lam_exp"), 1)
            gate()
            turns(1)
            attention(1)
            out_turn(1)
            row_segment("out1", ada=True)
            next_panel()
            norm(spread_gate=True)
            bias(2)
            held_split("out1")
            stream("up1")
            stream("down1", hold_last=True)
            next_panel()
            for s_ in range(2):
                act.wait_ge(unit_done, panel_end[9 if s_ == 0 else 11])
                act.dma_start(wk(0, 2048), pool_mats).then_inc(sem("pool_landed"), 16)
                act.dma_start(wk(2048, D), pool_scale_2[0:1].to_broadcast([P, D])).then_inc(sem("pool_landed"), 16)
                norm()
                if s_ == 0:
                    held_split("down1")
                else:
                    held_split("down20")
                gate_no[0] += 1
                next_panel()
                norm(spread_gate=True)
                split_unit(by_name[f"pool{s_}"]["base"] + 2)
                if s_ == 1:
                    bias(3)
                stream(f"up2{s_}")
                stream(f"down2{s_}", hold_last=True)
                next_panel()
            norm()
            held_split("down21")
            row_segment("kvc")
            panel_rows(kvc, 0, 1024)
            next_panel()
            norm()
            held_split("kvc")
            for name, rows in (("q3", q3), ("kvl", kvl)):
                row_segment(name)
                panel_rows(rows, 0, 1024)
                next_panel()
                held_split(name)
            gate()
            turns(3)
            attention(3)
            out_turn(3)
            row_segment("out3", ada=True)
            next_panel()
            norm(spread_gate=True)
            held_split("out3")
            stream("up3")
            stream("down3")
            next_panel()
            norm()

        @block.vector
        def _(dve):
            chained = [0]
            chain = sem("dve_chain")
            step_no = [0]
            panel_no = [0]
            norm_no = [0]
            gate_no = [0]

            def link(ins):
                chained[0] += 1
                ins.then_inc(chain, 1)
                dve.wait_ge(chain, chained[0])

            def vector_out(g, k=None):
                l, v = g // 6, g % 6
                r = ring_at(g, 3)
                dve.wait_ge(ring_used, r + 1 if k is None else k * 4 + (r + 1))
                if v == 0 and k is None:
                    dve.wait_ge(bias_landed, (16, 32, 64, 96)[l])
                at = v * 256 if k is None else k * 256 + v * 256
                m = modrow[:, :, :].rearrange("p v n -> p (v n)")[:, bass.ds(at, 256)]
                nc.vector.tensor_tensor(m, ps[:, ADA_BANK, 0:256], m, ALU.add).then_inc(mod_rows, 1)

            def ada_step(n=1):
                for _ in range(n):
                    q, j = step_no[0] // 4, step_no[0] % 4
                    step_no[0] += 1
                    if q < len(STEP_PLAN) and j == 3:
                        vector_out(STEP_PLAN[q])

            def columns(l, f):
                dve.wait_ge(ada_turn, 2 * l + f + 1)
                for strm in range(2 if l >= 2 else 1):
                    src = ps[:, ADA_BANK, :].rearrange("p (w q j r) -> p w q j r", w=2, q=2, r=32)[:, :, :, :, strm]
                    for w in range(2):
                        dst = modT[:, l, strm, f, w, :].rearrange("p (j q) -> p q j", q=2)
                        ins = nc.vector.tensor_copy(dst, src[:, w])
                link(ins)
                g = 16 * f + 8 * l if l < 2 else 32 + (l - 2) * 16 + 8 * f
                for strm in range(2 if l >= 2 else 1):
                    ins = nc.vector.scalar_tensor_tensor(out=modA[:, l, strm, f, :], in0=modT[:, l, strm, f, 1, :], scalar=1.0,
                                                         in1=paramT[:, g:g + 8], op0=ALU.add, op1=ALU.mult)
                ins.then_inc(mod_ready, 1)
                dve.wait_ge(mod_ready, 2 * l + f + 1)

            def split_weights(s_, i, k4=None):
                u = s_["base"] + i
                dve.wait_ge(hi_ready, 2 * u + 1 if k4 is None else k4 * 8 + (2 * u + 1))
                if s_["kind"] == "down":
                    at = 512 * i if k4 is None else k4 * 2048 + 512 * i
                    nc.vector.tensor_tensor(act_lo[:, u % 2, :], hid[:, bass.ds(at, 512)], act_hi[:, u % 2, :].bitcast(F32), ALU.subtract)
                w = unit_width(s_)
                for h in range(2):
                    part = slice(h * w // 2, (h + 1) * w // 2)
                    if h == 1:
                        dve.wait_ge(hi_ready, 2 * u + 2 if k4 is None else k4 * 8 + (2 * u + 2))
                    nc.vector.tensor_tensor(wlo[:, u % 2, part], wraw[:, u % 4, part], whi[:, u % 2, part].bitcast(F32), ALU.subtract).then_inc(lo_ready, 1)

            def split_unit(u):
                if u < UNITS:
                    s_ = seg_of(u)
                    split_weights(s_, u - s_["base"])

            def hidden_out(s_, i, k4=None):
                if s_["kind"] != "pair" or i % 2 == 0:
                    return
                u = s_["base"] + i
                n = i // 2
                hb = hid_base[s_["name"][2:]]
                dve.wait_ge(unit_done, u + 1 if k4 is None else k4 * 4 + (u + 1))
                dve.wait_ge(hact_done, hb + n + 1 if k4 is None else k4 * 2 + (hb + n + 1))
                at = 512 * n if k4 is None else k4 * 1024 + 512 * n
                nc.vector.tensor_tensor(hid[:, bass.ds(at, 512)], ps[:, H_BANKS[i % 4], :], hbuf[:, n % 2, :], ALU.mult).then_inc(hid_done, 1)

            def stream(name, hold_last=False):
                s_ = by_name[name]
                n = bodies(s_)
                for first, many, ada in loops_of(name):
                    if ada and many == 1:
                        for j in range(4):
                            hidden_out(s_, j)
                            split_unit(s_["base"] + j + 2)
                        vector_out(LOOP_PLAN[name][0])
                        continue
                    if ada:
                        g = LOOP_PLAN[name][0]
                        if g % 6 == 0:
                            dve.wait_ge(bias_landed, (16, 32, 64, 96)[g // 6])
                    with dve.Fori(first, first + many) as k4:
                        for j in range(4):
                            split_weights(s_, j + 2, k4)
                            hidden_out(s_, j, k4)
                        if ada:
                            vector_out(g, k4)
                for i in range(4 * n, s_["count"]):
                    hidden_out(s_, i)
                    if not (hold_last and i == s_["count"] - 1):
                        split_unit(s_["base"] + i + 2)

            def row_segment(name, hold_last=True, ada=False, heads=None):
                s_ = by_name[name]
                for i in range(s_["count"]):
                    if ada:
                        ada_step()
                    if not (hold_last and i == s_["count"] - 1):
                        split_unit(s_["base"] + i + 2)
                    if heads is not None:
                        heads(i)

            def held_split(name):
                s_ = by_name[name]
                split_unit(s_["base"] + s_["count"] + 1)

            def panel_rows(rows, col, width):
                dve.wait_ge(unit_done, panel_end[panel_no[0]])
                panel_no[0] += 1
                for h in range(2):
                    w = min(512, width - 512 * h)
                    nc.vector.tensor_copy(rows[:, 1, col + 512 * h:col + 512 * h + w], ps[:, D_BANKS[2 + h], 0:w]).then_inc(dve_emptied, 1)

            def residual(strm):
                n = panel_no[0]
                panel_no[0] += 1
                dve.wait_ge(unit_done, panel_end[n])
                e = gate_no[0]
                gate_no[0] += 1
                if GATES[e][0] == 2 and GATES[e][2] == 0:
                    dve.wait_ge(sem("pool_gate"), 2 * (GATES[e][1] + 1))
                else:
                    dve.wait_ge(gate_copied, 2 * sum(1 for g in GATES[:e + 1] if not (g[0] == 2 and g[2] == 0)))
                tmp = xn
                if norm_no[0] > 0:
                    dve.wait_ge(sem("hT_ready"), 4 * norm_no[0])
                for t in range(TT):
                    for h in range(2):
                        nc.vector.tensor_tensor(tmp[:, t, 512 * h:512 * h + 512], ps[:, D_BANKS[2 * t + h], :], gate_b[:, 512 * h:512 * h + 512], ALU.mult).then_inc(dve_emptied, 1)
                    dve.wait_ge(dve_emptied, dve_count[n + 1] - 2 + 2 * t)
                    nc.vector.tensor_tensor(res[:, strm, t, :], res[:, strm, t, :], tmp[:, t, :], ALU.add).then_inc(sem("res_ready"), 1)
                dve.wait_ge(sem("res_ready"), 2 * gate_no[0])

            def rsqrt(n):
                x, y, z = stat[:, 0:n], rstat[:, 0:n], nwt[:, 0:n]
                link(nc.vector.tensor_scalar(nwt_i[:, 0:n], stat[:, 0:n].bitcast(I32), 1, None, ALU.logical_shift_right))
                link(nc.vector.tensor_scalar(rstat[:, 0:n].bitcast(I32), nwt_i[:, 0:n], -1.0, float(0x5F3759DF), ALU.mult, ALU.add))
                nc.vector.tensor_scalar(x, x, -0.5, None, ALU.mult)
                for _ in range(3):
                    link(nc.vector.tensor_tensor(z, y, y, ALU.mult))
                    link(nc.vector.tensor_tensor(z, z, x, ALU.mult))
                    link(nc.vector.scalar_tensor_tensor(out=y, in0=z, scalar=1.5, in1=y, op0=ALU.add, op1=ALU.mult))

            def norm():
                n = norm_no[0]
                norm_no[0] += 1
                strm, l, f = NORMS[n] if n < len(NORMS) else (0, 0, 0)
                dve.wait_ge(sem("squares"), 2 * (n + 1))
                link(nc.vector.tensor_scalar(stat[:, 0:2], sums[:, n % 2, :], 1.0 / D, EPS, ALU.mult, ALU.add))
                rsqrt(2)
                for t in range(TT):
                    if n in (4, 6) or n >= len(NORMS):
                        nc.vector.tensor_scalar(xn[:, t, :], res[:, strm, t, :], rstat[:, t:t + 1], None, ALU.mult).then_inc(sem("xn_ready"), 1)
                    else:
                        nc.vector.tensor_scalar(diag[:, t, :], ident, rstat[:, t:t + 1], None, ALU.mult).then_inc(sem("xn_ready"), 1)
                if n >= len(NORMS):
                    return
                if n in (4, 6):
                    s_ = (n - 4) // 2
                    dve.wait_ge(sem("pool_landed"), 32 * (s_ + 1))
                    for h in range(2):
                        dve.wait_ge(gate_psum, 2 * (4 + 2 * s_) + h + 1)
                        nc.vector.tensor_tensor(gate_b[:, 512 * h:512 * h + 512], ps[:, D_BANKS[h], :], wk(2048 + 512 * h, 512), ALU.mult).then_inc(sem("pool_gate"), 1)
                for b in range(4):
                    pair = slice(2 * b, 2 * b + 2)
                    if b % 2 == 0:
                        dve.wait_ge(sem("xT_psum"), 4 * n + b + 1)
                        for k in (2 * b, 2 * b + 1):
                            src = ps[:, H_BANKS[b], (k % 2) * S:(k % 2 + 1) * S]
                            if n in (4, 6):
                                ins = nc.vector.tensor_scalar(full[:, k, :], src, modA[:, l, strm, f, k:k + 1], None, ALU.mult)
                            else:
                                ins = nc.vector.tensor_scalar(full[:, k, :], src, modA[:, l, strm, f, k:k + 1], modT[:, l, strm, f, 0, k:k + 1], ALU.mult, ALU.add)
                        link(ins)
                        link(nc.vector.tensor_copy(hT_hi[:, pair, :], full[:, pair, :]))
                    else:
                        dve.wait_ge(sem("hT_hi_act"), 2 * n + b // 2 + 1)
                    nc.vector.tensor_tensor(hT_lo[:, pair, :], full[:, pair, :], hT_hi[:, pair, :].bitcast(F32), ALU.subtract).then_inc(sem("hT_ready"), 1)

            def head_norm(views, width, sq, gain_aps, parts=range(4)):
                a, b = views[0].shape[1], views[0].shape[2]
                nh = a * b
                n = len(views) * nh

                def square(t):
                    return nc.vector.tensor_tensor(sq[t].rearrange("p (a b d) -> p a b d", a=a, b=b), views[t], views[t], ALU.mult)

                def total(t):
                    return nc.vector.tensor_reduce(stat[:, t * nh:(t + 1) * nh], sq[t].rearrange("p (h d) -> p h d", h=nh), AX, ALU.add)

                def scaled(t):
                    r = rstat[:, t * nh:(t + 1) * nh].rearrange("p (a b c) -> p a b c", a=a, b=b).to_broadcast([P, a, b, width])
                    return nc.vector.tensor_tensor(views[t], views[t], r, ALU.mult)

                def gained(t):
                    return nc.vector.tensor_tensor(views[t], views[t], gain_aps.to_broadcast([P, a, b, width]), ALU.mult)

                for part in parts:
                    if part == 0:
                        square(0)
                        link(square(1))
                        link(total(0))
                    elif part == 1:
                        link(total(1))
                        link(nc.vector.tensor_scalar(stat[:, 0:n], stat[:, 0:n], 1.0 / width, EPS, ALU.mult, ALU.add))
                        rsqrt(n)
                    elif part == 2:
                        scaled(0)
                        link(scaled(1))
                        link(gained(0))
                    else:
                        link(gained(1))

            def rotate(views, cos, sin, tmp, half):
                for v, c_, s_, z in zip(views, cos, sin, tmp):
                    a, b = v.shape[1], v.shape[2]
                    x1, x2 = v[:, :, :, 0:half], v[:, :, :, half:2 * half]
                    cb, sb_ = c_.to_broadcast([P, a, b, half]), s_.to_broadcast([P, a, b, half])
                    zz = [z[:, n * a * b * half:(n + 1) * a * b * half].rearrange("p (a b d) -> p a b d", a=a, b=b) for n in range(4)]
                    nc.vector.tensor_tensor(zz[0], x1, cb, ALU.mult)
                    nc.vector.tensor_tensor(zz[1], x2, sb_, ALU.mult)
                    nc.vector.tensor_tensor(zz[2], x2, cb, ALU.mult)
                    link(nc.vector.tensor_tensor(zz[3], x1, sb_, ALU.mult))
                    nc.vector.tensor_tensor(x1, zz[0], zz[1], ALU.subtract)
                    ins = nc.vector.tensor_tensor(x2, zz[2], zz[3], ALU.add)
                link(ins)

            def turns(stage):
                for g, (_, dst) in enumerate(q_groups(stage)):
                    if g % 2 == 1:
                        dve.wait_ge(sem(f"turned{stage}"), g + 1)
                        d = dst if len(dst.shape) == 2 else dst.rearrange("p a b -> p (a b)")
                        nc.vector.tensor_copy(d, ps[:, g % 4, :]).then_inc(sem(f"turn_dve{stage}"), 1)

            def attention(stage):
                a = ATT[stage]

                def maxima(i):
                    dve.wait_ge(a.scores, i + 1)
                    b = 2 * (i % 2)
                    if i >= 2:
                        dve.wait_ge(a.exps, i - 1)
                    if stage == 3:
                        link(nc.vector.tensor_reduce(rowmax[:, i % 2, 0:2], ps[:, b:b + 2, :], AX, ALU.max))
                        nc.vector.tensor_scalar(rowmax[:, i % 2, 0:2], rowmax[:, i % 2, 0:2], -a.scale, None, ALU.mult).then_inc(a.negmax, 1)
                    else:
                        mx = rowmax[:, i % 2, :].rearrange("p (m r) -> p m r", r=2)
                        nc.vector.tensor_reduce(mx[:, :, 0], ps[:, b:b + 2, 0:128], AX, ALU.max)
                        link(nc.vector.tensor_reduce(mx[:, :, 1], ps[:, b:b + 2, 128:384], AX, ALU.max))
                        nc.vector.tensor_scalar(rowmax[:, i % 2, :], rowmax[:, i % 2, :], -a.scale, None, ALU.mult).then_inc(a.negmax, 1)

                def mix(i):
                    dve.wait_ge(a.exps, i + 1)
                    if i >= 2:
                        dve.wait_ge(a.turned, i - 1)
                    cf = coef[:, i % 2, :]
                    link(nc.vector.reciprocal(cf, rowsum[:, 4 * i:4 * i + 4]))
                    link(nc.vector.tensor_scalar(cf[:, 2:4], cf[:, 2:4], lam_s[:, 4:5], None, ALU.mult))
                    for lo, hi, r in ((0, 128, 0), (128, 384, 1)):
                        ins = nc.vector.tensor_scalar(a.mix[:, i % 2, 0, lo:hi], a.p[:, i % 2, 1, lo:hi], cf[:, 2 + r:3 + r], None, ALU.mult)
                    link(ins)
                    for lo, hi, r in ((0, 128, 0), (128, 384, 1)):
                        ins = nc.vector.scalar_tensor_tensor(out=a.mix[:, i % 2, 0, lo:hi], in0=a.p[:, i % 2, 0, lo:hi], scalar=cf[:, r:r + 1],
                                                             in1=a.mix[:, i % 2, 0, lo:hi], op0=ALU.mult, op1=ALU.subtract)
                    ins.then_inc(a.mixed, 1)

                def take(i):
                    dve.wait_ge(a.pv, i + 1)
                    if stage == 0:
                        cf = coef[:, i % 2, :]
                        link(nc.vector.reciprocal(cf, rowsum[:, 4 * i:4 * i + 4]))
                        h = (2 * i) % 8
                        o = ps[:, 6, 0:256].rearrange("p (m t d) -> p m t d", m=2, t=TT)
                        cols = (0 if i < 4 else 512) + h * HD
                        dst = r0[:, :, cols:cols + 2 * HD].rearrange("p t (m d) -> p m t d", m=2)
                        cf3 = cf.rearrange("p (m t c) -> p m t c", m=2, t=TT)
                        if i < 4:
                            for m in range(2):
                                ins = nc.vector.tensor_tensor(dst[:, m], o[:, m], cf3[:, m].to_broadcast([P, TT, HD]), ALU.mult)
                            ins.then_inc(a.taken, 1)
                            return
                        y = 1 if i < 8 else 2
                        gs = gsig[:, :, 8 * y + h:8 * y + h + 2].rearrange("p t m -> p m t")
                        link(nc.vector.tensor_tensor(cf.rearrange("p (m t) -> p m t", m=2), cf.rearrange("p (m t) -> p m t", m=2), gs, ALU.mult))
                        tmp = hbuf[:, 0, 0:256].rearrange("p (m t d) -> p m t d", m=2, t=TT)
                        for m in range(2):
                            ins = nc.vector.tensor_tensor(tmp[:, m], o[:, m], cf3[:, m].to_broadcast([P, TT, HD]), ALU.mult)
                        link(ins)
                        for m in range(2):
                            ins = nc.vector.tensor_tensor(dst[:, m], dst[:, m], tmp[:, m], ALU.add)
                        ins.then_inc(a.taken, 1)
                        dve.wait_ge(a.taken, i + 1)
                    elif stage == 1:
                        o = r1[:, :, i * P:(i + 1) * P]
                        nc.vector.tensor_copy(o, ps[:, 6, 0:256].rearrange("p (t d) -> p t d", t=TT)).then_inc(a.taken, 1)
                        dve.wait_ge(a.taken, i + 1)
                        o2 = hbuf[:, i % 2, 0:2 * P].rearrange("p (t d) -> p t d", t=TT)
                        link(nc.vector.tensor_tensor(o2, o, o, ALU.mult))
                        nc.vector.tensor_reduce(stat[:, TT * i:TT * i + TT], o2, AX, ALU.add)
                    else:
                        cf = coef[:, i % 2, 0:2]
                        link(nc.vector.reciprocal(cf, rowsum[:, 2 * i:2 * i + 2]))
                        nc.vector.tensor_tensor(q3[:, :, i * P:(i + 1) * P], ps[:, 6, 0:256].rearrange("p (t d) -> p t d", t=TT),
                                                cf.rearrange("p (t c) -> p t c", c=1).to_broadcast([P, TT, P]), ALU.mult).then_inc(a.taken, 1)

                for i in range(a.steps + a.lag + 1):
                    if i < a.steps:
                        maxima(i)
                    if stage == 1 and 1 <= i <= a.steps:
                        mix(i - 1)
                    if i > a.lag:
                        take(i - a.lag - 1)
                    if i < a.ada:
                        ada_step()
                dve.wait_ge(a.taken, a.steps)

            def out_turn(stage):
                for b in range(4):
                    dve.wait_ge(sem(f"out_hi{stage}"), b + 1)
                    nc.vector.tensor_tensor(hT_lo[:, 2 * b:2 * b + 2, :], ps[:, H_BANKS[b], :].rearrange("p (k n) -> p k n", k=2),
                                            hT_hi[:, 2 * b:2 * b + 2, :].bitcast(F32), ALU.subtract).then_inc(sem(f"out_lo{stage}"), 1)

            nc.vector.memset(params[:, :], 0.0).then_inc(sem("params_zero"), 1)
            nc.vector.memset(zero16[:, :], 0.0).then_inc(hid_done, 2)
            nc.vector.memset(mark[:, :], 0.0).then_inc(hact_done, 2)
            nc.vector.memset(cpad[:, :, :, :], 0.0)
            nc.vector.memset(modrow[:, :, :], 0.0).then_inc(sem("modrow_zero"), 1)
            nc.vector.memset(lam_s[:, :], 0.0).then_inc(sem("zeros_set"), 1)
            dve.wait_ge(sem("small_params"), 128)
            nc.vector.tensor_copy(ident_r[:, :], ident)
            nc.vector.tensor_copy(causal_r[:, :], const("causal")).then_inc(sem("cst_r"), 1)
            dve.wait_ge(sem("param_psum"), 1)
            nc.vector.tensor_copy(paramT[:, :], ps[:, 0, 0:P]).then_inc(sem("paramT_ready"), 1)
            dve.wait_ge(sem("x_landed"), 32)
            link(nc.vector.tensor_copy(pos_f[:, :], pos_i[:, :]))
            ang = trig_t[:, 0, :, :]
            rev = trig[:, :, :, :]
            link(nc.vector.tensor_tensor(ang, pos_f[:, :].rearrange("p (t c) -> p t c", c=1).to_broadcast([P, TT, 8]),
                                         const("inv_freq").rearrange("p (c n) -> p c n", c=1).to_broadcast([P, TT, 8]), ALU.mult))
            MAGIC = 12582912.0
            link(nc.vector.tensor_scalar(rev[:, 0], ang, 1.0 / TWO_PI, 0.25, ALU.mult, ALU.add))
            link(nc.vector.tensor_scalar(rev[:, 1], ang, 1.0 / TWO_PI, None, ALU.mult))
            link(nc.vector.tensor_scalar(rev, rev, MAGIC, None, ALU.add))
            link(nc.vector.tensor_scalar(rev, rev, -MAGIC, None, ALU.add))
            link(nc.vector.tensor_copy(trig_t[:, 1, :, :], ang))
            c1 = 6.28125
            c2 = round((TWO_PI - c1) * 2 ** 20) / 2 ** 20
            c3 = TWO_PI - c1 - c2
            for part in (c1, c2, c3):
                link(nc.vector.scalar_tensor_tensor(out=trig_t[:, :, :, :], in0=rev, scalar=-part, in1=trig_t[:, :, :, :], op0=ALU.mult, op1=ALU.add))
            link(nc.vector.tensor_scalar(trig_t[:, 0, :, :], trig_t[:, 0, :, :], TWO_PI / 4, None, ALU.add))
            link(nc.vector.tensor_scalar(trig_t[:, :, :, :], trig_t[:, :, :, :], 3.141592, -3.141592, ALU.min, ALU.max))
            nc.vector.memset(mark[:, 2:3], 0.0).then_inc(sem("angles"), 1)

            split_unit(0)
            split_unit(1)
            ada_step(8)
            columns(0, 0)
            norm()
            cosv = [trig[:, 0, t:t + 1, :].rearrange("p a (b d) -> p a b d", b=1) for t in range(TT)]
            sinv = [trig[:, 1, t:t + 1, :].rearrange("p a (b d) -> p a b d", b=1) for t in range(TT)]
            sq0 = [wk(7728 + 1024 * t, 1024) for t in range(TT)]
            rot0 = [wk(9776 + 512 * t, 512) for t in range(TT)]

            def heads0(n, parts):
                if 0 in parts:
                    if n == 0:
                        dve.wait_ge(sem("gains_landed"), 16 * 18)
                        dve.wait_ge(sem("trig_ready"), 1)
                    dve.wait_ge(dve_emptied, 2 * n + 2)
                    dve.wait_ge(act_emptied, 2 * n + 2)
                if n == 0:
                    views = [r0[:, t, 0:1024].rearrange("p (a b d) -> p a b d", a=2, b=8) for t in range(TT)]
                    g = gains[:, 0:2, :].rearrange("p a (c d) -> p a c d", c=1)
                elif n == 1:
                    views = [r0[:, t, 1536:2048].rearrange("p (a b d) -> p a b d", a=1, b=8) for t in range(TT)]
                    g = gains[:, 2:3, :].rearrange("p a (c d) -> p a c d", c=1)
                else:
                    views = [r0[:, t, 2048:2816].rearrange("p (a z b d) -> p a z b d", a=3, z=2, b=2)[:, :, 0] for t in range(TT)]
                    g = gains[:, 3:6, :].rearrange("p a (c d) -> p a c d", c=1)
                nh = 16 if n == 0 else 8 if n == 1 else 6
                head_norm(views, HD, [q[:, 0:nh * HD] for q in sq0], g, parts)
                if 3 in parts:
                    rotate([v[:, :, :, 0:16] for v in views], cosv, sinv, rot0, 8)

            for n, w in enumerate((1024, 1024, 792)):
                row_segment(f"in0_{n}", ada=(n == 0), heads=(lambda i: heads0(n - 1, (i,))) if n else None)
                panel_rows(r0, 1024 * n, w)
                held_split(f"in0_{n}")
            heads0(2, range(4))
            nc.vector.memset(mark[:, 1:2], 0.0).then_inc(sem("heads0"), 1)
            dve.wait_ge(sem("gsig_exp"), 1)
            link(nc.vector.tensor_scalar(gsig[:, :, :], gsig[:, :, :], 1.0, None, ALU.add))
            link(nc.vector.reciprocal(gsig[:, :, :], gsig[:, :, :]))
            nc.vector.memset(hidr[:, :], 0.0).then_inc(sem("hidr_zero"), 1)
            turns(0)
            dve.wait_ge(sem("turn_act0"), 5)
            dve.wait_ge(sem("turn_dve0"), 5)
            blk = wk(12848, 1024).rearrange("p (s k n) -> p s k n", s=2, k=16)
            posT = paramT[:, 64:96].rearrange("p (s k c) -> p s k c", s=2, c=1)
            for s_ in range(2):
                for half in range(2):
                    lo, hi = 64 * half, 64 * half + 64
                    for g in range(2):
                        src = qt0[lo:hi, 16 + 2 * s_ + g, :].rearrange("p (n k a) -> p k n a", k=8, a=2)
                        for kh in range(2):
                            s_ap = src[:, :, kh:kh + NCMP, half]
                            dst = blk[lo:hi, s_, 8 * kh:8 * kh + 8, g * NCMP:(g + 1) * NCMP]
                            ins = nc.vector.tensor_tensor(dst, s_ap, posT[lo:hi, s_, 8 * kh:8 * kh + 8, :].to_broadcast([64, 8, NCMP]), ALU.add)
            ins.then_inc(sem("cmp_blocks"), 1)
            hidT = hbuf[:, 0, 0:128].rearrange("p (k n) -> p k n", k=2)
            vbd = hbuf[:, 1, :]
            dve.wait_ge(sem("cmp_hidT"), 1)
            nc.vector.tensor_copy(hidT, ps[:, 1, 0:128].rearrange("p (k n) -> p k n", k=2)).then_inc(sem("cmp_hidT_sb"), 1)
            dve.wait_ge(sem("cmp_kv"), 1)
            nc.vector.tensor_copy(kcs[:, 0:30], ps[:, 2, 0:30])
            nc.vector.tensor_copy(vcr[0:NCMP, :], ps[0:NCMP, 2, 64:192]).then_inc(sem("cmp_kv_sb"), 1)
            dve.wait_ge(sem("cmp_vrep"), 1)
            nc.vector.tensor_tensor(vbd, ps[:, 3, :], const("headmask"), ALU.mult).then_inc(sem("cmp_vbd"), 1)
            ada_step(4)
            link(nc.vector.memset(cmp_s, NEG))
            dve.wait_ge(sem("cmp_scores"), 1)
            neg = const("cmp_neg").rearrange("p (t c n) -> p t c n", t=TT, c=1)
            okm = const("cmp_ok").rearrange("p (t c n) -> p t c n", t=TT, c=1)
            for t in range(TT):
                for m in range(2):
                    ins = nc.vector.tensor_tensor(cmp_s[:, t, m:8:2, 0:NCMP], ps[:, t + 2 * m, 0:64].rearrange("p (h n) -> p h n", h=4)[:, :, 0:NCMP],
                                                  neg[:, t, :, 0:NCMP].to_broadcast([P, 4, NCMP]), ALU.add)
            link(ins)
            flat = cmp_s.rearrange("p t h n -> p (t h) n")
            link(nc.vector.tensor_reduce(cmp_m[:, :], flat, AX, ALU.max))
            nc.vector.tensor_tensor(flat, flat, cmp_m[:, :].rearrange("p (h c) -> p h c", c=1).to_broadcast([P, 16, 16]), ALU.subtract).then_inc(sem("cmp_shift"), 1)
            dve.wait_ge(sem("cmp_exp"), 1)
            for t in range(TT):
                ins = nc.vector.tensor_tensor(cmp_s[:, t], cmp_s[:, t], okm[:, t].to_broadcast([P, 8, 16]), ALU.mult)
            link(ins)
            link(nc.vector.tensor_reduce(cmp_m[:, :], flat, AX, ALU.add))
            link(nc.vector.tensor_scalar(cmp_m[:, :], cmp_m[:, :], 0.5, None, ALU.max))
            link(nc.vector.reciprocal(cmp_m[:, :], cmp_m[:, :]))
            link(nc.vector.tensor_tensor(cmp_m[:, :].rearrange("p (t h) -> p t h", t=TT), cmp_m[:, :].rearrange("p (t h) -> p t h", t=TT),
                                         gsig[:, :, 0:8], ALU.mult))
            nc.vector.tensor_tensor(flat, flat, cmp_m[:, :].rearrange("p (h c) -> p h c", c=1).to_broadcast([P, 16, 16]), ALU.mult).then_inc(sem("cmp_p"), 1)
            dve.wait_ge(sem("cmp_turned"), 1)
            nc.vector.tensor_copy(cmp_T, ps[:, 2, 0:256].rearrange("p (t n) -> p t n", t=TT)).then_inc(sem("cmp_pT"), 1)
            dve.wait_ge(sem("cmp_pv"), 1)
            link(nc.vector.tensor_copy(r0[:, :, 512:1024], ps[:, 0:2, :]))
            nc.vector.memset(mark[:, 1:2], 0.0).then_inc(sem("cmp_taken"), 1)
            ada_step(4)
            attention(0)
            columns(0, 1)
            out_turn(0)
            row_segment("out0")
            residual(0)
            norm()
            held_split("out0")
            stream("up0")
            columns(1, 0)
            stream("down0", hold_last=True)
            residual(0)
            norm()
            held_split("down0")
            sq1 = [wk(6144 + 2048 * t, 2048) for t in range(TT)]
            rot1 = [wk(10240 + 1024 * t, 1024) for t in range(TT)]

            def heads1(n, i):
                if i == 0:
                    dve.wait_ge(dve_emptied, dve_count[6 + n])
                    dve.wait_ge(act_emptied, act_count[6 + n])
                views = [r1[:, t, 1024 * n:1024 * n + 1024].rearrange("p (a b d) -> p a b d", a=1, b=16) for t in range(TT)]
                head_norm(views, HD, [q[:, 0:1024] for q in sq1], gains[:, 6 + n:7 + n, :].rearrange("p a (c d) -> p a c d", c=1), (i,))
                if i == 3:
                    rotate([v[:, :, :, 0:16] for v in views], cosv, sinv, [z[:, 0:512] for z in rot1], 8)

            for n in range(3):
                row_segment(f"in1_{n}", heads=(lambda i: heads1(n - 1, i)) if n else None)
                panel_rows(r1, 1024 * n, 1024)
                held_split(f"in1_{n}")
            lp = lam_p[:, :, :].rearrange("p (a b) d -> p a b d", b=2)
            lt = hbuf[:, 0, 0:128].rearrange("p (a d) -> p a d", a=2)
            link(nc.vector.tensor_tensor(lt, lp[:, :, 0, :], lp[:, :, 1, :], ALU.mult))
            nc.vector.tensor_reduce(lam_s[:, 0:2], lt, AX, ALU.add).then_inc(sem("lam_sum"), 1)
            dve.wait_ge(sem("lam_exp"), 1)
            link(nc.vector.tensor_tensor(lam_s[:, 4:5], lam_s[:, 2:3], lam_s[:, 3:4], ALU.subtract))
            link(nc.vector.tensor_scalar(lam_s[:, 4:5], lam_s[:, 4:5], LAM_INIT, None, ALU.add))
            link(nc.vector.tensor_scalar(gain_o[:, :], gain_o[:, :], 1.0 - LAM_INIT, None, ALU.mult))
            nc.vector.memset(mark[:, 1:2], 0.0).then_inc(sem("heads1"), 1)
            turns(1)
            attention(1)
            columns(1, 1)
            n = TT * ATT[1].steps
            link(nc.vector.tensor_scalar(stat[:, 0:n], stat[:, 0:n], 1.0 / HD2, EPS, ALU.mult, ALU.add))
            rsqrt(n)
            for h in range(ATT[1].steps):
                for t in range(TT):
                    o = r1[:, t, h * P:(h + 1) * P]
                    ins = nc.vector.scalar_tensor_tensor(out=o, in0=o, scalar=rstat[:, TT * h + t:TT * h + t + 1], in1=gain_o[:, :], op0=ALU.mult, op1=ALU.mult)
                if h % 2 == 1:
                    ins.then_inc(sem("rows1"), 1)
            out_turn(1)
            row_segment("out1", ada=True)
            residual(0)
            norm()
            held_split("out1")
            stream("up1")
            columns(2, 0)
            stream("down1", hold_last=True)
            columns(2, 1)
            residual(0)
            for s_ in range(2):
                norm()
                held_split("down1" if s_ == 0 else "down20")
                residual(s_)
                norm()
                split_unit(by_name[f"pool{s_}"]["base"] + 2)
                stream(f"up2{s_}")
                if s_ == 1:
                    columns(3, 0)
                stream(f"down2{s_}", hold_last=True)
                residual(s_)
            norm()
            held_split("down21")
            row_segment("kvc")
            panel_rows(kvc, 0, 1024)
            norm()
            held_split("kvc")
            acos = [const("ax_cos").rearrange("p (t a b d) -> p t a b d", t=TT, a=1, b=2)[:, t] for t in range(TT)]
            asin = [const("ax_sin").rearrange("p (t a b d) -> p t a b d", t=TT, a=1, b=2)[:, t] for t in range(TT)]
            sq3 = [wk(6144 + 1024 * t, 1024) for t in range(TT)]
            rot3 = [wk(8192 + 2048 * t, 2048) for t in range(TT)]

            def heads3(n, parts):
                rows, gn, nh = ((kvc, 1, 4), (q3, 0, 8), (kvl, 1, 4))[n]
                if 0 in parts:
                    dve.wait_ge(dve_emptied, dve_count[15 + n])
                    dve.wait_ge(act_emptied, act_count[15 + n])
                views = [rows[:, t, 0:nh * P].rearrange("p (a b d) -> p a b d", a=1, b=nh) for t in range(TT)]
                head_norm(views, HD2, [q[:, 0:nh * P] for q in sq3], gains2[:, gn:gn + 1, :].rearrange("p a (c d) -> p a c d", c=1), parts)
                if n > 0 and 3 in parts:
                    rv = [rows[:, t, 0:nh * P].rearrange("p (a b d) -> p a b d", a=nh, b=2) for t in range(TT)]
                    rotate(rv, acos, asin, [z[:, 0:nh * 256] for z in rot3], 32)

            for n, (name, rows) in enumerate((("q3", q3), ("kvl", kvl))):
                row_segment(name, heads=lambda i: heads3(n, (i,)))
                panel_rows(rows, 0, 1024)
                held_split(name)
            heads3(2, range(4))
            nc.vector.memset(mark[:, 1:2], 0.0).then_inc(sem("heads3"), 1)
            turns(3)
            attention(3)
            columns(3, 1)
            out_turn(3)
            row_segment("out3", ada=True)
            residual(0)
            norm()
            held_split("out3")
            stream("up3")
            stream("down3")
            residual(0)
            norm()
            dve.wait_ge(sem("xn_ready"), 2 * (len(NORMS) + 1))
            dve.wait_ge(sem("final_landed"), 16)
            for t in range(TT):
                nc.vector.tensor_tensor(xn[:, t, :], xn[:, t, :], wk(0, D), ALU.mult).then_inc(sem("out_ready"), 1)

        @block.tensor
        def _(pe):
            mm = nc.tensor.matmul
            step_no = [0]
            panel_no = [0]
            norm_no = [0]
            gate_no = [0]
            bank7 = [None]
            gate_out = [None]
            fed = [None]

            def fed_wait(pair):
                if fed[0] is not None:
                    pe.wait_ge(fed[0][0], fed[0][1] + pair + 1)

            def bank7_wait():
                if bank7[0] is not None:
                    pe.wait_ge(*bank7[0])

            def vector_unit(g, j, k=None):
                r = ring_at(g, j)
                if j == 0:
                    if g > 0:
                        pe.wait_ge(mod_rows, g if k is None else k + g)
                    if k is None:
                        bank7_wait()
                ring_wait(pe, r, k)
                for kk in range(2):
                    kt = 2 * j + kk
                    for c_ in range(4):
                        ins = mm(ps[32 * c_:32 * c_ + 32, ADA_BANK, 0:256], cpad[:, 0 if g < 12 else 1, kt, :],
                                 ring_view(r)[:, kk * D + 256 * c_:kk * D + 256 * (c_ + 1)], start=(kt == 0), stop=(kt == KT - 1))
                ins.then_inc(ring_used, 1)

            def ada_step(n=1):
                for _ in range(n):
                    q, j = step_no[0] // 4, step_no[0] % 4
                    step_no[0] += 1
                    if q < len(STEP_PLAN):
                        vector_unit(STEP_PLAN[q], j)

            def columns(l, f, done):
                pe.wait_ge(mod_rows, done)
                bank7_wait()
                for w in range(2):
                    for q in range(2):
                        ins = nc.tensor.transpose(ps[:, ADA_BANK, (2 * w + q) * P:(2 * w + q + 1) * P], modrow[:, 3 * f + w, q * P:(q + 1) * P], ident)
                ins.then_inc(ada_turn, 1)
                bank7[0] = (mod_ready, 2 * l + f + 1)

            def unit_wait(u, half, k4=None):
                v = 2 * u + 1 + half
                pe.wait_ge(lo_ready, v if k4 is None else k4 * 8 + v)

            def three(dst, s_hi, s_lo, m_hi, m_lo, start, stop, skip=False):
                mm(dst, s_hi, m_hi, start=start, stop=False, skip_group_check=skip)
                mm(dst, s_hi, m_lo, start=False, stop=False, skip_group_check=skip)
                return mm(dst, s_lo, m_hi, start=False, stop=stop, skip_group_check=skip)

            def emptied(n, t):
                if n == 0:
                    return
                if gate_out[0] is not None:
                    pe.wait_ge(*gate_out[0])
                if t == 0:
                    if act_count[n]:
                        pe.wait_ge(act_emptied, act_count[n])
                    if PANEL_KIND[n - 1] == "res":
                        pe.wait_ge(dve_emptied, dve_count[n])
                elif dve_count[n]:
                    pe.wait_ge(dve_emptied, dve_count[n])

            def row_segment(name, ada=False):
                s_ = by_name[name]
                n = panel_no[0]
                panel_no[0] += 1
                w = s_["width"]
                for i in range(4):
                    u = s_["base"] + i
                    if ada:
                        ada_step()
                    fed_wait(i)
                    for kk in range(2):
                        unit_wait(u, kk)
                        k = 2 * i + kk
                        for t in range(TT):
                            if k == 0:
                                emptied(n, t)
                            for h in range(2):
                                wd = min(512, w - 512 * h)
                                c0 = kk * w + 512 * h
                                ins = three(ps[:, D_BANKS[2 * t + h], 0:wd], hT_hi[:, k, t * P:(t + 1) * P], hT_lo[:, k, t * P:(t + 1) * P],
                                            whi[:, u % 2, c0:c0 + wd], wlo[:, u % 2, c0:c0 + wd], k == 0, k == KT - 1)
                    ins.then_inc(unit_done, 1)
                fed[0] = None

            def hidden_unit(s_, i, k4=None):
                u = s_["base"] + i
                hb = hid_base[s_["name"][2:]]
                unit_wait(u, 0, k4)
                if s_["kind"] == "pair":
                    which, v, per = (hact_done if i % 2 == 0 else hid_done), hb + i // 2 - 1, 2
                else:
                    which, v, per = hact_done, hb + i - 3, 4
                pe.wait_ge(which, v if k4 is None else k4 * per + v)
                for f in range(2):
                    for k in range(KT):
                        if i == 0 and f == 0 and k % 2 == 0:
                            fed_wait(k // 2)
                        if f == 0 and k == KT // 2:
                            unit_wait(u, 1, k4)
                        c0 = k * 256 + f * P
                        ins = three(ps[:, H_BANKS[i % 4], f * S:(f + 1) * S], whi[:, u % 2, c0:c0 + P], wlo[:, u % 2, c0:c0 + P], hT_hi[:, k, :], hT_lo[:, k, :],
                                    k == 0, k == KT - 1)
                ins.then_inc(unit_done, 1)

            def up_segment(name):
                s_ = by_name[name]
                n = bodies(s_)
                for first, many, ada in loops_of(name):
                    if ada:
                        bank7_wait()
                    with pe.Fori(first, first + many) as k4:
                        for j in range(4):
                            hidden_unit(s_, j, k4)
                            if ada:
                                vector_unit(LOOP_PLAN[name][0], j, k4)
                for i in range(4 * n, s_["count"]):
                    hidden_unit(s_, i)
                fed[0] = None

            def down_segment(name):
                s_ = by_name[name]
                n0 = panel_no[0]
                panel_no[0] += 1
                for t in range(TT):
                    emptied(n0, t)
                tag = s_["name"][4:]
                hb = hid_base[tag] + by_name["up" + tag]["count"] // (2 if by_name["up" + tag]["kind"] == "pair" else 1)
                pe.wait_ge(hact_done, hb)
                for q in range(4):
                    mm(ps[:, D_BANKS[q], :], zero16[0:1, 0:P], zero16[0:1, :], start=True, stop=False, skip_group_check=True)

                def unit(i, k4=None):
                    u = s_["base"] + i
                    for kk in range(2):
                        unit_wait(u, kk, k4)
                        for t in range(TT):
                            for h in range(2):
                                c0 = kk * 1024 + 512 * h
                                a0 = kk * S + t * P
                                ins = three(ps[:, D_BANKS[2 * t + h], :], act_hi[:, u % 2, a0:a0 + P], act_lo[:, u % 2, a0:a0 + P],
                                            whi[:, u % 2, c0:c0 + 512], wlo[:, u % 2, c0:c0 + 512], False, False, True)
                    ins.then_inc(unit_done, 1)

                n = bodies(s_)
                for first, many, ada in loops_of(name):
                    if ada:
                        for j in range(4):
                            unit(j)
                            vector_unit(LOOP_PLAN[name][0], j)
                        continue
                    with pe.Fori(first, first + many) as k4:
                        for j in range(4):
                            unit(j, k4)
                for i in range(4 * n, s_["count"]):
                    unit(i)

            def norm():
                n = norm_no[0]
                norm_no[0] += 1
                strm = NORMS[n][0]
                if n in (4, 6):
                    pe.wait_ge(sem("pool_landed"), 32 * (1 if n == 4 else 2))
                mats = wk(0, 2048).rearrange("p (g j n) -> p g j n", g=4, j=TT)
                pe.wait_ge(sem("xn_ready"), 2 * n + 2)
                for b in range(4):
                    for k in (2 * b, 2 * b + 1):
                        for t in range(TT):
                            if n in (4, 6):
                                ins = mm(ps[:, H_BANKS[b], (k % 2) * S:(k % 2 + 1) * S], xn[:, t, k * P:(k + 1) * P], mats[:, b, t, :],
                                         start=(t == 0), stop=(t == TT - 1))
                            else:
                                ins = mm(ps[:, H_BANKS[b], (k % 2) * S + t * P:(k % 2) * S + (t + 1) * P], res[:, strm, t, k * P:(k + 1) * P], diag[:, t, :],
                                         start=True, stop=True)
                    ins.then_inc(sem("xT_psum"), 1)
                fed[0] = (sem("hT_ready"), 4 * n)

            def gate():
                l, strm, f = GATES[gate_no[0]]
                e = gate_no[0]
                gate_no[0] += 1
                pooled = l == 2 and f == 0
                n = panel_no[0]
                for t in range(TT):
                    emptied(n, t)
                pe.wait_ge(mod_rows, 6 * l + 3 * f + 3)
                for h in range(2):
                    for c_ in range(2):
                        j = 2 * h + c_
                        sl = const("sel1" if strm else "sel0")
                        if c_:
                            pe.wait_ge(sem("gate_half"), gate_no[0] * 2 - 1 + h)
                        ins = mm(ps[:, D_BANKS[h], 256 * c_:256 * (c_ + 1)], sl[32 * j:32 * j + 32, :], modrow[32 * j:32 * j + 32, 2 + 3 * f, :],
                                 start=True, stop=True)
                        ins.then_inc(gate_psum if c_ else sem("gate_half"), 1)
                if pooled:
                    gate_out[0] = (sem("pool_gate"), 2 * strm + 2)
                else:
                    gate_out[0] = (gate_copied, 2 * sum(1 for g in GATES[:e + 1] if not (g[0] == 2 and g[2] == 0)))

            def turns(stage):
                for g, (srcs, _) in enumerate(q_groups(stage)):
                    if g >= 4:
                        which = "turn_act" if g % 2 == 0 else "turn_dve"
                        pe.wait_ge(sem(f"{which}{stage}"), (g - 4) // 2 + 1)
                    for n, src in enumerate(srcs):
                        ins = nc.tensor.transpose(ps[:, g % 4, n * P:(n + 1) * P], src, ident)
                    ins.then_inc(sem(f"turned{stage}"), 1)
                n = len(q_groups(stage))
                pe.wait_ge(sem(f"turn_act{stage}"), n // 2)
                pe.wait_ge(sem(f"turn_dve{stage}"), n // 2)

            def attention(stage):
                a = ATT[stage]

                def operands(i, m):
                    if stage == 0:
                        h = (2 * i) % 8 + m
                        lo, hi = 64 * m, 64 * m + 64
                        if i < 4:
                            q, k, v = qt0[lo:hi, i, :], qt0[lo:hi, 4 + i, :], 1024 + h * HD
                        else:
                            y = (i - 4) // 4
                            q, k, v = qt0[lo:hi, 8 + i % 4, :], qt0[lo:hi, 12 + 2 * y + h // 4, :], (2432 if y == 0 else 2688) + (h // 4) * HD
                        return q, k, [r0[:, t, v:v + HD] for t in range(TT)]
                    lo, hi = 64 * m, 64 * m + 64
                    return qt1[lo:hi, i, :], qt1[lo:hi, 8 + i, :], [r1[:, t, 2048 + i * P:2048 + (i + 1) * P] for t in range(TT)]

                def scores(i):
                    if i >= 2:
                        pe.wait_ge(a.exps, i - 1)
                    for m in range(2):
                        bank = 2 * (i % 2) + m
                        if stage == 3:
                            ins = mm(ps[:, bank, :], qt3[:, i, m * P:(m + 1) * P], kt3[:, i // 2, :], start=True, stop=True)
                            continue
                        q, k, _ = operands(i, m)
                        mm(ps[:, bank, 0:256], ident_r[:, :], causal_r[:, :], start=True, stop=False, skip_group_check=True)
                        mm(ps[:, bank, 0:128], q[:, 0:128], k[:, 0:128], start=False, stop=True, skip_group_check=True)
                        mm(ps[:, bank, 128:256], q[:, 128:256], k[:, 128:256], start=False, stop=True, skip_group_check=True)
                        ins = mm(ps[:, bank, 256:384], q[:, 128:256], k[:, 0:128], start=False, stop=True, skip_group_check=True)
                    ins.then_inc(a.scores, 1)

                def turn(i):
                    pe.wait_ge(a.mixed if stage == 1 else a.exps, i + 1)
                    if stage == 1:
                        if i >= 2:
                            pe.wait_ge(a.pT, i - 1)
                        maps = [(4 + i % 2, a.mix[:, i % 2, 0, :])]
                    else:
                        if i >= 1:
                            pe.wait_ge(a.pT, i)
                        maps = [(4 + m, a.p[:, i % 2, m, :]) for m in range(2)]
                    for bank, src in maps:
                        for b in range(a.width // P):
                            ins = nc.tensor.transpose(ps[:, bank, b * P:(b + 1) * P], src[:, b * P:(b + 1) * P], ident)
                    ins.then_inc(a.turned, 1)

                def values(i):
                    pe.wait_ge(a.pT, i + 1)
                    if i >= 1:
                        pe.wait_ge(a.taken, i)
                    if stage == 3:
                        vcol = 512 + (i // 2) * P
                        v = [kvc[:, 0, vcol:vcol + P], kvc[:, 1, vcol:vcol + P], kvl[:, 0, vcol:vcol + P], kvl[:, 1, vcol:vcol + P]]
                        for m in range(2):
                            for b in range(4):
                                ins = mm(ps[:, 6, m * P:(m + 1) * P], a.pt[:, i % 2, m, b * P:(b + 1) * P], v[b], start=(b == 0), stop=(b == 3))
                    else:
                        for m in range(a.maps):
                            _, _, v = operands(i, m)
                            w = HD if stage == 0 else HD2
                            pt = a.pt[:, i % 2, m, :]
                            o = ps[:, 6, m * 2 * w:(m + 1) * 2 * w]
                            mm(o[:, 0:w], pt[:, 0:128], v[0], start=True, stop=True)
                            mm(o[:, w:2 * w], pt[:, 128:256], v[1], start=True, stop=False)
                            ins = mm(o[:, w:2 * w], pt[:, 256:384], v[0], start=False, stop=True)
                    ins.then_inc(a.pv, 1)

                pe.wait_ge(*gate_out[0])
                for i in range(a.steps + a.lag + 1):
                    if i < a.steps:
                        scores(i)
                    if a.lag <= i < a.steps + a.lag:
                        turn(i - a.lag)
                    if i > a.lag:
                        values(i - a.lag - 1)
                    if i < a.ada:
                        ada_step()
                pe.wait_ge(a.taken, a.steps)

            def out_turn(stage):
                rows = out_rows[stage]
                for b in range(4):
                    if stage == 1:
                        pe.wait_ge(sem("rows1"), b + 1)
                    for k in (2 * b, 2 * b + 1):
                        for t in range(TT):
                            ins = nc.tensor.transpose(ps[:, H_BANKS[b], (k % 2) * S + t * P:(k % 2) * S + (t + 1) * P], rows[:, t, k * P:(k + 1) * P], ident)
                    ins.then_inc(sem(f"out_turned{stage}"), 1)
                fed[0] = (sem(f"out_lo{stage}"), 0)

            pe.wait_ge(sem("small_params"), 128)
            nc.tensor.transpose(ps[:, 0, 0:P], params[:, :], ident).then_inc(sem("param_psum"), 1)
            pe.wait_ge(sem("zeros_set"), 1)
            pe.wait_ge(sem("silu_c"), 1)
            pe.wait_ge(sem("cst_r"), 1)
            ada_step(8)
            columns(0, 0, 2)
            norm()
            for n in range(3):
                row_segment(f"in0_{n}", ada=(n == 0))
            gate()
            pe.wait_ge(sem("heads0"), 1)
            pe.wait_ge(sem("doubled"), 1)
            turns(0)
            pe.wait_ge(sem("cmp_blocks"), 1)
            blk = wk(12848, 1024).rearrange("p (s k n) -> p s k n", s=2, k=16)
            for s_ in range(2):
                for h in range(2):
                    r = CMP_AT + 2 * s_ + h
                    ring_wait(pe, r)
                    for kk in range(8):
                        k = 8 * h + kk
                        ins = mm(ps[32 * s_:32 * s_ + 30, 0, 0:256], blk[:, s_, k, 0:30], ring[:, r % 2, kk * 256:(kk + 1) * 256],
                                 start=(k == 0), stop=(k == 15))
                    ins.then_inc(ring_used, 1)
            ada_step()
            pe.wait_ge(sem("cmp_silu"), 1)
            for e in range(2):
                ins = nc.tensor.transpose(ps[:, 1, 64 * e:64 * e + 64], hidr[:, e * P:(e + 1) * P], ident[0:64, 0:64])
            ins.then_inc(sem("cmp_hidT"), 1)
            ada_step()
            pe.wait_ge(sem("cmp_hidT_sb"), 1)
            hidT = hbuf[:, 0, 0:128].rearrange("p (k n) -> p k n", k=2)
            vbd = hbuf[:, 1, :]
            for e in range(2):
                mm(ps[:, 2, 0:30], w2k[:, e, :, :].rearrange("p u d -> p (u d)"), hidT[:, e, 0:30], start=(e == 0), stop=(e == 1))
            for g in range(2):
                for e in range(2):
                    ins = mm(ps[0:NCMP, 2, 64 + 64 * g:128 + 64 * g], hidT[:, e, 32 + g * NCMP:32 + (g + 1) * NCMP], w2v[:, e, :],
                             start=(e == 0), stop=(e == 1))
            ins.then_inc(sem("cmp_kv"), 1)
            ada_step()
            pe.wait_ge(sem("cmp_kv_sb"), 1)
            for g in range(2):
                for r_ in range(4):
                    h = 4 * g + r_
                    ins = mm(ps[:, 3, h * HD:(h + 1) * HD], const("spread")[0:NCMP, :], vcr[0:NCMP, g * HD:(g + 1) * HD], start=True, stop=True)
            ins.then_inc(sem("cmp_vrep"), 1)
            ada_step()
            pe.wait_ge(sem("cmp_vbd"), 1)
            for t in range(TT):
                for h in range(8):
                    lo = 64 * (h % 2)
                    ins = mm(ps[:, t + 2 * (h % 2), (h // 2) * 16:(h // 2) * 16 + NCMP], qt0[lo:lo + 64, 8 + h // 2, t * P:(t + 1) * P], kcs[lo:lo + 64, (h // 4) * NCMP:(h // 4 + 1) * NCMP],
                             start=True, stop=True)
            ins.then_inc(sem("cmp_scores"), 1)
            ada_step(2)
            pe.wait_ge(sem("cmp_p"), 1)
            pe.wait_ge(sem("cmp_vbd"), 1)
            for t in range(TT):
                ins = nc.tensor.transpose(ps[:, 2, t * P:(t + 1) * P], cmp_s[:, t].rearrange("p h n -> p (h n)"), ident)
            ins.then_inc(sem("cmp_turned"), 1)
            ada_step()
            pe.wait_ge(sem("cmp_pT"), 1)
            for t in range(TT):
                ins = mm(ps[:, t, :], cmp_T[:, t, :], vbd, start=True, stop=True)
            ins.then_inc(sem("cmp_pv"), 1)
            ada_step()
            pe.wait_ge(sem("cmp_taken"), 1)
            attention(0)
            columns(0, 1, 6)
            out_turn(0)
            row_segment("out0")
            gate()
            norm()
            up_segment("up0")
            columns(1, 0, 9)
            down_segment("down0")
            norm()
            for n in range(3):
                row_segment(f"in1_{n}")
            gate()
            pe.wait_ge(sem("heads1"), 1)
            turns(1)
            attention(1)
            columns(1, 1, 11)
            out_turn(1)
            row_segment("out1", ada=True)
            gate()
            norm()
            up_segment("up1")
            columns(2, 0, 17)
            down_segment("down1")
            columns(2, 1, 18)
            for strm in range(2):
                gate()
                norm()
                s_ = by_name[f"pool{strm}"]
                u = s_["base"]
                n = panel_no[0]
                panel_no[0] += 1
                unit_wait(u, 1)
                for t in range(TT):
                    emptied(n, t)
                    for g in range(4):
                        if t == 0:
                            fed_wait(g)
                        for kk in range(2):
                            k = 2 * g + kk
                            ins = three(ps[:, D_BANKS[2 * t + g // 2], (g % 2) * 256:(g % 2 + 1) * 256], hT_hi[:, k, t * P:(t + 1) * P], hT_lo[:, k, t * P:(t + 1) * P],
                                        whi[:, u % 2, k * 256:(k + 1) * 256], wlo[:, u % 2, k * 256:(k + 1) * 256], kk == 0, kk == 1)
                ins.then_inc(unit_done, 1)
                gate()
                norm()
                up_segment(f"up2{strm}")
                if strm == 1:
                    columns(3, 0, 21)
                down_segment(f"down2{strm}")
            norm()
            row_segment("kvc")
            norm()
            row_segment("q3")
            row_segment("kvl")
            gate()
            pe.wait_ge(sem("heads3"), 1)
            turns(3)
            attention(3)
            columns(3, 1, 23)
            out_turn(3)
            row_segment("out3", ada=True)
            gate()
            norm()
            up_segment("up3")
            down_segment("down3")


_INS = ["x", "c", "positions", "ada_w", "ada_b", "attn_norm", "ffn_norm", "ffn_w_gate", "ffn_w_up", "ffn_w_down", "sp_w_in",
        "sp_w_out", "moba_q_norm", "moba_k_norm", "nsa_q_norm", "nsa_k_norm", "nsa_cmp_pos", "nsa_cmp_w1", "nsa_cmp_w2",
        "diff_w_in", "diff_w_out", "diff_q_norm", "diff_k_norm", "diff_lambda", "diff_out_norm", "c_2", "ctx_2", "c_ctx_2",
        "ada_w_2", "ada_b_2", "norm_g_2", "mlp_w1_2", "mlp_w2_2", "pool_w_2", "pool_scale_2", "attn_w_qkv_2", "attn_w_o_2",
        "attn_q_g_2", "attn_k_g_2", "final_g_2"]


def kernel(**inputs):
    import numpy as _np
    import concourse.bacc as _bacc
    from concourse import mybir as _mybir
    from concourse.bass_utils import run_bass_kernel_spmd as _run

    nc = _bacc.Bacc("TRN2", target_bir_lowering=False, num_devices=1, dynamic_dma_scratch_size=1024)
    arrays, args = {}, []
    consts, pool_mats = shape_constants()
    for name, a in [(n, _np.ascontiguousarray(inputs[n])) for n in _INS] + [("consts", consts), ("pool_mats", pool_mats)]:
        arrays[f"in_{name}_dram"] = a
        args.append(nc.dram_tensor(f"in_{name}_dram", a.shape, _mybir.dt.from_np(a.dtype), kind="ExternalInput").ap())
    args.append(nc.dram_tensor("out_0_dram", (1, S, D), F32, kind="ExternalOutput").ap())
    build(nc, *args)
    r = _run(nc, [arrays], core_ids=[0])
    return r.results[0]["out_0_dram"]
```
